# Optimizing a Trainium2 kernel written in Bass

```python
import math
import jax, jax.numpy as jnp
from jax import lax
import numpy as np

D_MODEL = 1024
BATCH = 1
SEQ = 256
DEPTH = 1

CONV_WIDTH = 512
CONV_K = 3
N_HEADS = 8
HEAD_DIM = 64
V_DIM = 2 * HEAD_DIM
ATTN_QK = N_HEADS * 2 * HEAD_DIM
ATTN_V = N_HEADS * V_DIM
Q_BLOCK = 128
N_BUCKETS = 32
MAX_DISTANCE = 128
N_EXPERTS = 32
TOP_K = 4
D_EXPERT = D_MODEL
SWIGLU_ALPHA = 1.702
SWIGLU_LIMIT = 7.0
MOE_BLOCK = 256
D_IN = 3 * CONV_WIDTH + 2 * ATTN_QK + ATTN_V + 2 * D_MODEL
EPS = 1e-6

kernel_name = "hybrid_conv_diffattn_moe_adaln_block"

def rmsnorm(x, g):
    xf = x.astype(jnp.float32)
    r = xf * lax.rsqrt(jnp.mean(xf * xf, axis=-1, keepdims=True) + EPS)
    return (r * g.astype(jnp.float32)).astype(x.dtype)

def t5_bucket(dist):
    max_exact = N_BUCKETS // 2
    d = jnp.maximum(dist, 1).astype(jnp.float32)
    large = max_exact + (jnp.log(d / max_exact) / math.log(MAX_DISTANCE / max_exact)
                         * (N_BUCKETS - max_exact)).astype(jnp.int32)
    large = jnp.minimum(large, N_BUCKETS - 1)
    return jnp.where(dist < max_exact, dist, large)

def causal_dwconv(u, w, b):
    S = u.shape[1]
    up = jnp.pad(u, ((0, 0), (CONV_K - 1, 0), (0, 0)))
    y = b
    for j in range(CONV_K):
        y = y + up[:, j:j + S] * w[j]
    return y

def diff_attention(q, k, v, lam, rel_table):
    B, S = q.shape[0], q.shape[1]
    nb = S // Q_BLOCK
    scale = HEAD_DIM ** -0.5
    k_pos = jnp.arange(S, dtype=jnp.int32)
    neg = jnp.finfo(jnp.float32).min
    qb = q.reshape(B, nb, Q_BLOCK, N_HEADS, 2, HEAD_DIM).transpose(1, 0, 2, 3, 4, 5)

    def block(args):
        q_blk, i = args
        q_pos = i * Q_BLOCK + jnp.arange(Q_BLOCK, dtype=jnp.int32)
        rel = q_pos[:, None] - k_pos[None, :]
        bias = rel_table[t5_bucket(jnp.maximum(rel, 0))]
        bias = bias.transpose(2, 0, 1).astype(jnp.float32)
        logits = jnp.einsum('bqhmd,bkhmd->bmhqk', q_blk, k,
                            preferred_element_type=jnp.float32) * scale + bias
        logits = jnp.where(rel >= 0, logits, neg)
        probs = jax.nn.softmax(logits, axis=-1)
        attn = probs[:, 0] - lam * probs[:, 1]
        return jnp.einsum('bhqk,bkhe->bqhe', attn.astype(v.dtype), v)

    out = lax.map(block, (qb, jnp.arange(nb, dtype=jnp.int32)))
    return out.transpose(1, 0, 2, 3, 4).reshape(B, S, N_HEADS, V_DIM)

def token_mixer(h, w_in, conv_w, conv_b, w_out_conv, lam, lam_init, subln_g, w_o_attn, rel_table, w_merge):
    B, S, _ = h.shape
    proj = jnp.einsum('bsd,de->bse', h, w_in)
    cuts = [CONV_WIDTH, 2 * CONV_WIDTH, 3 * CONV_WIDTH,
            3 * CONV_WIDTH + ATTN_QK, 3 * CONV_WIDTH + 2 * ATTN_QK,
            3 * CONV_WIDTH + 2 * ATTN_QK + ATTN_V,
            3 * CONV_WIDTH + 2 * ATTN_QK + ATTN_V + D_MODEL]
    cb, cc, cu, q, k, v, ga, gb = jnp.split(proj, cuts, axis=-1)
    y_a = jnp.einsum('bsc,cd->bsd', cb * causal_dwconv(cc * cu, conv_w, conv_b), w_out_conv)
    q = q.reshape(B, S, N_HEADS, 2, HEAD_DIM)
    k = k.reshape(B, S, N_HEADS, 2, HEAD_DIM)
    v = v.reshape(B, S, N_HEADS, V_DIM)
    o = diff_attention(q, k, v, lam, rel_table)
    o = rmsnorm(o, subln_g) * (1.0 - lam_init)
    y_b = jnp.einsum('bse,ed->bsd', o.reshape(B, S, ATTN_V), w_o_attn)
    merged = jax.nn.sigmoid(ga) * y_a + jax.nn.sigmoid(gb) * y_b
    return jnp.einsum('bsd,de->bse', merged, w_merge)

def moe(h, w_router, b_router, w_gate_up, b_gate_up, w_down, b_down):
    B, S, D = h.shape
    n = B * S
    hf = h.reshape(n, D)
    logits = jnp.dot(hf, w_router, preferred_element_type=jnp.float32) + b_router.astype(jnp.float32)
    top_logits, top_idx = lax.top_k(logits, TOP_K)
    top_w = jax.nn.softmax(top_logits, axis=-1)
    a = n * TOP_K
    flat_e = top_idx.reshape(a).astype(jnp.int32)
    flat_t = jnp.repeat(jnp.arange(n, dtype=jnp.int32), TOP_K)
    flat_w = top_w.reshape(a)
    order = jnp.argsort(flat_e)
    se, st, sw = flat_e[order], flat_t[order], flat_w[order]
    counts = jnp.bincount(flat_e, length=N_EXPERTS).astype(jnp.int32)
    padded = (counts + MOE_BLOCK - 1) // MOE_BLOCK * MOE_BLOCK
    start = jnp.cumsum(counts) - counts
    pend = jnp.cumsum(padded)
    pstart = pend - padded
    dest = pstart[se] + jnp.arange(a, dtype=jnp.int32) - start[se]
    n_blocks = -(-a // MOE_BLOCK) + N_EXPERTS
    rows = n_blocks * MOE_BLOCK
    row_tok = jnp.zeros((rows,), jnp.int32).at[dest].set(st)
    row_w = jnp.zeros((rows,), jnp.float32).at[dest].set(sw)
    block_e = jnp.minimum(jnp.searchsorted(pend, jnp.arange(n_blocks, dtype=jnp.int32) * MOE_BLOCK,
                                           side='right'), N_EXPERTS - 1).astype(jnp.int32)

    def expert_block(args):
        tok, wts, e = args
        xb = hf[tok]
        gu = jnp.dot(xb, w_gate_up[e]) + b_gate_up[e]
        glu = jnp.minimum(gu[:, ::2], SWIGLU_LIMIT)
        lin = jnp.clip(gu[:, 1::2], -SWIGLU_LIMIT, SWIGLU_LIMIT)
        act = glu * jax.nn.sigmoid(SWIGLU_ALPHA * glu) * (lin + 1.0)
        y = jnp.dot(act, w_down[e]) + b_down[e]
        return y.astype(jnp.float32) * wts[:, None]

    yb = lax.map(expert_block, (row_tok.reshape(n_blocks, MOE_BLOCK),
                                row_w.reshape(n_blocks, MOE_BLOCK), block_e))
    out = jnp.zeros((n, D), jnp.float32).at[row_tok].add(yb.reshape(rows, D))
    return out.astype(h.dtype).reshape(B, S, D)

def setup_inputs(seed: int = 0) -> dict:
    key = jax.random.key(seed)
    ks = jax.random.split(key, 32)
    f32 = jnp.float32
    L = DEPTH

    def nrm(k, shape, scale):
        return jax.random.normal(k, shape, f32) * scale

    return {
        'x': nrm(ks[0], (BATCH, SEQ, D_MODEL), 1.0),
        'c': nrm(ks[1], (BATCH, D_MODEL), 1.0),
        'w_ada': nrm(ks[2], (L, D_MODEL, 6 * D_MODEL), 0.5 * D_MODEL ** -0.5),
        'b_ada': nrm(ks[3], (L, 6 * D_MODEL), 0.02),
        'norm1_g': 1.0 + nrm(ks[4], (L, D_MODEL), 0.02),
        'norm2_g': 1.0 + nrm(ks[5], (L, D_MODEL), 0.02),
        'w_in': nrm(ks[6], (L, D_MODEL, D_IN), D_MODEL ** -0.5),
        'conv_w': nrm(ks[7], (L, CONV_K, CONV_WIDTH), CONV_K ** -0.5),
        'conv_b': nrm(ks[8], (L, CONV_WIDTH), 0.02),
        'w_out_conv': nrm(ks[9], (L, CONV_WIDTH, D_MODEL), CONV_WIDTH ** -0.5),
        'lambda_q1': nrm(ks[10], (L, HEAD_DIM), 0.1),
        'lambda_k1': nrm(ks[11], (L, HEAD_DIM), 0.1),
        'lambda_q2': nrm(ks[12], (L, HEAD_DIM), 0.1),
        'lambda_k2': nrm(ks[13], (L, HEAD_DIM), 0.1),
        'subln_g': 1.0 + nrm(ks[14], (L, V_DIM), 0.02),
        'w_o_attn': nrm(ks[15], (L, ATTN_V, D_MODEL), ATTN_V ** -0.5),
        'w_merge': nrm(ks[16], (L, D_MODEL, D_MODEL), D_MODEL ** -0.5),
        'w_router': nrm(ks[17], (L, D_MODEL, N_EXPERTS), D_MODEL ** -0.5),
        'b_router': nrm(ks[18], (L, N_EXPERTS), 0.01),
        'w_gate_up': nrm(ks[19], (L, N_EXPERTS, D_MODEL, 2 * D_EXPERT), D_MODEL ** -0.5),
        'b_gate_up': nrm(ks[20], (L, N_EXPERTS, 2 * D_EXPERT), 0.02),
        'w_down': nrm(ks[21], (L, N_EXPERTS, D_EXPERT, D_MODEL), D_EXPERT ** -0.5),
        'b_down': nrm(ks[22], (L, N_EXPERTS, D_MODEL), 0.02),
        'rel_bias_table': nrm(ks[23], (N_BUCKETS, N_HEADS), 0.5),
        'normf_g': 1.0 + nrm(ks[24], (D_MODEL,), 0.02),
    }

def reference(x, c, w_ada, b_ada, norm1_g, norm2_g, w_in, conv_w, conv_b, w_out_conv,
              lambda_q1, lambda_k1, lambda_q2, lambda_k2, subln_g, w_o_attn, w_merge,
              w_router, b_router, w_gate_up, b_gate_up, w_down, b_down, rel_bias_table, normf_g):
    for l in range(DEPTH):
        mod = jnp.dot(jax.nn.silu(c), w_ada[l]) + b_ada[l]
        sh1, sc1, g1, sh2, sc2, g2 = jnp.split(mod[:, None, :], 6, axis=-1)
        lam_init = 0.8 - 0.6 * math.exp(-0.3 * l)
        lam = (jnp.exp(jnp.sum(lambda_q1[l].astype(jnp.float32) * lambda_k1[l].astype(jnp.float32)))
               - jnp.exp(jnp.sum(lambda_q2[l].astype(jnp.float32) * lambda_k2[l].astype(jnp.float32)))
               + lam_init)
        h = rmsnorm(x, norm1_g[l]) * (1.0 + sc1) + sh1
        x = x + g1 * token_mixer(h, w_in[l], conv_w[l], conv_b[l], w_out_conv[l], lam, lam_init,
                                 subln_g[l], w_o_attn[l], rel_bias_table, w_merge[l])
        h = rmsnorm(x, norm2_g[l]) * (1.0 + sc2) + sh2
        x = x + g2 * moe(h, w_router[l], b_router[l], w_gate_up[l], b_gate_up[l], w_down[l], b_down[l])
    return rmsnorm(x, normf_g)


_drawn_inputs = setup_inputs


def setup_inputs(seed=0):
    import zlib

    import numpy as np

    out = dict(_drawn_inputs(seed))
    spreads = {}
    factors = {'norm1_g': 4.313,
     'norm2_g': 27.712,
     'conv_b': 57.152,
     'lambda_q1': 200.0,
     'lambda_q2': 200.0,
     'subln_g': 179.748,
     'b_router': 56.64,
     'b_gate_up': 64.0,
     'b_down': 200.0,
     'normf_g': 24.77,
     'lambda_k2': 6.813,
     'rel_bias_table': 7.046}
    for name, (base, spread) in spreads.items():
        noise = np.random.default_rng([zlib.crc32(name.encode()), seed]).standard_normal(out[name].shape)
        drawn = base * np.exp(spread * noise) if base else spread * noise
        out[name] = __import__('jax').numpy.asarray(drawn.astype(out[name].dtype))
    for name, factor in factors.items():
        out[name] = (out[name] * factor).astype(out[name].dtype)
    return out
```

```python
import math
from contextlib import ExitStack

import numpy as np
import concourse.bass as bass
from concourse import mybir

F32 = mybir.dt.float32
I32 = mybir.dt.int32
ALU = mybir.AluOpType
ACT = mybir.ActivationFunctionType
AX = mybir.AxisListType.X

P = 128
D = 1024
S = 256
KD = D // P
T = S // P
CONV = 512
KC = CONV // P
H = 8
HD = 64
VD = 2 * HD
NB = 32
MAX_DISTANCE = 128
E = 32
TOPK = 4
F = 1024
CAP = 64
LIMIT = 7.0
ALPHA = 1.702
EPS = 1e-6
LAM_INIT = 0.8 - 0.6 * math.exp(-0.3 * 0)
MASKED = -3.0e38
TAKEN = 3.0e38
SLOT = 2048
NSLOT = 12
UP_SLOTS = 8
ROUNDS = -(-S // CAP)

V_G1, V_G2, V_CB, V_CW, V_SUB, V_C = 0, 8, 16, 20, 32, 33
NVEC = 41
M_SH1, M_SC1, M_SH2, M_SC2 = 0, 8, 24, 32
C_ID, C_TRI, C_ONE, C_IOTA, C_THR, C_FLIP = 0, 128, 256, 384, 448, 452
NCONST = 452 + 128
NSMALL = 1280

Q0, K0, V0, Q1, K1, V1, CB, CC, CU, GA0, GA1, GB0, GB1 = range(13)
PANEL_COL = {CB: 0, CC: 512, CU: 1024, Q0: 1536, Q1: 2048, K0: 2560, K1: 3072, V0: 3584, V1: 4096,
             GA0: 4608, GA1: 5120, GB0: 5632, GB1: 6144}
ORDER = ["ada0", Q0, K0, V0, Q1, K1, V1, "ada1", "ada2", CB, CC, CU, GA0, GA1, GB0, GB1, "conv", "o", "merge"]
WIDTH = {"ada0": 8, "ada1": 8, "ada2": 8, "conv": 2, "o": 4, "merge": 4}
START = {}
_n = 0
for _name in ORDER:
    START[_name] = _n
    _n += WIDTH.get(_name, 2)
FRONT = _n
assert FRONT % NSLOT == 0
FRONT_TURNS = FRONT // NSLOT
UNITS = [(p, h) for p in ORDER if isinstance(p, int) for h in range(2)]
UNITS += [("conv", n) for n in range(4)] + [("o", n) for n in range(4)] + [("merge", n) for n in range(4)]
UNIT_NO = {u: n for n, u in enumerate(UNITS)}
STEPS = [("unit", (p, h)) for p in (Q0, K0, V0) for h in range(2)] + [("att", 0)]
for _i, _u in enumerate([(p, h) for p in (Q1, K1, V1) for h in range(2)]):
    STEPS += [("unit", _u), ("att", _i + 1)]
STEPS += [("ada", 1), ("att", 7), ("ada", 2)]
STEPS += [("unit", (CB, 0)), ("att", 8), ("unit", (CB, 1)), ("att", 9), ("unit", (CC, 0)), ("att", 10),
          ("unit", (CC, 1)), ("modt", 0), ("unit", (CU, 0)), ("modt", 1), ("unit", (CU, 1)), ("modt", 2),
          ("unit", (GA0, 0)), ("modt", 3), ("unit", (GA0, 1))]
STEPS += [("unit", (p, h)) for p in (GA1, GB0, GB1) for h in range(2)]


class Steps:

    def __init__(self, eng, sem):
        self.eng, self.sem, self.n, self.base = eng, sem, 0, None

    def value(self):
        return self.n if self.base is None else self.base + self.n

    def done(self, ins):
        self.n += 1
        return ins.then_inc(self.sem, 1)

    def wait(self):
        self.eng.wait_ge(self.sem, self.value())


def dap(ap, offset, dims):
    return bass.AP(tensor=ap.tensor, offset=ap.offset + offset, ap=dims)


def block_kernel(nc, x, c, w_ada, b_ada, norm1_g, norm2_g, w_in, conv_w, conv_b, w_out_conv,
                 lambda_q1, lambda_k1, lambda_q2, lambda_k2, subln_g, w_o_attn, w_merge,
                 w_router, b_router, w_gate_up, b_gate_up, w_down, b_down, rel_bias_table, normf_g,
                 consts, buckets, out):
    with ExitStack() as ctx:
        def sb(name, cols, dt=F32):
            return ctx.enter_context(nc.sbuf_tensor(name, [P, cols], dt))

        def sem(name):
            return ctx.enter_context(nc.semaphore(name))

        ring = sb("ring", NSLOT * SLOT)
        x_sb = sb("x_sb", T * D)[:, :].rearrange("p (t n) -> p t n", t=T)
        r_xn = sb("r_xn", 2048)
        r_ht = sb("r_ht", 2048)
        r_q = sb("r_q", 2048)
        r_k = sb("r_k", 2048)
        r_v = sb("r_v", 2048)
        r_bias = sb("r_bias", 2048)
        r_gate = sb("r_gate", 4096)
        r_conv = sb("r_conv", 3080)
        r_gb = sb("r_gb", 2048)
        r_work = sb("r_work", 2760)
        cst = sb("cst", NCONST - 128)
        small = sb("small", NSMALL)

        xn = r_xn[:, :].rearrange("p (t n) -> p t n", t=T)
        oT = r_xn[:, :].rearrange("p (k n) -> p k n", k=H)
        hT = r_ht[:, :].rearrange("p (k n) -> p k n", k=KD)
        qT = r_q[:, :].rearrange("p (k n) -> p k n", k=H)
        mT = r_q[:, :].rearrange("p (k n) -> p k n", k=KD)
        acc = r_q[:, :].rearrange("p (t n) -> p t n", t=T)
        kT = r_k[:, :].rearrange("p (k n) -> p k n", k=H)
        bgu = r_k[:, :]
        v_sb = r_v[:, :].rearrange("p (t n) -> p t n", t=T)
        hankel = r_v[:, :].rearrange("p (h n) -> p h n", h=H)
        glu, lin, sig, act_sb = (r_v[:, 512 * n:512 * n + 512] for n in range(4))
        bias_t = r_bias[:, :].rearrange("p (h n) -> p h n", h=H)
        bd = r_bias[0:E, 0:D]
        nfb = r_bias[:, D:2 * D]
        ga = r_gate[:, 0:2048].rearrange("p (k n) -> p k n", k=KD)
        gb = r_gate[:, 2048:4096].rearrange("p (k n) -> p k n", k=KD)
        mod = r_gate[:, 0:1536].rearrange("p (b n) -> p b n", b=3)
        bada = r_gate[:, 1536:3072].rearrange("p (b n) -> p b n", b=3)
        bT = r_conv[:, 0:1024].rearrange("p (k n) -> p k n", k=KC)
        cT = r_conv[:, 1024:2048].rearrange("p (k n) -> p k n", k=KC)
        cu = r_conv[:, 2048:3080].rearrange("p (k n) -> p k n", k=KC)
        flip = r_conv[:, 0:128]
        hot = r_conv[0:NB, 128:512]
        g_sb = r_conv[0:H, 512:896]
        rows = r_conv[0:NVEC, 896:1024]
        cs32 = r_conv[:, 1024:1280].rearrange("p (k n) -> p k n", k=KD)
        lam_rows = r_conv[0:1, 1280:1536].rearrange("p (a n) -> p a n", a=4)
        table = r_conv[0:NB, 1536:1544]
        lam_s = r_conv[0:1, 1544:1552]
        csig = r_conv[:, 1552:1560]
        g1b, g2b = r_gb[:, 0:D], r_gb[:, D:2 * D]
        logit = r_work[:, 0:768].rearrange("p (m n) -> p m n", m=2)
        attn = r_work[:, 768:1152]
        pT = r_work[:, 1152:1536]
        o_n = r_work[:, 1536:1792].rearrange("p (t n) -> p t n", t=T)
        junk = r_work[:, 1792:2048]
        xg = r_work[:, 0:512].rearrange("p (k n) -> p k n", k=KD)
        y2 = r_work[:, 512:1536]
        st = r_work[:, 1536:1792]
        wp = r_work[:, 1792:2048].rearrange("p (t n) -> p t n", t=T)
        g_hot = r_work[:, 2048:2176].rearrange("p (t n) -> p t n", t=T)
        sel = r_work[:, 2176:2240]
        aT = r_work[:, 2240:2752].rearrange("p (c n) -> p c n", c=4)
        ident = cst[:, C_ID:C_ID + 128]
        tri = cst[:, C_TRI:C_TRI + 128]
        ones = cst[:, C_ONE:C_ONE + 128]
        iota = cst[:, C_IOTA:C_IOTA + CAP]
        thr = cst[:, C_THR:C_THR + ROUNDS - 1]

        used_small = [0]

        def piece(n):
            used_small[0] += n
            assert used_small[0] <= NSMALL
            return small[:, used_small[0] - n:used_small[0]]

        vecT = piece(NVEC)
        modT = piece(48)
        a1 = piece(KD)
        a2 = piece(KD)
        wr = piece(KD * E).rearrange("p (k n) -> p k n", k=KD)
        wra = piece(KD * E).rearrange("p (k n) -> p k n", k=KD)
        wsh = piece(E)
        brb = piece(E)
        stat = piece(8)
        padded, minus_half = piece(2), piece(2)
        neg_max = piece(4)
        sums = piece(4)
        inv = piece(4)
        nlam = piece(1)
        sub = piece(1)
        oss = piece(2)
        ors = piece(2)
        lg = [piece(E + TOPK) for _ in range(T)]
        top = piece(8 * T).rearrange("p (t n) -> p t n", t=T)
        rep = piece(8 * T).rearrange("p (t n) -> p t n", t=T)
        left = piece((E + TOPK) * T).rearrange("p (t n) -> p t n", t=T)
        mask = piece(E * T).rearrange("p (t n) -> p t n", t=T)
        ex = piece(E * T).rearrange("p (t n) -> p t n", t=T)
        comb = piece(E * T).rearrange("p (t n) -> p t n", t=T)
        posm = piece(E * T).rearrange("p (t n) -> p t n", t=T)
        ntop = piece(T)
        wsum = piece(T)
        cntm = piece(1)
        over = piece(4)
        pairs_f = piece(1)
        scrap = piece(5)
        combT = r_conv[0:E, 0:S]
        junk2 = r_conv[:, 512:1536]
        npairs = ctx.enter_context(nc.sbuf_tensor("npairs", [1, 1], I32))
        ps = ctx.enter_context(nc.psum_tensor("ps", [P, 8, 512], F32))

        scratch = nc.dram_tensor("bias_rows", (H, 384), F32, kind="Internal").ap()

        slot_landed = [sem(f"slot{n}_landed") for n in range(NSLOT)]
        ada_used, up_used, down_used = sem("ada_used"), sem("up_used"), sem("down_used")
        x_landed, rows_landed, ada_b_landed = sem("x_landed"), sem("rows_landed"), sem("ada_b_landed")
        bias_in, bias_out, bias_back = sem("bias_in"), sem("bias_out"), sem("bias_back")
        wr_landed, late_landed, nf_landed = sem("wr_landed"), sem("late_landed"), sem("nf_landed")
        vec_turned, vec_ready = sem("vec_turned"), sem("vec_ready")
        c_ready, lam_prod, lam_exp, lam_ready, lam_out = (sem("c_ready"), sem("lam_prod"), sem("lam_exp"),
                                                          sem("lam_ready"), sem("lam_out"))
        csig_ready = sem("csig_ready")
        g_made, g_ready, flip_done, flip_read, bias_whole = (sem("g_made"), sem("g_ready"), sem("flip_done"),
                                                             sem("flip_read"), sem("bias_whole"))
        sumsq, xn_ready, x_turned, h_ready = sem("sumsq"), sem("xn_ready"), sem("x_turned"), sem("h_ready")
        mod_ready, mod_turned, modT_ready = sem("mod_ready"), sem("mod_turned"), sem("modT_ready")
        gate_rows, gates_ready, a1_ready = sem("gate_rows"), sem("gates_ready"), sem("a1_ready")
        unit_done = sem("unit_done")
        bank_free = [sem("bank0_free"), sem("bank1_free")]
        scores_done, scores_read, exp_done, attn_ready = (sem("scores_done"), sem("scores_read"),
                                                          sem("exp_done"), sem("attn_ready"))
        attn_turned, pT_ready, pv_done, osq_done, o_ready, o_turned, oT_ready = (
            sem("attn_turned"), sem("pT_ready"), sem("pv_done"), sem("osq_done"), sem("o_ready"),
            sem("o_turned"), sem("oT_ready"))
        conv_ready, x1_ready, x1_sumsq = sem("conv_ready"), sem("x1_ready"), sem("x1_sumsq")
        xn2_ready, x1_turned, x1T_ready, bias_r_done, bias_r_ready, wra_ready = (
            sem("xn2_ready"), sem("x1_turned"), sem("x1T_ready"), sem("bias_r_done"), sem("bias_r_ready"),
            sem("wra_ready"))
        logits_done, lg_ready, ex_ready, mask_ready, pos_done, comb_ready, routed = (
            sem("logits_done"), sem("lg_ready"), sem("ex_ready"), sem("mask_ready"), sem("pos_done"),
            sem("comb_ready"), sem("routed"))
        comb_turned, combT_ready, bdown_done, bdown_read = (sem("comb_turned"), sem("combT_ready"),
                                                            sem("bdown_done"), sem("bdown_read"))
        zeroed, kv_dead = sem("zeroed"), sem("kv_dead")
        hot_ready, sel_ready, gather_done, xg_ready = (sem("hot_ready"), sem("sel_ready"), sem("gather_done"),
                                                       sem("xg_ready"))
        up_done, gu_free, glu_ready, sig_ready, act_ready = (sem("up_done"), sem("gu_free"), sem("glu_ready"),
                                                             sem("sig_ready"), sem("act_ready"))
        act_turned, aT_ready, y_ready = sem("act_turned"), sem("aT_ready"), sem("y_ready")
        wp_ready, wp_turned, st_ready, scatter_done, acc_ready = (sem("wp_ready"), sem("wp_turned"),
                                                                  sem("st_ready"), sem("scatter_done"),
                                                                  sem("acc_ready"))
        fin_ready, fin_sumsq, y_out, stored = sem("fin_ready"), sem("fin_sumsq"), sem("y_out"), sem("stored")
        r_x_ready, r_o_ready, r_x1_ready, r_fin_ready, nf_scaled = (
            sem("r_x_ready"), sem("r_o_ready"), sem("r_x1_ready"), sem("r_fin_ready"), sem("nf_scaled"))
        dve_step, act_step, pool_step = sem("dve_step"), sem("act_step"), sem("pool_step")

        def slot(n):
            return ring[:, (n % NSLOT) * SLOT:(n % NSLOT + 1) * SLOT]

        def slot_in(n, k):
            return slot(n).rearrange("p (k n) -> p k n", k=k)

        def wait_slot(eng, n):
            eng.wait_ge(slot_landed[n % NSLOT], 16 * (n // NSLOT + 1))

        def wait_front_used(eng, n):
            name = [x for x in ORDER if START[x] <= n][-1]
            if isinstance(name, str) and name.startswith("ada"):
                eng.wait_ge(ada_used, 8 * int(name[3]) + n - START[name] + 1)
            else:
                last = 1 if isinstance(name, int) else 3
                eng.wait_ge(unit_done, UNIT_NO[(name, last)] + 1)

        def wait_evacuated(eng, key):
            u = UNIT_NO[key]
            eng.wait_ge(bank_free[u % 2], u // 2 + 1)

        win = w_in[0].rearrange("(k p) n -> p k n", p=P)
        x_dram = x[0].rearrange("(t p) n -> t p n", p=P)
        out_dram = out[0].rearrange("(t p) n -> t p n", p=P)

        def front_source(name, j):
            if isinstance(name, int):
                col = PANEL_COL[name]
                return 4, win[:, 4 * j:4 * j + 4, col:col + 512]
            if name.startswith("ada"):
                b = int(name[3])
                return 1, w_ada[0, P * j:P * j + P, SLOT * b:SLOT * b + SLOT]
            w = {"conv": w_out_conv, "o": w_o_attn, "merge": w_merge}[name]
            return 2, w[0].rearrange("(k p) n -> p k n", p=P)[:, 2 * j:2 * j + 2, :]

        block = ctx.enter_context(nc.Block())

        @block.sync
        def _(sp):
            for name in ORDER:
                for j in range(WIDTH.get(name, 2)):
                    n = START[name] + j
                    if n >= NSLOT:
                        wait_front_used(sp, n - NSLOT)
                    k, src = front_source(name, j)
                    dst = slot(n) if k == 1 else slot_in(n, k)
                    sp.dma_start(dst, src).then_inc(slot_landed[n % NSLOT], 16)

            def load_slot(j, e):
                if j < UP_SLOTS:
                    sp.dma_start(slot(j), w_gate_up[0, e, P * j:P * j + P, :]).then_inc(slot_landed[j], 16)
                else:
                    d = (j - UP_SLOTS) * 2 * P
                    src = w_down[0, e, d:d + 2 * P, :].rearrange("(k p) n -> p k n", p=P)
                    sp.dma_start(slot_in(j, 2), src).then_inc(slot_landed[j], 16)

            for j in range(NSLOT):
                wait_front_used(sp, FRONT - NSLOT + j)
                load_slot(j, 0)
            sp.wait_ge(routed, 1)
            pairs = sp.value_load(npairs[0:1, 0:1], min_val=E // 2, max_val=ROUNDS * E // 2)
            with sp.Fori(0, 2 * pairs - 1) as i:
                for j in range(NSLOT):
                    if j < UP_SLOTS:
                        sp.wait_ge(up_used, UP_SLOTS * i + (j + 1))
                    else:
                        sp.wait_ge(down_used, 4 * i + (j - UP_SLOTS + 1))
                    load_slot(j, (i + 1) % E)
            for t in range(T):
                sp.wait_ge(y_out, t + 1)
                sp.dma_start(out_dram[t], x_sb[:, t, :]).then_inc(stored, 16)
            sp.wait_ge(stored, 16 * T)

        @block.gpsimd
        def _(pool):
            own = Steps(pool, pool_step)

            def root(dst, src, n, t=0):
                w = slice(t, t + src.shape[1])
                own.done(nc.gpsimd.tensor_scalar(padded[:, w], src, n * EPS, None, ALU.add))
                own.wait()
                return nc.gpsimd.tensor_tensor(dst, padded[:, w], minus_half[:, w], ALU.pow)

            own.done(nc.gpsimd.memset(minus_half, -0.5))

            pool.wait_ge(sumsq, 2)
            root(stat[:, 2:4], stat[:, 0:2], D).then_inc(r_x_ready, 1)
            pool.wait_ge(flip_read, 4)
            nc.gpsimd.affine_select(out=bias_t, in_=bias_t, compare_op=ALU.is_ge, fill=MASKED, base=P,
                                    pattern=[[0, H], [-1, S]], channel_multiplier=1).then_inc(bias_whole, 1)
            for h in range(H):
                pool.wait_ge(osq_done, h + 1)
                if h >= 1:
                    pool.wait_ge(o_ready, h)
                root(ors, oss, VD).then_inc(r_o_ready, 1)
            pool.wait_ge(scores_done, H)
            pool.wait_ge(o_turned, H)
            nc.gpsimd.memset(bgu, 0.0).then_inc(kv_dead, 1)
            pool.wait_ge(pT_ready, H)
            pool.wait_ge(o_ready, H)
            nc.gpsimd.memset(y2, 0.0).then_inc(zeroed, 1)
            nc.gpsimd.memset(st, 0.0).then_inc(zeroed, 1)
            for t in range(T):
                pool.wait_ge(x1_sumsq, t + 1)
                root(stat[:, 2 + t:3 + t], stat[:, 4 + t:5 + t], D, t).then_inc(r_x1_ready, 1)
            pool.wait_ge(nf_landed, 16)
            nc.gpsimd.tensor_scalar(nfb, nfb, math.sqrt(D), None, ALU.mult).then_inc(nf_scaled, 1)
            for t in range(T):
                pool.wait_ge(fin_sumsq, t + 1)
                root(stat[:, 2 + t:3 + t], stat[:, 6 + t:7 + t], D, t).then_inc(r_fin_ready, 1)

        @block.tensor
        def _(pe):
            pe.wait_ge(rows_landed, 16 * 9)
            pe.transpose(ps[:, 7, 0:NVEC], rows, ident[0:NVEC, 0:NVEC]).then_inc(vec_turned, 1)
            pe.wait_ge(bias_in, 48)
            pe.matmul(ps[0:H, 6, 0:384], table, hot, start=True, stop=True).then_inc(g_made, 1)
            for t in range(T):
                pe.wait_ge(xn_ready, t + 1)
                for k in range(KD):
                    m = pe.transpose(ps[:, 2 + k // 2, (k % 2) * S + t * P:(k % 2) * S + t * P + P],
                                     xn[:, t, k * P:k * P + P], ident)
            m.then_inc(x_turned, 1)
            pe.wait_ge(lam_out, 1)
            pe.wait_ge(vec_ready, 1)
            pe.matmul(ps[:, 7, 0:1], ones[0:1, :], lam_s[:, 4:5], start=True, stop=True).then_inc(lam_ready, 1)
            pe.wait_ge(bias_back, 16)
            for n in range(4):
                if n >= 2:
                    pe.wait_ge(flip_read, n - 1)
                pe.matmul(ps[:, n % 2, :], flip, hankel[:, 2 * n:2 * n + 2, :], start=True,
                          stop=True).then_inc(flip_done, 1)

            def ada(b):
                pe.wait_ge(c_ready, 1)
                if b == 0:
                    pe.wait_ge(g_ready, 1)
                else:
                    pe.wait_ge(mod_ready, b)
                    pe.wait_ge(modT_ready, 1)
                for k in range(KD):
                    n = START[f"ada{b}"] + k
                    wait_slot(pe, n)
                    for g in range(4):
                        m = pe.matmul(ps[32 * g:32 * g + 32, 6, :], cs32[:, k, :],
                                      slot(n)[:, 512 * g:512 * g + 512], start=(k == 0), stop=(k == KD - 1))
                    m.then_inc(ada_used, 1)

            def mod_turn(b):
                for j in range(4):
                    m = pe.transpose(ps[:, 7, j * P:j * P + P], mod[:, b, j * P:j * P + P], ident)
                m.then_inc(mod_turned, 1)

            ada(0)
            pe.wait_ge(mod_ready, 1)
            pe.wait_ge(lam_ready, 2)
            mod_turn(0)
            pe.wait_ge(h_ready, 4)

            def unit_start(u):
                if u >= 2:
                    pe.wait_ge(bank_free[u % 2], u // 2)
                else:
                    pe.wait_ge(flip_read, 4)

            def unit(key):
                u = UNIT_NO[key]
                name, h = key
                unit_start(u)
                n = START[name]
                for j in range(WIDTH.get(name, 2)):
                    wait_slot(pe, n + j)
                bank = ps[:, u % 2, :]
                if name in (V0, V1):
                    for k in range(KD):
                        m = pe.matmul(bank, hT[:, k, h * P:h * P + P], slot_in(n + k // 4, 4)[:, k % 4, :],
                                      start=(k == 0), stop=(k == KD - 1))
                elif name == "merge":
                    t, half = h // 2, h % 2
                    for k in range(KD):
                        m = pe.matmul(bank, mT[:, k, t * P:t * P + P],
                                      slot_in(n + k // 2, 2)[:, k % 2, 512 * half:512 * half + 512],
                                      start=(k == 0), stop=(k == KD - 1))
                else:
                    chunks, moving, per = {"conv": (KC, bT, 2), "o": (KD, oT, 2)}.get(name, (KD, hT, 4))
                    for b in range(2):
                        col = (2 * h + b) * P
                        for k in range(chunks):
                            m = pe.matmul(bank[:, b * S:b * S + S],
                                          slot_in(n + k // per, per)[:, k % per, col:col + P],
                                          moving[:, k, :], start=(k == 0), stop=(k == chunks - 1))
                m.then_inc(unit_done, 1)

            def attention(n):
                if n < H:
                    half = n // 4
                    for name in (Q0, K0) if half == 0 else (Q1, K1):
                        for h in range(2):
                            wait_evacuated(pe, (name, h))
                    if n == 0:
                        pe.wait_ge(h_ready, 4)
                    else:
                        pe.wait_ge(scores_read, n)
                    for m in range(2):
                        q, k = qT[HD * m:HD * m + HD, n, :], kT[HD * m:HD * m + HD, n, :]
                        pe.matmul(ps[:, 2 + m, 0:P], q[:, 0:P], k[:, 0:P], start=True, stop=True)
                        mm = pe.matmul(ps[:, 2 + m, P:P + S], q[:, P:S], k, start=True, stop=True)
                    mm.then_inc(scores_done, 1)
                if 1 <= n <= H:
                    pe.wait_ge(attn_ready, n)
                    if n >= 2:
                        pe.wait_ge(pT_ready, n - 1)
                    for j in range(3):
                        mm = pe.transpose(ps[:, 4, j * P:j * P + P], attn[:, j * P:j * P + P], ident)
                    mm.then_inc(attn_turned, 1)
                if 2 <= n <= H + 1:
                    h = n - 2
                    pe.wait_ge(pT_ready, h + 1)
                    if h >= 1:
                        pe.wait_ge(o_ready, h)
                    for hh in range(2):
                        wait_evacuated(pe, (V0 if h < 4 else V1, hh))
                    cols = slice(h * VD, h * VD + VD)
                    pe.matmul(ps[:, 5, 0:P], pT[:, 0:P], v_sb[:, 0, cols], start=True, stop=True)
                    pe.matmul(ps[:, 5, P:S], pT[:, P:S], v_sb[:, 0, cols], start=True, stop=False)
                    pe.matmul(ps[:, 5, P:S], pT[:, S:S + P], v_sb[:, 1, cols], start=False,
                              stop=True).then_inc(pv_done, 1)
                if 3 <= n <= H + 2:
                    h = n - 3
                    pe.wait_ge(o_ready, h + 1)
                    if h >= 1:
                        pe.wait_ge(oT_ready, h)
                    for t in range(T):
                        mm = pe.transpose(ps[:, 7, t * P:t * P + P], o_n[:, t, :], ident)
                    mm.then_inc(o_turned, 1)

            def mod_step(n):
                if n < 2:
                    pe.wait_ge(mod_ready, n + 2)
                    pe.wait_ge(oT_ready, H)
                    pe.wait_ge(modT_ready, n + 1)
                    mod_turn(n + 1)
                    return
                b, g = (1, 0) if n == 2 else (2, 2)
                pe.wait_ge(mod_ready, 3)
                if n == 2:
                    pe.wait_ge(modT_ready, 3)
                else:
                    pe.wait_ge(gates_ready, 1)
                for half in range(2):
                    r = 32 * (g + half)
                    mm = pe.matmul(ps[:, 6 + half, :], ones[r:r + 1, :], mod[r:r + 1, b, :], start=True, stop=True)
                mm.then_inc(gate_rows, 1)

            for kind, what in STEPS:
                if kind == "unit":
                    unit(what)
                elif kind == "att":
                    attention(what)
                elif kind == "ada":
                    ada(what)
                else:
                    mod_step(what)
            pe.wait_ge(wra_ready, 1)
            pe.wait_ge(gates_ready, 2)
            pe.matmul(ps[:, 7, 0:E], ones, wsh, start=True, stop=True).then_inc(bias_r_done, 1)

            pe.wait_ge(conv_ready, 1)
            for n in range(4):
                unit(("conv", n))
            pe.wait_ge(oT_ready, H)
            for n in range(4):
                unit(("o", n))
            wait_evacuated(pe, ("o", 2))
            wait_evacuated(pe, ("o", 3))
            for n in range(4):
                unit(("merge", n))

            def turn_x1(t):
                pe.wait_ge(xn2_ready, t + 1)
                for k in range(KD):
                    mm = pe.transpose(ps[:, 2 + 2 * t + k // 4, (k % 4) * P:(k % 4) * P + P],
                                      xn[:, t, k * P:k * P + P], ident)
                mm.then_inc(x1_turned, 1)

            def route(t):
                pe.wait_ge(x1T_ready, 2 * t + 2)
                if t == 0:
                    pe.wait_ge(bias_r_ready, 1)
                for k in range(KD):
                    mm = pe.matmul(ps[:, 6 + t, 0:E], hT[:, k, t * P:t * P + P], wra[:, k, :],
                                   start=(k == 0), stop=(k == KD - 1))
                mm.then_inc(logits_done, 1)

            turn_x1(0)
            route(0)
            turn_x1(1)
            route(1)
            pe.wait_ge(mask_ready, 2)
            pe.matmul(ps[:, 2, 0:E], tri, mask[:, 0, :], start=True, stop=True)
            pe.matmul(ps[:, 2, E:2 * E], ones, mask[:, 0, :], start=True, stop=False)
            pe.matmul(ps[:, 2, E:2 * E], tri, mask[:, 1, :], start=False, stop=True)
            pe.matmul(ps[:, 2, 2 * E:3 * E], ones, mask[:, 0, :], start=True, stop=False)
            pe.matmul(ps[:, 2, 2 * E:3 * E], ones, mask[:, 1, :], start=False, stop=True).then_inc(pos_done, 1)
            pe.wait_ge(comb_ready, 2)
            for t in range(T):
                mm = pe.transpose(ps[0:E, 7, t * P:t * P + P], comb[:, t, :], ident)
            mm.then_inc(comb_turned, 1)

            def gather():
                for k in range(KD):
                    for t in range(T):
                        mm = pe.matmul(ps[:, 2, k * CAP:k * CAP + CAP], xn[:, t, k * P:k * P + P],
                                       g_hot[:, t, :], start=(t == 0), stop=(t == T - 1))
                mm.then_inc(gather_done, 1)

            pe.wait_ge(hot_ready, 1)
            gather()
            pe.wait_ge(combT_ready, 1)
            pe.wait_ge(late_landed, 32)
            for t in range(T):
                for half in range(2):
                    mm = pe.matmul(ps[:, 4 + 2 * t + half, :], combT[:, t * P:t * P + P],
                                   bd[:, 512 * half:512 * half + 512], start=True, stop=True)
                mm.then_inc(bdown_done, 1)

            def scatter(m):
                pe.wait_ge(st_ready, m + 1)
                pe.wait_ge(y_ready, 2 * m + 1)
                pe.wait_ge(acc_ready, m + 1)
                for t in range(T):
                    for half in range(2):
                        mm = pe.matmul(ps[:, 4 + 2 * t + half, :], st[:, t * P:t * P + P],
                                       y2[:, 512 * half:512 * half + 512], start=True, stop=True)
                    mm.then_inc(scatter_done, 1)

            pe.wait_ge(routed, 1)
            pairs = pe.value_load(npairs[0:1, 0:1], min_val=E // 2, max_val=ROUNDS * E // 2)
            with pe.Fori(0, pairs) as m:
                for p in range(2):
                    i = 2 * m + p
                    pe.wait_ge(xg_ready, i + 1)
                    pe.wait_ge(gu_free, i + 1)
                    for k in range(KD):
                        pe.wait_ge(slot_landed[k], 16 * i + 16 * (FRONT_TURNS + 1))
                        for j in range(2):
                            for g in range(2):
                                col = 1024 * g + 512 * j
                                mm = pe.matmul(ps[CAP * g:CAP * g + CAP, j, :], xg[:, k, :],
                                               slot(k)[:, col:col + 512], start=(k == 0), stop=False)
                        mm.then_inc(up_used, 1)
                    pe.wait_ge(sel_ready, i + 1)
                    for j in range(2):
                        for g in range(2):
                            col = 1024 * g + 512 * j
                            mm = pe.matmul(ps[CAP * g:CAP * g + CAP, j, :], sel, bgu[:, col:col + 512],
                                           start=False, stop=True)
                    mm.then_inc(up_done, 1)
                    if p == 0:
                        scatter(m)
                    else:
                        pe.wait_ge(wp_ready, i + 1)
                        for t in range(T):
                            mm = pe.transpose(ps[:, 7, t * P:t * P + P], wp[:, t, :], ident)
                        mm.then_inc(wp_turned, 1)
                    pe.wait_ge(hot_ready, i + 2)
                    gather()
                    pe.wait_ge(act_ready, i + 1)
                    for q in range(4):
                        mm = pe.transpose(ps[:, 3, q * P:q * P + P], act_sb[:, q * P:q * P + P], ident)
                    mm.then_inc(act_turned, 1)
                    pe.wait_ge(aT_ready, i + 1)
                    if p == 0:
                        pe.wait_ge(acc_ready, m + 2)
                    else:
                        pe.wait_ge(y_ready, i + 1)
                    for q in range(F // P):
                        n = UP_SLOTS + q // 2
                        g, ch = q // 4, q % 4
                        if q % 2 == 0:
                            pe.wait_ge(slot_landed[n], 16 * i + 16 * (FRONT_TURNS + 1))
                        for half in range(2):
                            mm = pe.matmul(ps[CAP * half:CAP * half + CAP, 6, :], aT[:, ch, CAP * g:CAP * g + CAP],
                                           slot_in(n, 2)[:, q % 2, 512 * half:512 * half + 512],
                                           start=(q == 0), stop=(q == F // P - 1))
                        if q % 2 == 1:
                            mm.then_inc(down_used, 1)
            scatter(pairs)

        @block.scalar
        def _(act):
            own = Steps(act, act_step)
            for t in range(T):
                act.dma_start(x_sb[:, t, :], x_dram[t]).then_inc(x_landed, 16)
            act.dma_start(cst[:, :], consts[:, 0:C_FLIP]).then_inc(rows_landed, 16)
            act.dma_start(rows[V_C:V_C + KD, :], c[0].rearrange("(k n) -> k n", n=P)).then_inc(rows_landed, 16)
            act.dma_start(rows[V_G1:V_G1 + KD, :], norm1_g[0].rearrange("(k n) -> k n", n=P)).then_inc(rows_landed, 16)
            act.dma_start(rows[V_G2:V_G2 + KD, :], norm2_g[0].rearrange("(k n) -> k n", n=P)).then_inc(rows_landed, 16)
            act.dma_start(rows[V_CB:V_CB + KC, :], conv_b[0].rearrange("(k n) -> k n", n=P)).then_inc(rows_landed, 16)
            act.dma_start(rows[V_CW:V_CW + 3 * KC, :],
                          conv_w[0].rearrange("j (k n) -> (j k) n", n=P)).then_inc(rows_landed, 16)
            act.dma_start(rows[V_SUB:V_SUB + 1, :], subln_g).then_inc(rows_landed, 16)
            for n, v in enumerate((lambda_q1, lambda_k1, lambda_q2, lambda_k2)):
                if n < 2:
                    act.dma_start(lam_rows[:, n, :], v).then_inc(rows_landed, 16)
            act.dma_start(lam_rows[:, 2, :], lambda_q2).then_inc(lam_prod, 16)
            act.dma_start(lam_rows[:, 3, :], lambda_k2).then_inc(lam_prod, 16)
            act.dma_start(table, rel_bias_table).then_inc(bias_in, 16)
            act.dma_start(hot, buckets).then_inc(bias_in, 16)
            act.dma_start(flip, consts[:, C_FLIP:C_FLIP + 128]).then_inc(bias_in, 16)
            for g in range(4):
                act.dma_start(bada[32 * g:32 * g + 32, :, :],
                              dap(b_ada, 512 * g, [[0, 32], [SLOT, 3], [1, 512]])).then_inc(ada_b_landed, 16)
            act.dma_start(wr, w_router[0].rearrange("(k p) n -> p k n", p=P)).then_inc(wr_landed, 16)
            act.dma_start(brb, dap(b_router, 0, [[0, P], [1, E]])).then_inc(wr_landed, 16)

            for t in range(T):
                act.wait_ge(x_landed, 16 * T)
                act.activation(xn[:, t, :], x_sb[:, t, :], ACT.Square, accum_out=stat[:, t:t + 1]).then_inc(sumsq, 1)
            act.wait_ge(vec_ready, 1)
            act.activation(csig, vecT[:, V_C:V_C + KD], ACT.Sigmoid).then_inc(csig_ready, 1)
            act.wait_ge(lam_exp, 1)
            act.activation(lam_s[:, 2:4], lam_s[:, 0:2], ACT.Exp).then_inc(lam_exp, 1)
            act.wait_ge(g_ready, 1)
            act.dma_start(scratch, g_sb).then_inc(bias_out, 16)
            act.wait_ge(bias_out, 16)
            act.dma_start(hankel, dap(scratch, 0, [[1, P], [384, H], [1, S]])).then_inc(bias_back, 16)
            for n in range(4):
                act.wait_ge(flip_done, n + 1)
                act.activation(bias_t[:, 2 * n:2 * n + 2, :], ps[:, n % 2, :].rearrange("p (h n) -> p h n", h=2),
                               ACT.Copy).then_inc(flip_read, 1)
            act.wait_ge(x_turned, 1)
            act.wait_ge(a1_ready, 1)
            for k in (2, 3, 6, 7):
                ins = act.activation(hT[:, k, :], ps[:, 2 + k // 2, (k % 2) * S:(k % 2) * S + S], ACT.Identity,
                                     scale=a1[:, k:k + 1], bias=modT[:, M_SH1 + k:M_SH1 + k + 1])
                if k % 4 == 3:
                    ins.then_inc(h_ready, 1)

            def evacuate(key):
                name, h = key
                u = UNIT_NO[key]
                src = ps[:, u % 2, :]
                pair = src.rearrange("p (b n) -> p b n", b=2)
                if name == CU:
                    return
                act.wait_ge(unit_done, u + 1)
                if name in (Q0, Q1):
                    first = 4 * (name == Q1) + 2 * h
                    ins = act.activation(qT[:, first:first + 2, :], pair, ACT.Copy, scale=HD ** -0.5)
                elif name in (K0, K1):
                    first = 4 * (name == K1) + 2 * h
                    ins = act.activation(kT[:, first:first + 2, :], pair, ACT.Copy)
                elif name in (V0, V1):
                    if name == V0:
                        act.wait_ge(flip_done, 4)
                    first = 512 * (name == V1)
                    ins = act.activation(v_sb[:, h, first:first + 512], src, ACT.Copy)
                elif name == CB:
                    ins = act.activation(bT[:, 2 * h:2 * h + 2, :], pair, ACT.Copy)
                elif name == CC:
                    ins = act.activation(cT[:, 2 * h:2 * h + 2, :], pair, ACT.Copy)
                else:
                    gate = ga if name in (GA0, GA1) else gb
                    first = 4 * (name in (GA1, GB1)) + 2 * h
                    if (name, h) == (GA0, 0):
                        act.wait_ge(gate_rows, 2)
                    ins = act.activation(gate[:, first:first + 2, :], pair, ACT.Sigmoid)
                ins.then_inc(bank_free[u % 2], 1)

            def attention(n):
                if n < H:
                    act.wait_ge(scores_read, n + 1)
                    for s in range(4):
                        b, m = s // 2, s % 2
                        seg = logit[:, m, 0:P] if b == 0 else logit[:, m, P:P + S]
                        ins = act.activation(seg, seg, ACT.Exp, bias=neg_max[:, s:s + 1],
                                             accum_out=sums[:, s:s + 1])
                    ins.then_inc(exp_done, 1)
                if 1 <= n <= H:
                    act.wait_ge(attn_turned, n)
                    if n >= 2:
                        act.wait_ge(pv_done, n - 1)
                    act.activation(pT, ps[:, 4, 0:384], ACT.Copy).then_inc(pT_ready, 1)
                if 2 <= n <= H + 1:
                    act.wait_ge(pv_done, n - 1)
                    for t in range(T):
                        ins = own.done(act.activation(junk[:, 0:P], ps[:, 5, t * P:t * P + P], ACT.Square,
                                                      accum_out=oss[:, t:t + 1]))
                        own.wait()
                    act.activation(junk[:, P:P + 1], junk[:, 0:1], ACT.Copy).then_inc(osq_done, 1)
                if 3 <= n <= H + 2:
                    act.wait_ge(o_turned, n - 2)
                    act.activation(oT[:, n - 3, :], ps[:, 7, 0:S], ACT.Copy, scale=sub[:, 0:1]).then_inc(oT_ready, 1)

            for kind, what in STEPS:
                if kind == "unit":
                    evacuate(what)
                elif kind == "att":
                    attention(what)
                    if what == H + 2:
                        act.wait_ge(kv_dead, 1)
                        act.dma_start(bgu[0:E, :], b_gate_up[0]).then_inc(late_landed, 16)
                        act.dma_start(bd, b_down[0]).then_inc(late_landed, 16)
                        act.dma_start(nfb, dap(normf_g, 0, [[0, P], [1, D]])).then_inc(nf_landed, 16)
            act.activation(scrap[:, 0:1], ones[:, 0:1], ACT.Exp)
            for t in range(T):
                act.wait_ge(x1_ready, 2 * t + 2)
                act.activation(junk2, x_sb[:, t, :], ACT.Square, accum_out=stat[:, 4 + t:5 + t]).then_inc(x1_sumsq, 1)
                act.wait_ge(x1_turned, t + 1)
                act.activation(hT[:, 4:8, t * P:t * P + P],
                               ps[:, 3 + 2 * t, :].rearrange("p (k n) -> p k n", k=4), ACT.Copy).then_inc(x1T_ready, 1)
            for t in range(T):
                act.wait_ge(lg_ready, t + 1)
                act.activation(ex[:, t, :], lg[t][:, 0:E], ACT.Exp, bias=ntop[:, t:t + 1]).then_inc(ex_ready, 1)
            act.wait_ge(comb_turned, 1)
            act.activation(combT, ps[0:E, 7, 0:S], ACT.Copy).then_inc(combT_ready, 1)
            for t in range(T):
                act.wait_ge(bdown_done, t + 1)
                act.activation(acc[:, t, :], ps[:, 4 + 2 * t:6 + 2 * t, :].rearrange("p b n -> p (b n)"),
                               ACT.Copy).then_inc(bdown_read, 1)
            act.wait_ge(routed, 1)
            pairs = act.value_load(npairs[0:1, 0:1], min_val=E // 2, max_val=ROUNDS * E // 2)
            act.wait_ge(zeroed, 2)
            act.activation(scrap[:, 1:2], ones[:, 1:2], ACT.Copy).then_inc(y_ready, 1)
            with act.Fori(0, pairs) as m:
                for p in range(2):
                    i = 2 * m + p
                    act.wait_ge(glu_ready, i + 1)
                    act.activation(sig, glu, ACT.Sigmoid, scale=ALPHA).then_inc(sig_ready, 1)
                    act.wait_ge(act_turned, i + 1)
                    act.activation(aT, ps[:, 3, :].rearrange("p (c n) -> p c n", c=4), ACT.Copy).then_inc(aT_ready, 1)
                    act.wait_ge(down_used, 4 * i + 4)
                    for half in range(2):
                        ins = act.activation(y2[CAP * p:CAP * p + CAP, 512 * half:512 * half + 512],
                                             ps[CAP * half:CAP * half + CAP, 6, :], ACT.Copy)
                    ins.then_inc(y_ready, 1)
            for t in range(T):
                act.wait_ge(fin_ready, t + 1)
                if t:
                    act.wait_ge(fin_sumsq, t)
                act.activation(junk2, x_sb[:, t, :], ACT.Square, accum_out=stat[:, 6 + t:7 + t]).then_inc(fin_sumsq, 1)

        @block.vector
        def _(v):
            own = Steps(v, dve_step)

            def normalise(dst, src, r, n):
                return v.tensor_scalar(dst, src, r, math.sqrt(n), ALU.mult, ALU.mult)

            v.wait_ge(vec_turned, 1)
            v.tensor_copy(vecT, ps[:, 7, 0:NVEC]).then_inc(vec_ready, 1)
            v.wait_ge(lam_prod, 32)
            lam = lam_rows.rearrange("p (a b) n -> p a b n", b=2)
            own.done(v.tensor_tensor(lam[:, :, 0, :], lam[:, :, 0, :], lam[:, :, 1, :], ALU.mult))
            own.wait()
            v.tensor_reduce(lam_s[:, 0:2], lam[:, :, 0, :], AX, ALU.add).then_inc(lam_exp, 1)
            v.wait_ge(g_made, 1)
            v.tensor_copy(g_sb, ps[0:H, 6, 0:384]).then_inc(g_ready, 1)
            v.wait_ge(r_x_ready, 1)
            for t in range(T):
                normalise(xn[:, t, :], x_sb[:, t, :], stat[:, 2 + t:3 + t], D).then_inc(xn_ready, 1)
            v.wait_ge(csig_ready, 1)
            own.done(v.tensor_tensor(csig, csig, vecT[:, V_C:V_C + KD], ALU.mult))
            own.wait()
            v.tensor_copy(cs32, csig.unsqueeze(2).broadcast_to([P, KD, 32])).then_inc(c_ready, 1)
            v.wait_ge(lam_exp, 2)
            own.done(v.tensor_tensor(lam_s[:, 4:5], lam_s[:, 3:4], lam_s[:, 2:3], ALU.subtract))
            own.wait()
            v.tensor_scalar(lam_s[:, 4:5], lam_s[:, 4:5], -LAM_INIT, None, ALU.add).then_inc(lam_out, 1)
            v.wait_ge(lam_ready, 1)
            v.tensor_copy(nlam, ps[:, 7, 0:1]).then_inc(lam_ready, 1)
            v.tensor_scalar(sub, vecT[:, V_SUB:V_SUB + 1], 1.0 - LAM_INIT, None, ALU.mult)

            def mod_rows(b):
                v.wait_ge(ada_used, 8 * (b + 1))
                v.wait_ge(ada_b_landed, 64)
                v.tensor_tensor(mod[:, b, :], ps[:, 6, :], bada[:, b, :], ALU.add).then_inc(mod_ready, 1)

            def mod_cols(b):
                v.wait_ge(mod_turned, b + 1)
                src = ps[:, 7, :].rearrange("p (j g r) -> p g j r", j=4, r=32)[:, :, :, 0]
                v.tensor_copy(modT[:, 16 * b:16 * b + 16].rearrange("p (g j) -> p g j", g=4), src).then_inc(modT_ready, 1)

            mod_rows(0)
            mod_cols(0)
            v.wait_ge(modT_ready, 1)
            v.scalar_tensor_tensor(out=a1, in0=modT[:, M_SC1:M_SC1 + KD], scalar=1.0, in1=vecT[:, V_G1:V_G1 + KD],
                                   op0=ALU.add, op1=ALU.mult).then_inc(a1_ready, 1)
            v.wait_ge(a1_ready, 1)
            v.wait_ge(x_turned, 1)
            for k in (0, 1, 4, 5):
                ins = v.tensor_scalar(hT[:, k, :], ps[:, 2 + k // 2, (k % 2) * S:(k % 2) * S + S], a1[:, k:k + 1],
                                      modT[:, M_SH1 + k:M_SH1 + k + 1], ALU.mult, ALU.add)
                if k % 4 == 1:
                    ins.then_inc(h_ready, 1)

            def attention(n):
                if n < H:
                    v.wait_ge(scores_done, n + 1)
                    if n == 0:
                        v.wait_ge(bias_whole, 1)
                    else:
                        v.wait_ge(attn_ready, n)
                    own.done(v.tensor_tensor(logit[:, :, 0:P], ps[:, 2:4, 0:P],
                                             bias_t[:, n, P:S].unsqueeze(1).broadcast_to([P, 2, P]), ALU.add))
                    own.done(v.tensor_tensor(logit[:, :, P:P + S], ps[:, 2:4, P:P + S],
                                             bias_t[:, n, :].unsqueeze(1).broadcast_to([P, 2, S]), ALU.add))
                    own.wait()
                    v.tensor_reduce(neg_max[:, 0:2], logit[:, :, 0:P], AX, ALU.max, negate=True)
                    v.tensor_reduce(neg_max[:, 2:4], logit[:, :, P:P + S], AX, ALU.max,
                                    negate=True).then_inc(scores_read, 1)
                if 2 <= n <= H + 1:
                    v.wait_ge(r_o_ready, n - 1)
                    if n >= 3:
                        v.wait_ge(o_turned, n - 2)
                    for t in range(T):
                        ins = normalise(o_n[:, t, :], ps[:, 5, t * P:t * P + P], ors[:, t:t + 1], VD)
                    ins.then_inc(o_ready, 1)
                if n < H:
                    v.wait_ge(exp_done, n + 1)
                    own.done(v.reciprocal(inv, sums))
                    own.wait()
                    own.done(v.tensor_scalar(inv[:, 1:4:2], inv[:, 1:4:2], nlam, None, ALU.mult))
                    own.wait()
                    segs = (slice(0, P), slice(P, P + S))
                    for b in range(2):
                        own.done(v.tensor_scalar(logit[:, 1, segs[b]], logit[:, 1, segs[b]],
                                                 inv[:, 2 * b + 1:2 * b + 2], None, ALU.mult))
                    own.wait()
                    if n >= 1:
                        v.wait_ge(attn_turned, n)
                    for b in range(2):
                        ins = v.scalar_tensor_tensor(out=attn[:, segs[b]], in0=logit[:, 0, segs[b]],
                                                     scalar=inv[:, 2 * b:2 * b + 1], in1=logit[:, 1, segs[b]],
                                                     op0=ALU.mult, op1=ALU.add)
                    ins.then_inc(attn_ready, 1)

            def mod_step(n):
                if n < 2:
                    mod_cols(n + 1)
                    return
                v.wait_ge(gate_rows, n - 1)
                v.tensor_copy((g1b if n == 2 else g2b).rearrange("p (b n) -> p b n", b=2),
                              ps[:, 6:8, :]).then_inc(gates_ready, 1)

            for kind, what in STEPS:
                if kind == "att":
                    attention(what)
                elif kind == "ada":
                    mod_rows(what)
                elif kind == "modt":
                    mod_step(what)
                elif what[0] == CU:
                    u, h = UNIT_NO[what], what[1]
                    if h == 0:
                        own.done(v.memset(cu[:, :, 0:2], 0.0))
                    v.wait_ge(unit_done, u + 1)
                    wait_evacuated(v, (CC, 0))
                    wait_evacuated(v, (CC, 1))
                    v.tensor_tensor(cu[:, 2 * h:2 * h + 2, 2:2 + S], ps[:, u % 2, :].rearrange("p (b n) -> p b n", b=2),
                                    cT[:, 2 * h:2 * h + 2, :], ALU.mult).then_inc(bank_free[u % 2], 1)
                    if h == 1:
                        wait_evacuated(v, (CU, 0))
                        wait_evacuated(v, (CU, 1))
                        own.wait()
                        for j in range(3):
                            for k in range(KC):
                                w = vecT[:, V_CW + j * KC + k:V_CW + j * KC + k + 1]
                                tap = cu[:, k, j:j + S]
                                if j == 0:
                                    own.done(v.tensor_scalar(cT[:, k, :], tap, w, vecT[:, V_CB + k:V_CB + k + 1],
                                                             ALU.mult, ALU.add))
                                else:
                                    own.done(v.scalar_tensor_tensor(out=cT[:, k, :], in0=tap, scalar=w,
                                                                    in1=cT[:, k, :], op0=ALU.mult, op1=ALU.add))
                            own.wait()
                        v.tensor_tensor(bT, bT, cT, ALU.mult).then_inc(conv_ready, 1)
            v.wait_ge(modT_ready, 3)
            own.done(v.scalar_tensor_tensor(out=a2, in0=modT[:, M_SC2:M_SC2 + KD], scalar=1.0,
                                            in1=vecT[:, V_G2:V_G2 + KD], op0=ALU.add, op1=ALU.mult))
            own.wait()
            v.wait_ge(wr_landed, 32)
            own.done(v.tensor_scalar(wsh, wr[:, 0, :], modT[:, M_SH2:M_SH2 + 1], None, ALU.mult))
            for k in range(1, KD):
                own.wait()
                ins = own.done(v.scalar_tensor_tensor(out=wsh, in0=wr[:, k, :],
                                                      scalar=modT[:, M_SH2 + k:M_SH2 + k + 1], in1=wsh,
                                                      op0=ALU.mult, op1=ALU.add))
            own.wait()
            v.tensor_tensor(wra, wr, a2.unsqueeze(2).broadcast_to([P, KD, E]), ALU.mult).then_inc(wra_ready, 1)
            v.wait_ge(bias_r_done, 1)
            v.tensor_tensor(brb, brb, ps[:, 7, 0:E], ALU.add).then_inc(bias_r_ready, 1)
            for n in range(4):
                u = UNIT_NO[("conv", n)]
                v.wait_ge(unit_done, u + 1)
                if n == 0:
                    wait_evacuated(v, (GB1, 0))
                    wait_evacuated(v, (GB1, 1))
                v.tensor_tensor(mT[:, 2 * n:2 * n + 2, :], ps[:, u % 2, :].rearrange("p (b n) -> p b n", b=2),
                                ga[:, 2 * n:2 * n + 2, :], ALU.mult).then_inc(bank_free[u % 2], 1)
            for n in range(4):
                u = UNIT_NO[("o", n)]
                v.wait_ge(unit_done, u + 1)
                g = gb[:, 2 * n:2 * n + 2, :]
                own.done(v.tensor_tensor(g, ps[:, u % 2, :].rearrange("p (b n) -> p b n", b=2), g, ALU.mult))
                own.wait()
                v.tensor_tensor(mT[:, 2 * n:2 * n + 2, :], mT[:, 2 * n:2 * n + 2, :], g,
                                ALU.add).then_inc(bank_free[u % 2], 1)
            for n in range(4):
                u = UNIT_NO[("merge", n)]
                t, cols = n // 2, slice(512 * (n % 2), 512 * (n % 2) + 512)
                tmp = r_gate[:, 512 * n:512 * n + 512]
                v.wait_ge(unit_done, u + 1)
                v.tensor_tensor(tmp, ps[:, u % 2, :], g1b[:, cols], ALU.mult).then_inc(bank_free[u % 2], 1)
                wait_evacuated(v, ("merge", n))
                v.tensor_tensor(x_sb[:, t, cols], x_sb[:, t, cols], tmp, ALU.add).then_inc(x1_ready, 1)
                if n % 2 == 1:
                    v.wait_ge(r_x1_ready, t + 1)
                    normalise(xn[:, t, :], x_sb[:, t, :], stat[:, 2 + t:3 + t], D).then_inc(xn2_ready, 1)
            for t in range(T):
                v.wait_ge(x1_turned, t + 1)
                v.tensor_copy(hT[:, 0:4, t * P:t * P + P],
                              ps[:, 2 + 2 * t, :].rearrange("p (k n) -> p k n", k=4)).then_inc(x1T_ready, 1)
            for t in range(T):
                own.done(v.memset(lg[t][:, E:E + TOPK], TAKEN))
                own.done(v.memset(rep[:, t, TOPK:8], TAKEN))
            for t in range(T):
                v.wait_ge(logits_done, t + 1)
                own.done(v.tensor_tensor(lg[t][:, 0:E], ps[:, 6 + t, 0:E], brb, ALU.add))
                own.wait()
                own.done(v.max(top[:, t, :], lg[t][:, 0:E]))
                own.wait()
                v.tensor_scalar(ntop[:, t:t + 1], top[:, t, 0:1], -1.0, None, ALU.mult).then_inc(lg_ready, 1)
                own.done(v.tensor_copy(rep[:, t, 0:TOPK], top[:, t, 0:TOPK]))
                own.wait()
                own.done(v.match_replace(left[:, t, :], rep[:, t, :], lg[t], -TAKEN))
                own.wait()
                v.tensor_tensor(mask[:, t, :], left[:, t, 0:E], lg[t][:, 0:E], ALU.not_equal).then_inc(mask_ready, 1)
            for t in range(T):
                v.wait_ge(mask_ready, t + 1)
                v.wait_ge(ex_ready, t + 1)
                own.done(v.tensor_tensor(ex[:, t, :], ex[:, t, :], mask[:, t, :], ALU.mult))
                own.wait()
                own.done(v.tensor_reduce(wsum[:, t:t + 1], ex[:, t, :], AX, ALU.add))
                own.wait()
                own.done(v.reciprocal(wsum[:, t:t + 1], wsum[:, t:t + 1]))
                own.wait()
                v.tensor_scalar(comb[:, t, :], ex[:, t, :], wsum[:, t:t + 1], None, ALU.mult).then_inc(comb_ready, 1)
            v.wait_ge(pos_done, 1)
            own.done(v.scalar_tensor_tensor(out=posm, in0=ps[:, 2, 0:2 * E].rearrange("p (t n) -> p t n", t=T),
                                            scalar=1.0, in1=mask, op0=ALU.add, op1=ALU.mult))
            own.done(v.tensor_reduce(cntm, ps[:, 2, 2 * E:3 * E], AX, ALU.max))
            own.wait()
            own.done(v.tensor_scalar(posm, posm, -1.0, None, ALU.add))
            own.done(v.tensor_scalar(over[:, 0:ROUNDS - 1], thr, cntm, None, ALU.is_lt))
            own.wait()

            def gather_hot(e):
                for t in range(T):
                    ins = v.tensor_scalar(g_hot[:, t, :], iota, posm[:, t, bass.ds(e, 1)] if not isinstance(e, int)
                                          else posm[:, t, e:e + 1], None, ALU.is_equal)
                ins.then_inc(hot_ready, 1)

            def select(e):
                src = ident[:, bass.ds(e, 1)] if not isinstance(e, int) else ident[:, e:e + 1]
                v.tensor_copy(sel, src.broadcast_to([P, CAP])).then_inc(sel_ready, 1)

            def tokens_in():
                own.done(v.tensor_tensor(xg, ps[:, 2, :].rearrange("p (k n) -> p k n", k=KD),
                                         a2.unsqueeze(2).broadcast_to([P, KD, CAP]), ALU.mult))
                own.wait()
                v.tensor_tensor(xg, xg, modT[:, M_SH2:M_SH2 + KD].unsqueeze(2).broadcast_to([P, KD, CAP]),
                                ALU.add).then_inc(xg_ready, 1)

            gather_hot(0)
            own.done(v.tensor_reduce(pairs_f, over[:, 0:ROUNDS - 1], AX, ALU.add))
            own.wait()
            own.done(v.tensor_scalar(pairs_f, pairs_f, float(E // 2), float(E // 2), ALU.mult, ALU.add))
            own.wait()
            v.tensor_copy(npairs[:, :], pairs_f[0:1, :]).then_inc(routed, 1)
            v.wait_ge(late_landed, 32)
            v.wait_ge(x1_ready, 4)
            select(0)
            v.wait_ge(gather_done, 1)
            tokens_in()
            v.wait_ge(zeroed, 2)
            v.wait_ge(routed, 1)
            v.tensor_copy(scrap[:, 2:3], ones[:, 0:1]).then_inc(gu_free, 1)
            v.wait_ge(bdown_read, 2)
            v.tensor_copy(scrap[:, 3:4], ones[:, 0:1]).then_inc(st_ready, 1)
            v.tensor_copy(scrap[:, 4:5], ones[:, 0:1]).then_inc(acc_ready, 1)
            own.wait()

            def accumulate(m):
                for t in range(T):
                    v.wait_ge(scatter_done, 2 * m + t + 1)
                    ins = v.tensor_tensor(acc[:, t, :], acc[:, t, :],
                                          ps[:, 4 + 2 * t:6 + 2 * t, :].rearrange("p b n -> p (b n)"), ALU.add)
                ins.then_inc(acc_ready, 1)

            pairs = v.value_load(npairs[0:1, 0:1], min_val=E // 2, max_val=ROUNDS * E // 2)
            before, per_pair = own.n, 2 * 3
            with v.Fori(0, pairs) as m:
                own.n, own.base = before, per_pair * m
                for p in range(2):
                    i = 2 * m + p
                    e, e_next = (2 * m + p) % E, (2 * m + p + 1) % E
                    v.wait_ge(gather_done, i + 1)
                    gather_hot(e_next)
                    if p == 0:
                        v.wait_ge(st_ready, m + 1)
                    for t in range(T):
                        ins = v.tensor_scalar(wp[:, t, CAP * p:CAP * p + CAP], iota, posm[:, t, bass.ds(e, 1)],
                                              comb[:, t, bass.ds(e, 1)], ALU.is_equal, ALU.mult)
                    ins.then_inc(wp_ready, 1)
                    v.wait_ge(wp_ready, i + 1)
                    own.done(v.tensor_scalar(posm[:, :, bass.ds(e, 1)], posm[:, :, bass.ds(e, 1)], float(-CAP), None,
                                             ALU.add))
                    v.wait_ge(up_done, i + 1)
                    gu = ps[:, 0:2, :].rearrange("p b (n two) -> p b n two", two=2)
                    v.tensor_scalar(glu.rearrange("p (b n) -> p b n", b=2), gu[:, :, :, 0], LIMIT, None,
                                    ALU.min).then_inc(glu_ready, 1)
                    v.tensor_scalar(lin.rearrange("p (b n) -> p b n", b=2), gu[:, :, :, 1], LIMIT, -LIMIT,
                                    ALU.min, ALU.max).then_inc(gu_free, 1)
                    v.wait_ge(glu_ready, i + 1)
                    v.wait_ge(gu_free, i + 2)
                    own.done(v.scalar_tensor_tensor(out=lin, in0=lin, scalar=1.0, in1=glu, op0=ALU.add, op1=ALU.mult))
                    own.wait()
                    v.wait_ge(sig_ready, i + 1)
                    v.tensor_tensor(act_sb, lin, sig, ALU.mult).then_inc(act_ready, 1)
                    select(e_next)
                    if p == 0:
                        accumulate(m)
                    else:
                        v.wait_ge(wp_turned, m + 1)
                        v.tensor_copy(st, ps[:, 7, 0:S]).then_inc(st_ready, 1)
                    v.wait_ge(gather_done, i + 2)
                    tokens_in()
                assert own.n == before + per_pair, own.n - before
            own.base, own.n = per_pair * (pairs - 1), before + per_pair
            for t in range(T):
                v.wait_ge(scatter_done, 2 * pairs + t + 1)
                own.done(v.tensor_tensor(acc[:, t, :], acc[:, t, :],
                                         ps[:, 4 + 2 * t:6 + 2 * t, :].rearrange("p b n -> p (b n)"), ALU.add))
                own.wait()
                own.done(v.tensor_tensor(acc[:, t, :], acc[:, t, :], g2b, ALU.mult))
                own.wait()
                v.tensor_tensor(x_sb[:, t, :], x_sb[:, t, :], acc[:, t, :], ALU.add).then_inc(fin_ready, 1)
            v.wait_ge(nf_scaled, 1)
            for t in range(T):
                v.wait_ge(r_fin_ready, t + 1)
                v.scalar_tensor_tensor(out=x_sb[:, t, :], in0=x_sb[:, t, :], scalar=stat[:, 2 + t:3 + t], in1=nfb,
                                       op0=ALU.mult, op1=ALU.mult).then_inc(y_out, 1)


def distance_bucket(dist):
    exact = NB // 2
    d = np.maximum(dist, 1).astype(np.float32)
    large = exact + (np.log(d / np.float32(exact)) / np.float32(math.log(MAX_DISTANCE / exact))
                     * np.float32(NB - exact)).astype(np.int32)
    return np.where(dist < exact, dist, np.minimum(large, NB - 1))


def constants():
    cst = np.zeros((P, NCONST), np.float32)
    cst[:, C_ID:C_ID + P] = np.eye(P)
    cst[:, C_TRI:C_TRI + P] = np.triu(np.ones((P, P)), 1)
    cst[:, C_ONE:C_ONE + P] = 1.0
    cst[:, C_IOTA:C_IOTA + CAP] = np.arange(CAP)
    cst[:, C_THR:C_THR + ROUNDS - 1] = CAP * np.arange(1, ROUNDS)
    cst[:, C_FLIP:C_FLIP + P] = np.eye(P)[::-1]
    dist = np.maximum(S - 1 - np.arange(384), 0)
    hot = (distance_bucket(dist)[None, :] == np.arange(NB)[:, None]).astype(np.float32)
    return cst, hot


_INS = ["x", "c", "w_ada", "b_ada", "norm1_g", "norm2_g", "w_in", "conv_w", "conv_b", "w_out_conv",
        "lambda_q1", "lambda_k1", "lambda_q2", "lambda_k2", "subln_g", "w_o_attn", "w_merge",
        "w_router", "b_router", "w_gate_up", "b_gate_up", "w_down", "b_down", "rel_bias_table", "normf_g"]


def kernel(**inputs):
    import concourse.bacc as _bacc
    from concourse.bass_utils import run_bass_kernel_spmd as _run

    nc = _bacc.Bacc("TRN2", target_bir_lowering=False, num_devices=1)
    cst, hot = constants()
    given = {n: np.ascontiguousarray(inputs[n]) for n in _INS} | {"consts": cst, "buckets": hot}
    arrays, args = {}, []
    for name, a in given.items():
        arrays[f"in_{name}"] = a
        args.append(nc.dram_tensor(f"in_{name}", a.shape, mybir.dt.from_np(a.dtype), kind="ExternalInput").ap())
    args.append(nc.dram_tensor("out_0", (1, S, D), F32, kind="ExternalOutput").ap())
    block_kernel(nc, *args)
    r = _run(nc, [arrays], core_ids=[0])
    return r.results[0]["out_0"]
```

```python
import math
from contextlib import ExitStack

import numpy as np
import concourse.bass as bass
from concourse import mybir

F32 = mybir.dt.float32
F32R = mybir.dt.float32r
I32 = mybir.dt.int32
ALU = mybir.AluOpType
ACT = mybir.ActivationFunctionType
AX = mybir.AxisListType.X

P = 128
D = 1024
S = 256
KD = D // P
T = S // P
CONV = 512
KC = CONV // P
H = 8
HD = 64
VD = 2 * HD
NB = 32
MAX_DISTANCE = 128
E = 32
TOPK = 4
F = 1024
CAP = 64
LIMIT = 7.0
ALPHA = 1.702
EPS = 1e-6
LAM_INIT = 0.8 - 0.6 * math.exp(-0.3 * 0)
MASKED = -3.0e38
TAKEN = 3.0e38
SLOT = 2048
CATCH_UP = 8
NSLOT = 12
UP_SLOTS = 8
TWICE = 6
ROUNDS = -(-S // CAP)

V_G1, V_G2, V_CB, V_CW, V_SUB, V_C = 0, 8, 16, 20, 32, 33
NVEC = 41
M_SH1, M_SC1, M_SH2, M_SC2 = 0, 8, 24, 32
C_ID, C_TRI, C_ONE, C_IOTA, C_THR, C_FLIP = 0, 128, 256, 384, 448, 452
NCONST = 452 + 128
NSMALL = 1300

Q0, K0, V0, Q1, K1, V1, CB, CC, CU, GA0, GA1, GB0, GB1, OC0, OC1, WO0, WO1, MG0, MG1 = range(19)
PANEL_COL = {CB: 0, CC: 512, CU: 1024, Q0: 1536, Q1: 2048, K0: 2560, K1: 3072, V0: 3584, V1: 4096,
             GA0: 4608, GA1: 5120, GB0: 5632, GB1: 6144}
CHUNKS = [(p, j) for p in range(19) for j in range(1 if p in (OC0, OC1) else 2)]
CHUNK_NO = {pj: n for n, pj in enumerate(CHUNKS)}
LAST_CHUNK = {p: CHUNK_NO[(p, 0 if p in (OC0, OC1) else 1)] for p in range(19)}
ADA_FROM = 3
STREAM = [("ada", 0, k) for k in range(KD)] + [("w", n) for n in range(ADA_FROM)]
_ada = [("ada", b, k) for b in (1, 2) for k in range(KD)]
for _n in range(ADA_FROM, len(CHUNKS)):
    STREAM.append(("w", _n))
    if _ada:
        STREAM.append(_ada.pop(0))
FIRST, STAGE, WIDE, WIDE_UNTIL = KD, 3, 5, 16
BUFFER, BEFORE, USES = {}, {}, {}
_last = {b: b for b in range(STAGE)}
_uses = {b: 0 for b in range(WIDE)}
_wide = True
for _n in range(FIRST, len(STREAM)):
    _wide = _wide and STREAM[_n][:2] <= ("w", WIDE_UNTIL)
    _b = min(range(WIDE if _wide else STAGE), key=lambda b: _last.get(b, -1))
    BEFORE[_n] = _last.get(_b)
    _last[_b] = _n
    _uses[_b] += 1
    BUFFER[_n], USES[_n] = _b, _uses[_b]
FLIP_AFTER = 1
AFTER = {5: [("att", 0)], 6: [("att", 1)], 7: [("att", 2)], 8: [("att", 3)], 10: [("att", 4)], 11: [("att", 5)],
         12: [("att", 6)], 13: [("att", 7)], 14: [("att", 8)], 15: [("att", 9)], 16: [("att", 10)],
         19: [("modt", 0)], 20: [("modt", 1)], 21: [("modt", 2)], 22: [("modt", 3)]}
CONV_HI, CONV_LO, ROUTER_WEIGHTS, ROUTER_BIAS = 20, 21, 22, 23
EARLY = {18: 0, 25: 1, 26: 2, 31: 3}


class Steps:

    def __init__(self, eng, sem):
        self.eng, self.sem, self.n, self.base = eng, sem, 0, None

    def value(self):
        return self.n if self.base is None else self.base + self.n

    def done(self, ins):
        self.n += 1
        return ins.then_inc(self.sem, 1)

    def wait(self):
        self.eng.wait_ge(self.sem, self.value())


def dap(ap, offset, dims):
    return bass.AP(tensor=ap.tensor, offset=ap.offset + offset, ap=dims)


def block_kernel(nc, x, c, w_ada, b_ada, norm1_g, norm2_g, w_in, conv_w, conv_b, w_out_conv,
                 lambda_q1, lambda_k1, lambda_q2, lambda_k2, subln_g, w_o_attn, w_merge,
                 w_router, b_router, w_gate_up, b_gate_up, w_down, b_down, rel_bias_table, normf_g,
                 consts, buckets, out):
    with ExitStack() as ctx:
        base = [(nc.sbuf_base + 31) // 32 * 32]

        def region(cols):
            cols = -(-cols // 8) * 8
            base[0] += 4 * cols
            return base[0] - 4 * cols

        def at(name, offset, cols, dt=F32):
            return nc.alloc_sbuf_tensor_at(name, [P, cols], dt, offset=offset)

        def sb(name, cols):
            return at(name, region(cols), cols)

        def sem(name):
            return ctx.enter_context(nc.semaphore(name))

        x_sb = sb("x_sb", T * D)[:, :].rearrange("p (t n) -> p t n", t=T)
        o_xn = region(2048)
        r_xn = at("r_xn", o_xn, 2048)
        o_ht = region(2048)
        r_ht = at("r_ht", o_ht, 2048)
        r_q = sb("r_q", 2048)
        r_k = sb("r_k", 2048)
        r_v = sb("r_v", 2048)
        o_bias = region(2048)
        r_bias = at("r_bias", o_bias, 2048)
        r_gb = sb("r_gb", 2048)
        r_work = sb("r_work", 2756)
        r_cu = sb("r_cu", 1544)
        cst = sb("cst", NCONST - 128)
        small = sb("small", NSMALL)
        o_gate, o_oh, o_ol, o_conv, o_bp = region(4096), region(2048), region(2048), region(2048), region(2048)
        o_stage = [region(SLOT) for _ in range(STAGE)]
        o_w = [region(SLOT) for _ in range(4)]
        o_hh, o_hl = region(2048), region(2048)
        assert base[0] <= nc.sbuf_usable_end
        r_gate = at("r_gate", o_gate, 4096)
        r_conv = at("r_conv", o_conv, 2048)
        stage = [at(f"stage{n}", o, SLOT) for n, o in enumerate([*o_stage, o_gate, o_gate + 8192])]
        w_hi = [at(f"w_hi{n}", o_w[2 * n], SLOT, F32R)[:, :].rearrange("p (k n) -> p k n", k=4) for n in range(2)]
        w_lo = [at(f"w_lo{n}", o_w[2 * n + 1], SLOT, F32R)[:, :].rearrange("p (k n) -> p k n", k=4) for n in range(2)]
        x_hi = at("x_hi", o_hh, 2048, F32R)[:, :].rearrange("p (k n) -> p k n", k=KD)
        x_lo = at("x_lo", o_hl, 2048, F32R)[:, :].rearrange("p (k n) -> p k n", k=KD)
        o_hi = at("o_hi", o_oh, 2048, F32R)[:, :].rearrange("p (k n) -> p k n", k=KD)
        o_lo = at("o_lo", o_ol, 2048, F32R)[:, :].rearrange("p (k n) -> p k n", k=KD)
        b_parts = at("b_parts", o_bp, 2048, F32R)
        b_hi = b_parts[:, 0:1024].rearrange("p (k n) -> p k n", k=KC)
        b_lo = b_parts[:, 1024:2048].rearrange("p (k n) -> p k n", k=KC)
        r_bada = at("r_bada", o_bp, 1536)
        ada_first = [at(f"ada_first{n}", o, SLOT)
                     for n, o in enumerate([*o_stage, *o_w, o_oh])]
        order = [o_bias, o_conv, o_xn, o_bp, o_oh, o_ol, o_gate, o_gate + 8192, *o_stage, *o_w, o_hh, o_hl, o_ht]
        expert = [at(f"expert{n}", o, SLOT) for n, o in enumerate(order)]

        xn = r_xn[:, :].rearrange("p (t n) -> p t n", t=T)
        hT = r_ht[:, :].rearrange("p (k n) -> p k n", k=KD)
        qT = r_q[:, :].rearrange("p (k n) -> p k n", k=H)
        mT = r_q[:, :].rearrange("p (k n) -> p k n", k=KD)
        h_sb = r_q[:, :].rearrange("p (k n) -> p k n", k=KD)
        acc = r_q[:, :].rearrange("p (t n) -> p t n", t=T)
        kT = r_k[:, :].rearrange("p (k n) -> p k n", k=H)
        bgu = r_k[:, :]
        v_sb = r_v[:, :].rearrange("p (t n) -> p t n", t=T)
        hankel = r_v[:, :].rearrange("p (h n) -> p h n", h=H)
        glu, lin, sig, act_sb = (r_v[:, 512 * n:512 * n + 512] for n in range(4))
        bias_t = r_bias[:, :].rearrange("p (h n) -> p h n", h=H)
        ga = r_gate[:, 0:2048].rearrange("p (k n) -> p k n", k=KD)
        gb = r_gate[:, 2048:4096].rearrange("p (k n) -> p k n", k=KD)
        mod = r_xn[:, 0:1536].rearrange("p (b n) -> p b n", b=3)
        bada = r_bada[:, :].rearrange("p (b n) -> p b n", b=3)
        bT = r_conv[:, 0:1024].rearrange("p (k n) -> p k n", k=KC)
        cT = r_conv[:, 1024:2048].rearrange("p (k n) -> p k n", k=KC)
        cu = r_cu[:, 0:1032].rearrange("p (k n) -> p k n", k=KC)
        flip = r_conv[:, 0:128]
        hot = r_conv[0:NB, 128:512]
        g_sb = r_conv[0:H, 512:896]
        rows = r_conv[0:NVEC, 896:1024]
        cs32 = r_cu[:, 1288:1544].rearrange("p (k n) -> p k n", k=KD)
        lam_rows = r_conv[0:1, 1280:1536].rearrange("p (a n) -> p a n", a=4)
        table = r_conv[0:NB, 1536:1544]
        lam_s = r_conv[0:1, 1544:1552]
        csig = r_conv[:, 1552:1560]
        nfb = r_gb[:, 0:D]
        g1b, g2b = r_gb[:, 0:D], r_gb[:, D:2 * D]
        logit = r_work[:, 0:768].rearrange("p (m n) -> p m n", m=2)
        attn = r_work[:, 768:1152]
        pT = r_work[:, 1152:1536]
        o_n = r_work[:, 1536:1792].rearrange("p (t n) -> p t n", t=T)
        junk = r_work[:, 1792:2048]
        xg = r_work[:, 0:512].rearrange("p (k n) -> p k n", k=KD)
        y2 = r_work[:, 512:1536]
        st = r_work[:, 1536:1792]
        wp = r_work[:, 1792:2048].rearrange("p (t n) -> p t n", t=T)
        g_hot = r_work[:, 2048:2176].rearrange("p (t n) -> p t n", t=T)
        sel = r_work[:, 2176:2240]
        aT = r_work[:, 2240:2752].rearrange("p (c n) -> p c n", c=4)
        ident = cst[:, C_ID:C_ID + 128]
        tri = cst[:, C_TRI:C_TRI + 128]
        ones = cst[:, C_ONE:C_ONE + 128]
        iota = cst[:, C_IOTA:C_IOTA + CAP]
        thr = cst[:, C_THR:C_THR + ROUNDS - 1]

        used_small = [0]

        def piece(n):
            used_small[0] += n
            assert used_small[0] <= NSMALL
            return small[:, used_small[0] - n:used_small[0]]

        vecT = piece(NVEC)
        modT = piece(48)
        a1 = piece(KD)
        a2 = piece(KD)
        wr = piece(KD * E).rearrange("p (k n) -> p k n", k=KD)
        wra = piece(KD * E).rearrange("p (k n) -> p k n", k=KD)
        wsh = piece(E)
        brb = piece(E)
        stat = piece(8)
        padded, minus_half = piece(2), piece(2)
        neg_max = piece(4)
        sums = piece(4)
        inv = piece(4)
        nlam = piece(1)
        sub = piece(1)
        oss = piece(2)
        ors = piece(2)
        lg = [piece(E + TOPK) for _ in range(T)]
        top = piece(8 * T).rearrange("p (t n) -> p t n", t=T)
        rep = piece(8 * T).rearrange("p (t n) -> p t n", t=T)
        left = piece((E + TOPK) * T).rearrange("p (t n) -> p t n", t=T)
        mask = piece(E * T).rearrange("p (t n) -> p t n", t=T)
        ex = piece(E * T).rearrange("p (t n) -> p t n", t=T)
        comb = piece(E * T).rearrange("p (t n) -> p t n", t=T)
        posm = piece(E * T).rearrange("p (t n) -> p t n", t=T)
        ntop = piece(T)
        wsum = piece(T)
        cntm = piece(1)
        over = piece(4)
        last_f = piece(1)
        scrap = piece(5)
        junk2 = r_cu[:, 0:512]
        last_pair = at("last_pair", region(8), 1, I32)
        ps = ctx.enter_context(nc.psum_tensor("ps", [P, 8, 512], F32))

        scratch = nc.dram_tensor("bias_rows", (H, 384), F32, kind="Internal").ap()

        first_landed = [sem(f"first{n}_landed") for n in range(FIRST)]
        stage_landed = [sem(f"stage{n}_landed") for n in range(WIDE)]
        slot_landed = [sem(f"slot{n}_landed") for n in range(NSLOT + TWICE)]
        ada_used, up_used, down_used = sem("ada_used"), sem("up_used"), sem("down_used")
        x_landed, rows_landed, ada_b_landed = sem("x_landed"), sem("rows_landed"), sem("ada_b_landed")
        bias_in, bias_out, bias_back = sem("bias_in"), sem("bias_out"), sem("bias_back")
        wr_landed, late_landed, nf_landed = sem("wr_landed"), sem("late_landed"), sem("nf_landed")
        vec_turned, vec_ready = sem("vec_turned"), sem("vec_ready")
        c_ready, lam_prod, lam_exp, lam_ready, lam_out = (sem("c_ready"), sem("lam_prod"), sem("lam_exp"),
                                                          sem("lam_ready"), sem("lam_out"))
        csig_ready = sem("csig_ready")
        g_made, g_ready, flip_done, flip_read, bias_whole = (sem("g_made"), sem("g_ready"), sem("flip_done"),
                                                             sem("flip_read"), sem("bias_whole"))
        sumsq, xn_ready, x_turned = sem("sumsq"), sem("xn_ready"), sem("x_turned")
        xT_act, xT_dve = sem("xT_act"), sem("xT_dve")
        mod_ready, mod_turned, modT_ready = sem("mod_ready"), sem("mod_turned"), sem("modT_ready")
        gate_rows, gates_ready, a1_ready = sem("gate_rows"), sem("gates_ready"), sem("a1_ready")
        half_done, hi_ready, lo_ready = sem("half_done"), sem("hi_ready"), sem("lo_ready")
        h_hi_ready, h_lo_ready, conv_hi, conv_lo = sem("h_hi_ready"), sem("h_lo_ready"), sem("conv_hi"), sem("conv_lo")
        oT_hi, m_ready, m_hi, m_lo = sem("oT_hi"), sem("m_ready"), sem("m_hi"), sem("m_lo")
        bank_free = [sem("bank0_free"), sem("bank1_free")]
        scores_done, scores_read, exp_done, attn_ready = (sem("scores_done"), sem("scores_read"),
                                                          sem("exp_done"), sem("attn_ready"))
        attn_turned, pT_ready, pv_done, osq_done, o_ready, o_turned, oT_ready = (
            sem("attn_turned"), sem("pT_ready"), sem("pv_done"), sem("osq_done"), sem("o_ready"),
            sem("o_turned"), sem("oT_ready"))
        conv_ready, x1_ready, x1_sumsq = sem("conv_ready"), sem("x1_ready"), sem("x1_sumsq")
        x1_turned, x1T_ready, bias_r_done, bias_r_ready, wra_ready = (
            sem("x1_turned"), sem("x1T_ready"), sem("bias_r_done"), sem("bias_r_ready"),
            sem("wra_ready"))
        logits_done, lg_ready, ex_ready, mask_ready, pos_done, comb_ready, routed = (
            sem("logits_done"), sem("lg_ready"), sem("ex_ready"), sem("mask_ready"), sem("pos_done"),
            sem("comb_ready"), sem("routed"))
        comb_turned, acc_started, last_scatter = sem("comb_turned"), sem("acc_started"), sem("last_scatter")
        zeroed, kv_dead = sem("zeroed"), sem("kv_dead")
        hot_ready, sel_ready, gather_done, xg_ready = (sem("hot_ready"), sem("sel_ready"), sem("gather_done"),
                                                       sem("xg_ready"))
        gu_free, glu_ready, sig_ready, act_ready = (sem("gu_free"), sem("glu_ready"),
                                                             sem("sig_ready"), sem("act_ready"))
        act_turned, aT_ready, y_ready = sem("act_turned"), sem("aT_ready"), sem("y_ready")
        wp_ready, wp_turned, st_ready, scatter_done, acc_ready = (sem("wp_ready"), sem("wp_turned"),
                                                                  sem("st_ready"), sem("scatter_done"),
                                                                  sem("acc_ready"))
        fin_ready, fin_sumsq, y_out, stored = sem("fin_ready"), sem("fin_sumsq"), sem("y_out"), sem("stored")
        r_x_ready, r_o_ready, r_x1_ready, r_fin_ready = (
            sem("r_x_ready"), sem("r_o_ready"), sem("r_x1_ready"), sem("r_fin_ready"))
        dve_step, act_step, pool_step = sem("dve_step"), sem("act_step"), sem("pool_step")

        def slot(j, parity):
            return NSLOT + j if j < TWICE and parity else j

        def wait_slot(eng, j, m, parity):
            eng.wait_ge(slot_landed[slot(j, parity)], 16 * m + 16 if j < TWICE else 16 * (2 * m + parity) + 16)

        def front_chunk(n):
            if n < FIRST:
                return ada_first[n], first_landed[n], 16
            return stage[BUFFER[n]], stage_landed[BUFFER[n]], 16 * USES[n]

        def wait_chunk(eng, what):
            _, landed, value = front_chunk(STREAM.index(what))
            eng.wait_ge(landed, value)

        def wait_front_used(eng, what):
            if what[0] == "ada":
                eng.wait_ge(ada_used, KD * what[1] + what[2] + 1)
            else:
                eng.wait_ge(lo_ready, what[1] + 1)

        def wait_product(eng, p, h):
            eng.wait_ge(half_done, 2 * LAST_CHUNK[p] + h + 1)

        def wait_evacuated(eng, p, h):
            eng.wait_ge(bank_free[h], p + 1)

        win = w_in[0].rearrange("(k p) n -> p k n", p=P)
        x_dram = x[0].rearrange("(t p) n -> t p n", p=P)
        out_dram = out[0].rearrange("(t p) n -> t p n", p=P)

        def front_source(what):
            if what[0] == "ada":
                _, b, k = what
                return w_ada[0, P * k:P * k + P, SLOT * b:SLOT * b + SLOT]
            p, j = CHUNKS[what[1]]
            if p in PANEL_COL:
                w, col = win, PANEL_COL[p]
            else:
                w = {OC0: w_out_conv, OC1: w_out_conv, WO0: w_o_attn, WO1: w_o_attn, MG0: w_merge, MG1: w_merge}[p]
                w, col = w[0].rearrange("(k p) n -> p k n", p=P), 512 * (p in (OC1, WO1, MG1))
            return w[:, 4 * j:4 * j + 4, col:col + 512]

        block = ctx.enter_context(nc.Block())

        @block.sync
        def _(sp):
            def load_slot(j, e, parity):
                n = slot(j, parity)
                if j < UP_SLOTS:
                    sp.dma_start(expert[n][:, :], w_gate_up[0, e, P * j:P * j + P, :]).then_inc(slot_landed[n], 16)
                else:
                    d = (j - UP_SLOTS) * 2 * P
                    src = w_down[0, e, d:d + 2 * P, :].rearrange("(k p) n -> p k n", p=P)
                    sp.dma_start(expert[n][:, :].rearrange("p (k n) -> p k n", k=2), src).then_inc(slot_landed[n], 16)

            for t in range(T):
                sp.dma_start(x_sb[:, t, :], x_dram[t]).then_inc(x_landed, 16)
            sp.dma_start(cst[:, :], consts[:, 0:C_FLIP]).then_inc(rows_landed, 16)
            for n, what in enumerate(STREAM):
                if n == 1:
                    sp.dma_start(table, rel_bias_table).then_inc(bias_in, 16)
                    sp.dma_start(hot, buckets).then_inc(bias_in, 16)
                    sp.dma_start(flip, consts[:, C_FLIP:C_FLIP + 128]).then_inc(bias_in, 16)
                buf, landed, _ = front_chunk(n)
                if n >= FIRST and BEFORE[n] is not None:
                    wait_front_used(sp, STREAM[BEFORE[n]])
                dst = buf[:, :] if what[0] == "ada" else buf[:, :].rearrange("p (k n) -> p k n", k=4)
                sp.dma_start(dst, front_source(what)).then_inc(landed, 16)
                early = EARLY.get(what[1]) if what[0] == "w" else None
                if early == 0:
                    sp.wait_ge(scores_read, H)
                elif early == 1:
                    sp.wait_ge(conv_lo, 1)
                elif early == 2:
                    sp.wait_ge(gates_ready, 2)
                elif early == 3:
                    wait_product(sp, OC1, 1)
                if early is not None:
                    load_slot(early, 0, 0)

            for j in range(len(EARLY), NSLOT + TWICE):
                if j < 6:
                    wait_product(sp, WO1, 1)
                elif j < 8:
                    sp.wait_ge(m_ready, 4)
                elif j < 8 + STAGE:
                    sp.wait_ge(lo_ready, len(CHUNKS))
                elif j < NSLOT + TWICE - 1:
                    wait_product(sp, MG1, 1)
                else:
                    sp.wait_ge(logits_done, T)
                load_slot(j % NSLOT, j // NSLOT, j // NSLOT)
            sp.wait_ge(routed, 1)
            final = sp.value_load(last_pair[0:1, 0:1], min_val=E // 2 - 1, max_val=ROUNDS * E // 2 - 1)

            def rest_of_next(i, parity):
                for j in range(TWICE, NSLOT):
                    if j < UP_SLOTS:
                        sp.wait_ge(up_used, UP_SLOTS * i + (j + 1))
                    else:
                        sp.wait_ge(down_used, 4 * i + (j - UP_SLOTS + 1))
                    load_slot(j, (i + 1) % E, 1 - parity)

            def first_of_second(i, parity):
                for j in range(TWICE):
                    sp.wait_ge(up_used, UP_SLOTS * i + (j + 1))
                    load_slot(j, (i + 2) % E, parity)

            with sp.Fori(0, CATCH_UP) as m:
                for p in range(2):
                    first_of_second(2 * m + p, p)
                    rest_of_next(2 * m + p, p)
            with sp.Fori(CATCH_UP, final) as m:
                for p in range(2):
                    rest_of_next(2 * m + p, p)
                    first_of_second(2 * m + p, p)
            rest_of_next(2 * final, 0)
            for n in range(2 * T):
                t, cols = n // 2, slice(512 * (n % 2), 512 * (n % 2) + 512)
                sp.wait_ge(y_out, n + 1)
                sp.dma_start(out_dram[t, :, cols], acc[:, t, cols]).then_inc(stored, 16)
            sp.wait_ge(stored, 16 * 2 * T)

        @block.gpsimd
        def _(pool):
            own = Steps(pool, pool_step)

            def root(dst, src, n, t=0):
                w = slice(t, t + src.shape[1])
                own.done(nc.gpsimd.tensor_scalar(padded[:, w], src, 1.0 / n, EPS, ALU.mult, ALU.add))
                own.wait()
                return nc.gpsimd.tensor_tensor(dst, padded[:, w], minus_half[:, w], ALU.pow)

            def root_of_halves(t):
                own.done(nc.gpsimd.tensor_tensor(stat[:, 4 + t:5 + t], stat[:, 4 + t:5 + t], stat[:, 6 + t:7 + t],
                                                 ALU.add))
                own.wait()
                return root(stat[:, 2 + t:3 + t], stat[:, 4 + t:5 + t], D, t)

            own.done(nc.gpsimd.memset(minus_half, -0.5))

            pool.wait_ge(sumsq, 2)
            root(stat[:, 2:4], stat[:, 0:2], D).then_inc(r_x_ready, 1)
            pool.wait_ge(flip_read, 4)
            nc.gpsimd.affine_select(out=bias_t, in_=bias_t, compare_op=ALU.is_ge, fill=MASKED, base=P,
                                    pattern=[[0, H], [-1, S]], channel_multiplier=1).then_inc(bias_whole, 1)
            for h in range(H):
                pool.wait_ge(osq_done, h + 1)
                if h >= 1:
                    pool.wait_ge(o_ready, h)
                root(ors, oss, VD).then_inc(r_o_ready, 1)
            pool.wait_ge(scores_done, H)
            pool.wait_ge(o_turned, H)
            nc.gpsimd.memset(bgu, 0.0).then_inc(kv_dead, 1)
            pool.wait_ge(pT_ready, H)
            pool.wait_ge(o_ready, H)
            nc.gpsimd.memset(y2, 0.0).then_inc(zeroed, 1)
            nc.gpsimd.memset(st, 0.0).then_inc(zeroed, 1)
            for t in range(T):
                pool.wait_ge(x1_sumsq, T + t + 1)
                root_of_halves(t).then_inc(r_x1_ready, 1)
            pool.wait_ge(m_lo, 4)
            for t in range(T):
                nc.gpsimd.tensor_copy(acc[:, t, :], x_sb[:, t, :]).then_inc(acc_started, 1)
            for t in range(T):
                pool.wait_ge(fin_sumsq, 2 * t + 2)
                root_of_halves(t).then_inc(r_fin_ready, 1)

        @block.tensor
        def _(pe):
            pe.wait_ge(rows_landed, 16 * 9)
            pe.transpose(ps[:, 7, 0:NVEC], rows, ident[0:NVEC, 0:NVEC]).then_inc(vec_turned, 1)
            pe.wait_ge(bias_in, 48)
            pe.matmul(ps[0:H, 6, 0:384], table, hot, start=True, stop=True).then_inc(g_made, 1)
            for t in range(T):
                pe.wait_ge(xn_ready, t + 1)
                for k in range(KD):
                    m = pe.transpose(ps[:, 2 + k // 2, (k % 2) * S + t * P:(k % 2) * S + t * P + P],
                                     xn[:, t, k * P:k * P + P], ident)
            m.then_inc(x_turned, 1)
            pe.wait_ge(lam_out, 1)
            pe.wait_ge(vec_ready, 1)
            pe.matmul(ps[:, 7, 0:1], ones[0:1, :], lam_s[:, 4:5], start=True, stop=True).then_inc(lam_ready, 1)

            def ada_chunk(b, k):
                if k == 0:
                    pe.wait_ge(c_ready, 1)
                    if b == 0:
                        pe.wait_ge(g_ready, 1)
                    else:
                        pe.wait_ge(mod_ready, b)
                wait_chunk(pe, ("ada", b, k))
                buf = front_chunk(STREAM.index(("ada", b, k)))[0]
                for g in range(4):
                    m = pe.matmul(ps[32 * g:32 * g + 32, 6, :], cs32[:, k, :], buf[:, 512 * g:512 * g + 512],
                                  start=(k == 0), stop=(k == KD - 1))
                m.then_inc(ada_used, 1)

            def mod_turn(b):
                for j in range(4):
                    m = pe.transpose(ps[:, 7, j * P:j * P + P], mod[:, b, j * P:j * P + P], ident)
                m.then_inc(mod_turned, 1)

            for k in range(KD):
                ada_chunk(0, k)
            pe.wait_ge(mod_ready, 1)
            pe.wait_ge(lam_ready, 2)
            mod_turn(0)
            def product(n):
                p, j = CHUNKS[n]
                if p in PANEL_COL:
                    hi, lo = x_hi, x_lo
                    pe.wait_ge(h_lo_ready, j + 1 if p == Q0 else 2)
                elif p in (OC0, OC1):
                    hi, lo = b_hi, b_lo
                    pe.wait_ge(conv_lo, 1)
                elif p in (WO0, WO1):
                    hi, lo = o_hi, o_lo
                    pe.wait_ge(oT_ready, H)
                else:
                    hi, lo = x_hi, x_lo
                    pe.wait_ge(m_lo, 2 * j + 2)
                pe.wait_ge(lo_ready, n + 1)
                wh, wl = w_hi[n % 2], w_lo[n % 2]
                ends = n == LAST_CHUNK[p]
                for h in range(2):
                    if j == 0 and p > Q0:
                        wait_evacuated(pe, p - 1, h)
                    if p in (V0, V1, MG0, MG1):
                        toks = slice(h * P, h * P + P)
                        parts = [(ps[:, h, :], x_part[:, 4 * j + k, toks], w_part[:, k, :])
                                 for k in range(4) for x_part, w_part in ((hi, wh), (hi, wl), (lo, wh))]
                        groups = [parts]
                    else:
                        groups = []
                        for blk in range(2):
                            col = (2 * h + blk) * P
                            groups.append([(ps[:, h, blk * S:blk * S + S], w_part[:, k, col:col + P],
                                            x_part[:, 4 * j + k, :])
                                           for k in range(4) for w_part, x_part in ((wh, hi), (wh, lo), (wl, hi))])
                    for group in groups:
                        for i, (out_ap, lhs, rhs) in enumerate(group):
                            first = group is groups[0] and j == 0 and i == 0
                            last = group is groups[-1] and ends and i == len(group) - 1
                            m = pe.matmul(out_ap, lhs, rhs, start=first, stop=last, skip_group_check=True)
                    m.then_inc(half_done, 1)

            def attention(n):
                if n < H:
                    half = n // 4
                    for p in (Q0, K0) if half == 0 else (Q1, K1):
                        for h in range(2):
                            wait_evacuated(pe, p, h)
                    if n > 0:
                        pe.wait_ge(scores_read, n)
                    else:
                        pe.wait_ge(flip_read, 4)
                    for m in range(2):
                        q, k = qT[HD * m:HD * m + HD, n, :], kT[HD * m:HD * m + HD, n, :]
                        pe.matmul(ps[:, 2 + m, 0:P], q[:, 0:P], k[:, 0:P], start=True, stop=True)
                        mm = pe.matmul(ps[:, 2 + m, P:P + S], q[:, P:S], k, start=True, stop=True)
                    mm.then_inc(scores_done, 1)
                if 1 <= n <= H:
                    pe.wait_ge(attn_ready, n)
                    if n >= 2:
                        pe.wait_ge(pT_ready, n - 1)
                    for j in range(3):
                        mm = pe.transpose(ps[:, 4, j * P:j * P + P], attn[:, j * P:j * P + P], ident)
                    mm.then_inc(attn_turned, 1)
                if 2 <= n <= H + 1:
                    h = n - 2
                    pe.wait_ge(pT_ready, h + 1)
                    if h >= 1:
                        pe.wait_ge(o_ready, h)
                    for hh in range(2):
                        wait_evacuated(pe, V0 if h < 4 else V1, hh)
                    cols = slice(h * VD, h * VD + VD)
                    pe.matmul(ps[:, 5, 0:P], pT[:, 0:P], v_sb[:, 0, cols], start=True, stop=True)
                    pe.matmul(ps[:, 5, P:S], pT[:, P:S], v_sb[:, 0, cols], start=True, stop=False)
                    pe.matmul(ps[:, 5, P:S], pT[:, S:S + P], v_sb[:, 1, cols], start=False,
                              stop=True).then_inc(pv_done, 1)
                if 3 <= n <= H + 2:
                    h = n - 3
                    pe.wait_ge(o_ready, h + 1)
                    if h >= 1:
                        pe.wait_ge(oT_ready, h)
                    for t in range(T):
                        mm = pe.transpose(ps[:, 7, t * P:t * P + P], o_n[:, t, :], ident)
                    mm.then_inc(o_turned, 1)

            def mod_step(n):
                if n < 2:
                    pe.wait_ge(mod_ready, n + 2)
                    pe.wait_ge(oT_ready, H)
                    pe.wait_ge(modT_ready, n + 1)
                    mod_turn(n + 1)
                    return
                b, g = (1, 0) if n == 2 else (2, 2)
                pe.wait_ge(mod_ready, 3)
                if n == 2:
                    pe.wait_ge(modT_ready, 3)
                else:
                    pe.wait_ge(gates_ready, 1)
                for half in range(2):
                    r = 32 * (g + half)
                    mm = pe.matmul(ps[:, 6 + half, :], ones[r:r + 1, :], mod[r:r + 1, b, :], start=True, stop=True)
                mm.then_inc(gate_rows, 1)

            def turn_x1(half, t):
                pe.wait_ge(x1_ready, 2 * half + t + 1)
                for k in range(4):
                    mm = pe.transpose(ps[:, 2 + 2 * t + half, k * P:k * P + P],
                                      x_sb[:, t, 512 * half + k * P:512 * half + k * P + P], ident)
                mm.then_inc(x1_turned, 1)

            def route(half, t):
                pe.wait_ge(x1T_ready, 2 * half + t + 1)
                for k in range(4 * half, 4 * half + 4):
                    mm = pe.matmul(ps[:, 6 + t, 0:E], hT[:, k, t * P:t * P + P], wra[:, k, :],
                                   start=(k == 0), stop=(k == KD - 1))
                if half:
                    mm.then_inc(logits_done, 1)

            for n in range(len(CHUNKS)):
                what = STREAM.index(("w", n)) + 1
                if what < len(STREAM) and STREAM[what][0] == "ada":
                    ada_chunk(*STREAM[what][1:])
                product(n)
                if n == FLIP_AFTER:
                    pe.wait_ge(xT_act, 2)
                    pe.wait_ge(xT_dve, 2)
                    pe.wait_ge(bias_back, 16)
                    for b in range(4):
                        pe.matmul(ps[:, 2 + b, :], flip, hankel[:, 2 * b:2 * b + 2, :], start=True,
                                  stop=True).then_inc(flip_done, 1)
                for kind, step in AFTER.get(n, []):
                    if kind == "att":
                        attention(step)
                    else:
                        mod_step(step)
                if n == ROUTER_BIAS:
                    pe.wait_ge(wra_ready, 1)
                    pe.wait_ge(gates_ready, 2)
                    pe.matmul(ps[:, 7, 0:E], ones, wsh, start=True, stop=True).then_inc(bias_r_done, 1)
                if n == LAST_CHUNK[MG1] - 1:
                    for t in range(T):
                        turn_x1(0, t)
            pe.wait_ge(bias_r_ready, 1)
            for t in range(T):
                route(0, t)

            for t in range(T):
                turn_x1(1, t)
            for t in range(T):
                route(1, t)
            pe.wait_ge(mask_ready, 2)
            pe.matmul(ps[:, 2, 0:E], tri, mask[:, 0, :], start=True, stop=True)
            pe.matmul(ps[:, 2, E:2 * E], ones, mask[:, 0, :], start=True, stop=False)
            pe.matmul(ps[:, 2, E:2 * E], tri, mask[:, 1, :], start=False, stop=True)
            pe.matmul(ps[:, 2, 2 * E:3 * E], ones, mask[:, 0, :], start=True, stop=False)
            pe.matmul(ps[:, 2, 2 * E:3 * E], ones, mask[:, 1, :], start=False, stop=True).then_inc(pos_done, 1)
            def gather():
                for k in range(KD):
                    for t in range(T):
                        mm = pe.matmul(ps[:, 2, k * CAP:k * CAP + CAP], x_sb[:, t, k * P:k * P + P],
                                       g_hot[:, t, :], start=(t == 0), stop=(t == T - 1))
                mm.then_inc(gather_done, 1)

            pe.wait_ge(hot_ready, 1)
            gather()
            pe.wait_ge(comb_ready, 2)
            for t in range(T):
                mm = pe.transpose(ps[0:E, 7, t * P:t * P + P], comb[:, t, :], ident)
            mm.then_inc(comb_turned, 1)

            def scatter(m):
                pe.wait_ge(st_ready, m + 1)
                pe.wait_ge(y_ready, 2 * m + 1)
                pe.wait_ge(acc_ready, m + 1)
                for t in range(T):
                    for half in range(2):
                        mm = pe.matmul(ps[:, 4 + 2 * t + half, :], st[:, t * P:t * P + P],
                                       y2[:, 512 * half:512 * half + 512], start=True, stop=True)
                    mm.then_inc(scatter_done, 1)

            pe.wait_ge(routed, 1)
            final = pe.value_load(last_pair[0:1, 0:1], min_val=E // 2 - 1, max_val=ROUNDS * E // 2 - 1)

            def pair(m, last):
                for p in range(2):
                    i = 2 * m + p
                    pe.wait_ge(xg_ready, i + 1)
                    pe.wait_ge(gu_free, i + 1)
                    pe.wait_ge(sel_ready, i + 1)
                    for j in range(2):
                        for g in range(2):
                            col = 1024 * g + 512 * j
                            pe.matmul(ps[CAP * g:CAP * g + CAP, j, :], sel, bgu[:, col:col + 512],
                                      start=True, stop=False)
                    for k in range(KD):
                        wait_slot(pe, k, m, p)
                        buf = expert[slot(k, p)]
                        for j in range(2):
                            for g in range(2):
                                col = 1024 * g + 512 * j
                                mm = pe.matmul(ps[CAP * g:CAP * g + CAP, j, :], xg[:, k, :],
                                               buf[:, col:col + 512], start=False, stop=(k == KD - 1))
                        mm.then_inc(up_used, 1)
                    if p == 0:
                        scatter(m)
                    else:
                        pe.wait_ge(wp_ready, i + 1)
                        for t in range(T):
                            mm = pe.transpose(ps[:, 7, t * P:t * P + P], wp[:, t, :], ident)
                        mm.then_inc(wp_turned, 1)
                    if not (last and p == 1):
                        pe.wait_ge(hot_ready, i + 2)
                        gather()
                    pe.wait_ge(act_ready, i + 1)
                    for q in range(4):
                        mm = pe.transpose(ps[:, 3, q * P:q * P + P], act_sb[:, q * P:q * P + P], ident)
                    mm.then_inc(act_turned, 1)
                    pe.wait_ge(aT_ready, i + 1)
                    if p == 0:
                        pe.wait_ge(acc_ready, m + 2)
                    else:
                        pe.wait_ge(y_ready, i + 1)
                    for q in range(F // P):
                        n = UP_SLOTS + q // 2
                        g, ch = q // 4, q % 4
                        if q % 2 == 0:
                            wait_slot(pe, n, m, p)
                        for half in range(2):
                            mm = pe.matmul(ps[CAP * half:CAP * half + CAP, 6, :], aT[:, ch, CAP * g:CAP * g + CAP],
                                           expert[n][:, 1024 * (q % 2) + 512 * half:1024 * (q % 2) + 512 * half + 512],
                                           start=(q == 0), stop=(q == F // P - 1))
                        if q % 2 == 1:
                            mm.then_inc(down_used, 1)
            with pe.Fori(0, final) as m:
                pair(m, False)
            pair(final, True)
            pe.wait_ge(st_ready, final + 2)
            pe.wait_ge(y_ready, 2 * final + 3)
            pe.wait_ge(acc_ready, final + 2)
            for t in range(T):
                for half in range(2):
                    pe.matmul(ps[:, 4 + 2 * t + half, :], st[:, t * P:t * P + P], y2[:, 512 * half:512 * half + 512],
                              start=True, stop=True).then_inc(last_scatter, 1)

        @block.scalar
        def _(act):
            own = Steps(act, act_step)
            act.dma_start(rows[V_C:V_C + KD, :], c[0].rearrange("(k n) -> k n", n=P)).then_inc(rows_landed, 16)
            act.dma_start(rows[V_G1:V_G1 + KD, :], norm1_g[0].rearrange("(k n) -> k n", n=P)).then_inc(rows_landed, 16)
            act.dma_start(rows[V_G2:V_G2 + KD, :], norm2_g[0].rearrange("(k n) -> k n", n=P)).then_inc(rows_landed, 16)
            act.dma_start(rows[V_CB:V_CB + KC, :], conv_b[0].rearrange("(k n) -> k n", n=P)).then_inc(rows_landed, 16)
            act.dma_start(rows[V_CW:V_CW + 3 * KC, :],
                          conv_w[0].rearrange("j (k n) -> (j k) n", n=P)).then_inc(rows_landed, 16)
            act.dma_start(rows[V_SUB:V_SUB + 1, :], subln_g).then_inc(rows_landed, 16)
            for n, v in enumerate((lambda_q1, lambda_k1, lambda_q2, lambda_k2)):
                if n < 2:
                    act.dma_start(lam_rows[:, n, :], v).then_inc(rows_landed, 16)
            act.dma_start(lam_rows[:, 2, :], lambda_q2).then_inc(lam_prod, 16)
            act.dma_start(lam_rows[:, 3, :], lambda_k2).then_inc(lam_prod, 16)
            for g in range(4):
                act.dma_start(bada[32 * g:32 * g + 32, :, :],
                              dap(b_ada, 512 * g, [[0, 32], [SLOT, 3], [1, 512]])).then_inc(ada_b_landed, 16)
            act.dma_start(wr, w_router[0].rearrange("(k p) n -> p k n", p=P)).then_inc(wr_landed, 16)
            act.dma_start(brb, dap(b_router, 0, [[0, P], [1, E]])).then_inc(wr_landed, 16)

            for t in range(T):
                act.wait_ge(x_landed, 16 * T)
                act.activation(xn[:, t, :], x_sb[:, t, :], ACT.Square, accum_out=stat[:, t:t + 1]).then_inc(sumsq, 1)
            act.wait_ge(vec_ready, 1)
            act.activation(csig, vecT[:, V_C:V_C + KD], ACT.Sigmoid).then_inc(csig_ready, 1)
            act.wait_ge(lam_exp, 1)
            act.activation(lam_s[:, 2:4], lam_s[:, 0:2], ACT.Exp).then_inc(lam_exp, 1)
            act.wait_ge(g_ready, 1)
            act.dma_start(scratch, g_sb).then_inc(bias_out, 16)
            act.wait_ge(x_turned, 1)
            for b in (1, 3):
                act.activation(hT[:, 2 * b:2 * b + 2, :], ps[:, 2 + b, :].rearrange("p (k n) -> p k n", k=2),
                               ACT.Copy).then_inc(xT_act, 1)

            def h_parts(half):
                act.wait_ge(a1_ready, 1)
                act.wait_ge(xT_act, 2)
                act.wait_ge(xT_dve, 2)
                for k in range(4 * half, 4 * half + 4):
                    ins = act.activation(x_hi[:, k, :], hT[:, k, :], ACT.Identity, scale=a1[:, k:k + 1],
                                         bias=modT[:, M_SH1 + k:M_SH1 + k + 1])
                ins.then_inc(h_hi_ready, 1)

            def split(n):
                wait_chunk(act, ("w", n))
                if n >= 2:
                    act.wait_ge(half_done, 2 * (n - 2) + 2)
                else:
                    act.wait_ge(ada_used, STAGE + 2 * n + 2)
                src = front_chunk(STREAM.index(("w", n)))[0][:, :].rearrange("p (k n) -> p k n", k=4)
                act.activation(w_hi[n % 2], src, ACT.Copy).then_inc(hi_ready, 1)

            def evacuate(p, h):
                src = ps[:, h, :]
                pair = src.rearrange("p (b n) -> p b n", b=2)
                if p == CU or p > GB1:
                    return
                wait_product(act, p, h)
                if p in (Q0, Q1):
                    first = 4 * (p == Q1) + 2 * h
                    ins = act.activation(qT[:, first:first + 2, :], pair, ACT.Copy, scale=HD ** -0.5)
                elif p in (K0, K1):
                    first = 4 * (p == K1) + 2 * h
                    ins = act.activation(kT[:, first:first + 2, :], pair, ACT.Copy)
                elif p in (V0, V1):
                    if p == V0:
                        act.wait_ge(flip_done, 4)
                    first = 512 * (p == V1)
                    ins = act.activation(v_sb[:, h, first:first + 512], src, ACT.Copy)
                elif p == CB:
                    ins = act.activation(bT[:, 2 * h:2 * h + 2, :], pair, ACT.Copy)
                elif p == CC:
                    ins = act.activation(cT[:, 2 * h:2 * h + 2, :], pair, ACT.Copy)
                else:
                    gate = ga if p in (GA0, GA1) else gb
                    first = 4 * (p in (GA1, GB1)) + 2 * h
                    ins = act.activation(gate[:, first:first + 2, :], pair, ACT.Sigmoid)
                ins.then_inc(bank_free[h], 1)

            def attention(n):
                if n < H:
                    act.wait_ge(scores_read, n + 1)
                    for s in range(4):
                        b, m = s // 2, s % 2
                        seg = logit[:, m, 0:P] if b == 0 else logit[:, m, P:P + S]
                        ins = act.activation(seg, seg, ACT.Exp, bias=neg_max[:, s:s + 1],
                                             accum_out=sums[:, s:s + 1])
                    ins.then_inc(exp_done, 1)
                if 1 <= n <= H:
                    act.wait_ge(attn_turned, n)
                    if n >= 2:
                        act.wait_ge(pv_done, n - 1)
                    act.activation(pT, ps[:, 4, 0:384], ACT.Copy).then_inc(pT_ready, 1)
                if 2 <= n <= H + 1:
                    act.wait_ge(pv_done, n - 1)
                    for t in range(T):
                        ins = own.done(act.activation(junk[:, 0:P], ps[:, 5, t * P:t * P + P], ACT.Square,
                                                      accum_out=oss[:, t:t + 1]))
                        own.wait()
                    act.activation(junk[:, P:P + 1], junk[:, 0:1], ACT.Copy).then_inc(osq_done, 1)
                if 3 <= n <= H + 2:
                    act.wait_ge(o_turned, n - 2)
                    act.activation(o_hi[:, n - 3, :], ps[:, 7, 0:S], ACT.Copy, scale=sub[:, 0:1]).then_inc(oT_hi, 1)

            h_parts(0)
            split(0)
            act.wait_ge(bias_out, 16)
            act.dma_start(hankel, dap(scratch, 0, [[1, P], [384, H], [1, S]])).then_inc(bias_back, 16)
            h_parts(1)
            split(1)
            for n, (p, j) in enumerate(CHUNKS):
                if n == LAST_CHUNK[p]:
                    for h in range(2):
                        evacuate(p, h)
                if n + 2 < len(CHUNKS):
                    split(n + 2)
                if n == FLIP_AFTER:
                    for b in range(4):
                        act.wait_ge(flip_done, b + 1)
                        act.activation(bias_t[:, 2 * b:2 * b + 2, :],
                                       ps[:, 2 + b, :].rearrange("p (h n) -> p h n", h=2),
                                       ACT.Copy).then_inc(flip_read, 1)
                for kind, step in AFTER.get(n, []):
                    if kind == "att":
                        attention(step)
                if n == CONV_HI:
                    act.wait_ge(conv_ready, 1)
                    act.wait_ge(mod_ready, 3)
                    act.activation(b_hi, bT, ACT.Copy).then_inc(conv_hi, 1)
                if n == LAST_CHUNK[CU]:
                    act.wait_ge(kv_dead, 1)
                    act.dma_start(bgu[0:E, :], b_gate_up[0]).then_inc(late_landed, 16)
                    act.wait_ge(zeroed, 2)
                    act.dma_start(y2[0:E, :], b_down[0]).then_inc(late_landed, 16)
                if p in (WO0, WO1) and n == LAST_CHUNK[p]:
                    for q in (2 * (p == WO1), 2 * (p == WO1) + 1):
                        act.wait_ge(m_ready, q + 1)
                        act.activation(x_hi[:, 2 * q:2 * q + 2, :], mT[:, 2 * q:2 * q + 2, :],
                                       ACT.Copy).then_inc(m_hi, 1)
            act.activation(scrap[:, 0:1], ones[:, 0:1], ACT.Exp)
            for half in range(2):
                for t in range(T):
                    act.wait_ge(x1_ready, 2 * half + t + 1)
                    if half or t:
                        act.wait_ge(x1_sumsq, 2 * half + t)
                    act.activation(junk2, x_sb[:, t, 512 * half:512 * half + 512], ACT.Square,
                                   accum_out=stat[:, 4 + 2 * half + t:5 + 2 * half + t]).then_inc(x1_sumsq, 1)
                for t in range(T):
                    act.wait_ge(x1_turned, 2 * half + t + 1)
                    act.activation(hT[:, 4 * half:4 * half + 4, t * P:t * P + P],
                                   ps[:, 2 + 2 * t + half, :].rearrange("p (k n) -> p k n", k=4),
                                   ACT.Copy).then_inc(x1T_ready, 1)
            for t in range(T):
                act.wait_ge(lg_ready, t + 1)
                act.activation(ex[:, t, :], lg[t][:, 0:E], ACT.Exp, bias=ntop[:, t:t + 1]).then_inc(ex_ready, 1)
            act.dma_start(nfb, dap(normf_g, 0, [[0, P], [1, D]])).then_inc(nf_landed, 16)
            act.wait_ge(routed, 1)
            final = act.value_load(last_pair[0:1, 0:1], min_val=E // 2 - 1, max_val=ROUNDS * E // 2 - 1)
            with act.Fori(0, final + 1) as m:
                for p in range(2):
                    i = 2 * m + p
                    act.wait_ge(glu_ready, i + 1)
                    act.activation(sig, glu, ACT.Sigmoid, scale=ALPHA).then_inc(sig_ready, 1)
                    act.wait_ge(act_turned, i + 1)
                    act.activation(aT, ps[:, 3, :].rearrange("p (c n) -> p c n", c=4), ACT.Copy).then_inc(aT_ready, 1)
            for n in range(2 * T):
                t, half = n // 2, n % 2
                act.wait_ge(fin_ready, n + 1)
                if n:
                    act.wait_ge(fin_sumsq, n)
                act.activation(junk2, acc[:, t, 512 * half:512 * half + 512], ACT.Square,
                               accum_out=stat[:, 4 + 2 * half + t:5 + 2 * half + t]).then_inc(fin_sumsq, 1)

        @block.vector
        def _(v):
            own = Steps(v, dve_step)

            def normalise(dst, src, r):
                return v.tensor_scalar(dst, src, r, None, ALU.mult)

            v.wait_ge(vec_turned, 1)
            v.tensor_copy(vecT, ps[:, 7, 0:NVEC]).then_inc(vec_ready, 1)
            v.wait_ge(lam_prod, 32)
            lam = lam_rows.rearrange("p (a b) n -> p a b n", b=2)
            own.done(v.tensor_tensor(lam[:, :, 0, :], lam[:, :, 0, :], lam[:, :, 1, :], ALU.mult))
            own.wait()
            v.tensor_reduce(lam_s[:, 0:2], lam[:, :, 0, :], AX, ALU.add).then_inc(lam_exp, 1)
            v.wait_ge(g_made, 1)
            v.tensor_copy(g_sb, ps[0:H, 6, 0:384]).then_inc(g_ready, 1)
            v.wait_ge(r_x_ready, 1)
            for t in range(T):
                normalise(xn[:, t, :], x_sb[:, t, :], stat[:, 2 + t:3 + t]).then_inc(xn_ready, 1)
            v.wait_ge(csig_ready, 1)
            own.done(v.tensor_tensor(csig, csig, vecT[:, V_C:V_C + KD], ALU.mult))
            own.wait()
            v.tensor_copy(cs32, csig.unsqueeze(2).broadcast_to([P, KD, 32])).then_inc(c_ready, 1)
            v.wait_ge(lam_exp, 2)
            own.done(v.tensor_tensor(lam_s[:, 4:5], lam_s[:, 3:4], lam_s[:, 2:3], ALU.subtract))
            own.wait()
            v.tensor_scalar(lam_s[:, 4:5], lam_s[:, 4:5], -LAM_INIT, None, ALU.add).then_inc(lam_out, 1)
            v.wait_ge(lam_ready, 1)
            v.tensor_copy(nlam, ps[:, 7, 0:1]).then_inc(lam_ready, 1)
            v.tensor_scalar(sub, vecT[:, V_SUB:V_SUB + 1], 1.0 - LAM_INIT, None, ALU.mult)
            v.wait_ge(x_turned, 1)
            for b in (0, 2):
                v.tensor_copy(hT[:, 2 * b:2 * b + 2, :],
                              ps[:, 2 + b, :].rearrange("p (k n) -> p k n", k=2)).then_inc(xT_dve, 1)

            def mod_rows(b):
                v.wait_ge(ada_used, 8 * (b + 1))
                v.wait_ge(ada_b_landed, 64)
                v.tensor_tensor(mod[:, b, :], ps[:, 6, :], bada[:, b, :], ALU.add).then_inc(mod_ready, 1)

            def mod_cols(b):
                v.wait_ge(mod_turned, b + 1)
                src = ps[:, 7, :].rearrange("p (j g r) -> p g j r", j=4, r=32)[:, :, :, 0]
                v.tensor_copy(modT[:, 16 * b:16 * b + 16].rearrange("p (g j) -> p g j", g=4), src).then_inc(modT_ready, 1)

            mod_rows(0)
            mod_cols(0)
            v.wait_ge(modT_ready, 1)
            v.scalar_tensor_tensor(out=a1, in0=modT[:, M_SC1:M_SC1 + KD], scalar=1.0, in1=vecT[:, V_G1:V_G1 + KD],
                                   op0=ALU.add, op1=ALU.mult).then_inc(a1_ready, 1)
            v.wait_ge(a1_ready, 1)

            def h_parts(half):
                v.wait_ge(xT_act, 2)
                v.wait_ge(xT_dve, 2)
                for k in range(4 * half, 4 * half + 4):
                    own.done(v.tensor_scalar(h_sb[:, k, :], hT[:, k, :], a1[:, k:k + 1],
                                             modT[:, M_SH1 + k:M_SH1 + k + 1], ALU.mult, ALU.add))
                own.wait()
                v.wait_ge(h_hi_ready, half + 1)
                ks = slice(4 * half, 4 * half + 4)
                v.tensor_tensor(x_lo[:, ks, :], h_sb[:, ks, :], x_hi[:, ks, :], ALU.subtract).then_inc(h_lo_ready, 1)

            def split(n):
                v.wait_ge(hi_ready, n + 1)
                src = front_chunk(STREAM.index(("w", n)))[0][:, :].rearrange("p (k n) -> p k n", k=4)
                v.tensor_tensor(w_lo[n % 2], src, w_hi[n % 2], ALU.subtract).then_inc(lo_ready, 1)

            def attention(n, between):
                if n < H:
                    v.wait_ge(scores_done, n + 1)
                    if n == 0:
                        v.wait_ge(bias_whole, 1)
                    else:
                        v.wait_ge(attn_ready, n)
                    own.done(v.tensor_tensor(logit[:, :, 0:P], ps[:, 2:4, 0:P],
                                             bias_t[:, n, P:S].unsqueeze(1).broadcast_to([P, 2, P]), ALU.add))
                    own.done(v.tensor_tensor(logit[:, :, P:P + S], ps[:, 2:4, P:P + S],
                                             bias_t[:, n, :].unsqueeze(1).broadcast_to([P, 2, S]), ALU.add))
                    own.wait()
                    v.tensor_reduce(neg_max[:, 0:2], logit[:, :, 0:P], AX, ALU.max, negate=True)
                    v.tensor_reduce(neg_max[:, 2:4], logit[:, :, P:P + S], AX, ALU.max,
                                    negate=True).then_inc(scores_read, 1)
                between()
                if 3 <= n <= H + 2:
                    h = n - 3
                    v.wait_ge(oT_hi, h + 1)
                    v.scalar_tensor_tensor(out=o_lo[:, h, :], in0=ps[:, 7, 0:S], scalar=sub[:, 0:1],
                                           in1=o_hi[:, h, :], op0=ALU.mult, op1=ALU.subtract).then_inc(oT_ready, 1)
                if n < H:
                    v.wait_ge(exp_done, n + 1)
                    own.done(v.reciprocal(inv, sums))
                    own.wait()
                    own.done(v.tensor_scalar(inv[:, 1:4:2], inv[:, 1:4:2], nlam, None, ALU.mult))
                    own.wait()
                    segs = (slice(0, P), slice(P, P + S))
                    for b in range(2):
                        own.done(v.tensor_scalar(logit[:, 1, segs[b]], logit[:, 1, segs[b]],
                                                 inv[:, 2 * b + 1:2 * b + 2], None, ALU.mult))
                    own.wait()
                    if n >= 1:
                        v.wait_ge(attn_turned, n)
                    for b in range(2):
                        ins = v.scalar_tensor_tensor(out=attn[:, segs[b]], in0=logit[:, 0, segs[b]],
                                                     scalar=inv[:, 2 * b:2 * b + 1], in1=logit[:, 1, segs[b]],
                                                     op0=ALU.mult, op1=ALU.add)
                    ins.then_inc(attn_ready, 1)
                if 2 <= n <= H + 1:
                    v.wait_ge(r_o_ready, n - 1)
                    if n >= 3:
                        v.wait_ge(o_turned, n - 2)
                    for t in range(T):
                        ins = normalise(o_n[:, t, :], ps[:, 5, t * P:t * P + P], ors[:, t:t + 1])
                    ins.then_inc(o_ready, 1)

            def mod_step(n):
                if n < 2:
                    mod_cols(n + 1)
                    return
                v.wait_ge(gate_rows, n - 1)
                v.tensor_copy((g1b if n == 2 else g2b).rearrange("p (b n) -> p b n", b=2),
                              ps[:, 6:8, :]).then_inc(gates_ready, 1)

            def router_weights():
                v.wait_ge(modT_ready, 3)
                own.done(v.scalar_tensor_tensor(out=a2, in0=modT[:, M_SC2:M_SC2 + KD], scalar=1.0,
                                                in1=vecT[:, V_G2:V_G2 + KD], op0=ALU.add, op1=ALU.mult))
                own.wait()
                v.wait_ge(wr_landed, 32)
                own.done(v.tensor_tensor(wra, wr, modT[:, M_SH2:M_SH2 + KD].unsqueeze(2).broadcast_to([P, KD, E]),
                                         ALU.mult))
                own.wait()
                own.done(v.tensor_reduce(wsh, wra.rearrange("p k n -> p n k"), AX, ALU.add))
                own.wait()
                v.tensor_tensor(wra, wr, a2.unsqueeze(2).broadcast_to([P, KD, E]), ALU.mult).then_inc(wra_ready, 1)

            def conv_u(h):
                if h == 0:
                    own.done(v.memset(cu[:, :, 0:2], 0.0))
                wait_product(v, CU, h)
                wait_evacuated(v, CC, 0)
                wait_evacuated(v, CC, 1)
                v.tensor_tensor(cu[:, 2 * h:2 * h + 2, 2:2 + S], ps[:, h, :].rearrange("p (b n) -> p b n", b=2),
                                cT[:, 2 * h:2 * h + 2, :], ALU.mult).then_inc(bank_free[h], 1)

            def conv_tap(j):
                wait_evacuated(v, CU, 0)
                wait_evacuated(v, CU, 1)
                own.wait()
                for k in range(KC):
                    w = vecT[:, V_CW + j * KC + k:V_CW + j * KC + k + 1]
                    tap = cu[:, k, j:j + S]
                    if j == 0:
                        own.done(v.tensor_scalar(cT[:, k, :], tap, w, vecT[:, V_CB + k:V_CB + k + 1],
                                                 ALU.mult, ALU.add))
                    else:
                        own.done(v.scalar_tensor_tensor(out=cT[:, k, :], in0=tap, scalar=w, in1=cT[:, k, :],
                                                        op0=ALU.mult, op1=ALU.add))

            def merge_a(p, h):
                q = 2 * (p == OC1) + h
                wait_product(v, p, h)
                v.tensor_tensor(mT[:, 2 * q:2 * q + 2, :], ps[:, h, :].rearrange("p (b n) -> p b n", b=2),
                                ga[:, 2 * q:2 * q + 2, :], ALU.mult).then_inc(bank_free[h], 1)

            def merge_b(p, h):
                q = 2 * (p == WO1) + h
                wait_product(v, p, h)
                g = gb[:, 2 * q:2 * q + 2, :]
                v.tensor_tensor(g, ps[:, h, :].rearrange("p (b n) -> p b n", b=2), g, ALU.mult).then_inc(bank_free[h], 1)
                wait_evacuated(v, p, h)
                v.tensor_tensor(mT[:, 2 * q:2 * q + 2, :], mT[:, 2 * q:2 * q + 2, :], g, ALU.add).then_inc(m_ready, 1)

            def merged_lo(q):
                v.wait_ge(m_hi, q + 1)
                v.tensor_tensor(x_lo[:, 2 * q:2 * q + 2, :], mT[:, 2 * q:2 * q + 2, :], x_hi[:, 2 * q:2 * q + 2, :],
                                ALU.subtract).then_inc(m_lo, 1)

            def residual(half, t):
                n, cols = 2 * half + t, slice(512 * half, 512 * half + 512)
                p = (MG0, MG1)[half]
                tmp = r_v[:, 512 * n:512 * n + 512]
                wait_product(v, p, t)
                v.tensor_tensor(tmp, ps[:, t, :], g1b[:, cols], ALU.mult).then_inc(bank_free[t], 1)
                wait_evacuated(v, p, t)
                v.tensor_tensor(x_sb[:, t, cols], x_sb[:, t, cols], tmp, ALU.add).then_inc(x1_ready, 1)

            h_parts(0)
            split(0)
            h_parts(1)
            split(1)
            for n, (p, j) in enumerate(CHUNKS):
                def split_next():
                    if n + 2 < len(CHUNKS):
                        split(n + 2)

                what = STREAM.index(("w", n))
                if STREAM[what + 1:what + 2] and STREAM[what + 1][0] == "ada" and STREAM[what + 1][2] == KD - 1:
                    mod_rows(STREAM[what + 1][1])
                ends = n == LAST_CHUNK[p]
                for h in range(2 if ends else 0):
                    if p == CU:
                        conv_u(h)
                    elif p in (OC0, OC1):
                        merge_a(p, h)
                    elif p in (WO0, WO1):
                        merge_b(p, h)
                    elif p == MG0:
                        residual(0, h)
                steps = AFTER.get(n, [])
                if not steps or steps[0][0] != "att":
                    split_next()
                if ends and p == CU:
                    for tap in range(3):
                        conv_tap(tap)
                    own.wait()
                    v.tensor_tensor(bT, bT, cT, ALU.mult).then_inc(conv_ready, 1)
                if n == CONV_LO:
                    v.wait_ge(conv_hi, 1)
                    v.tensor_tensor(b_lo, bT, b_hi, ALU.subtract).then_inc(conv_lo, 1)
                if ends and p in (WO0, WO1):
                    for q in (2 * (p == WO1), 2 * (p == WO1) + 1):
                        merged_lo(q)
                for kind, step in steps:
                    if kind == "att":
                        attention(step, split_next)
                    else:
                        mod_step(step)
                if n == ROUTER_WEIGHTS:
                    router_weights()
                    v.wait_ge(late_landed, 32)
                    v.wait_ge(gates_ready, 2)
                    v.tensor_tensor(y2[0:E, :], y2[0:E, :], g2b[0:E, :], ALU.mult).then_inc(y_ready, 1)
                if n == ROUTER_BIAS + 1:
                    v.wait_ge(bias_r_done, 1)
                    v.tensor_tensor(brb, brb, ps[:, 7, 0:E], ALU.add).then_inc(bias_r_ready, 1)
            for t in range(T):
                residual(1, t)
            for t in range(T):
                own.done(v.memset(lg[t][:, E:E + TOPK], TAKEN))
                own.done(v.memset(rep[:, t, TOPK:8], TAKEN))
            for t in range(T):
                v.wait_ge(logits_done, t + 1)
                v.wait_ge(r_x1_ready, t + 1)
                own.done(v.scalar_tensor_tensor(out=lg[t][:, 0:E], in0=ps[:, 6 + t, 0:E], scalar=stat[:, 2 + t:3 + t],
                                                in1=brb, op0=ALU.mult, op1=ALU.add))
                own.wait()
                own.done(v.max(top[:, t, :], lg[t][:, 0:E]))
                own.wait()
                v.tensor_scalar(ntop[:, t:t + 1], top[:, t, 0:1], -1.0, None, ALU.mult).then_inc(lg_ready, 1)
                own.done(v.tensor_copy(rep[:, t, 0:TOPK], top[:, t, 0:TOPK]))
                own.wait()
                own.done(v.match_replace(left[:, t, :], rep[:, t, :], lg[t], -TAKEN))
                own.wait()
                v.tensor_tensor(mask[:, t, :], left[:, t, 0:E], lg[t][:, 0:E], ALU.not_equal).then_inc(mask_ready, 1)
            for t in range(T):
                v.wait_ge(mask_ready, t + 1)
                v.wait_ge(ex_ready, t + 1)
                own.done(v.tensor_tensor(ex[:, t, :], ex[:, t, :], mask[:, t, :], ALU.mult))
                own.wait()
                own.done(v.tensor_reduce(wsum[:, t:t + 1], ex[:, t, :], AX, ALU.add))
                own.wait()
                own.done(v.reciprocal(wsum[:, t:t + 1], wsum[:, t:t + 1]))
                own.wait()
                v.tensor_scalar(comb[:, t, :], ex[:, t, :], wsum[:, t:t + 1], None, ALU.mult).then_inc(comb_ready, 1)
            v.wait_ge(pos_done, 1)
            own.done(v.scalar_tensor_tensor(out=posm, in0=ps[:, 2, 0:2 * E].rearrange("p (t n) -> p t n", t=T),
                                            scalar=1.0, in1=mask, op0=ALU.add, op1=ALU.mult))
            own.done(v.tensor_reduce(cntm, ps[:, 2, 2 * E:3 * E], AX, ALU.max))
            own.wait()
            own.done(v.tensor_scalar(posm, posm, -1.0, None, ALU.add))
            own.done(v.tensor_scalar(over[:, 0:ROUNDS - 1], thr, cntm, None, ALU.is_lt))
            own.wait()

            def gather_hot(e):
                for t in range(T):
                    ins = v.tensor_scalar(g_hot[:, t, :], iota, posm[:, t, bass.ds(e, 1)] if not isinstance(e, int)
                                          else posm[:, t, e:e + 1], stat[:, 2 + t:3 + t], ALU.is_equal, ALU.mult)
                ins.then_inc(hot_ready, 1)

            def select(e):
                src = ident[:, bass.ds(e, 1)] if not isinstance(e, int) else ident[:, e:e + 1]
                v.tensor_copy(sel, src.broadcast_to([P, CAP])).then_inc(sel_ready, 1)

            def tokens_in():
                own.done(v.tensor_tensor(xg, ps[:, 2, :].rearrange("p (k n) -> p k n", k=KD),
                                         a2.unsqueeze(2).broadcast_to([P, KD, CAP]), ALU.mult))
                own.wait()
                v.tensor_tensor(xg, xg, modT[:, M_SH2:M_SH2 + KD].unsqueeze(2).broadcast_to([P, KD, CAP]),
                                ALU.add).then_inc(xg_ready, 1)

            gather_hot(0)
            own.done(v.tensor_reduce(last_f, over[:, 0:ROUNDS - 1], AX, ALU.add))
            own.wait()
            own.done(v.tensor_scalar(last_f, last_f, float(E // 2), float(E // 2 - 1), ALU.mult, ALU.add))
            own.wait()
            v.tensor_copy(last_pair[0:1, :], last_f[0:1, :]).then_inc(routed, 1)
            select(0)
            v.wait_ge(gather_done, 1)
            tokens_in()
            v.tensor_copy(scrap[:, 2:3], ones[:, 0:1]).then_inc(gu_free, 1)
            v.wait_ge(comb_turned, 1)
            v.wait_ge(zeroed, 2)
            v.tensor_copy(st[0:E, :], ps[0:E, 7, 0:S]).then_inc(st_ready, 1)
            v.wait_ge(st_ready, 1)
            v.tensor_copy(scrap[:, 4:5], ones[:, 0:1]).then_inc(acc_ready, 1)
            v.wait_ge(acc_started, T)
            own.wait()

            def accumulate(m):
                for t in range(T):
                    v.wait_ge(scatter_done, 2 * m + t + 1)
                    ins = v.tensor_tensor(acc[:, t, :], acc[:, t, :],
                                          ps[:, 4 + 2 * t:6 + 2 * t, :].rearrange("p b n -> p (b n)"), ALU.add)
                ins.then_inc(acc_ready, 1)

            final = v.value_load(last_pair[0:1, 0:1], min_val=E // 2 - 1, max_val=ROUNDS * E // 2 - 1)
            before, per_pair = own.n, 2 * 3

            def pair(m, last):
                for p in range(2):
                    i = 2 * m + p
                    e, e_next = (2 * m + p) % E, (2 * m + p + 1) % E
                    if not (last and p == 1):
                        v.wait_ge(gather_done, i + 1)
                        gather_hot(e_next)
                    if p == 0:
                        v.wait_ge(st_ready, m + 1)
                    for t in range(T):
                        ins = v.tensor_scalar(wp[:, t, CAP * p:CAP * p + CAP], iota, posm[:, t, bass.ds(e, 1)],
                                              comb[:, t, bass.ds(e, 1)], ALU.is_equal, ALU.mult)
                    ins.then_inc(wp_ready, 1)
                    v.wait_ge(wp_ready, i + 1)
                    own.done(v.tensor_scalar(posm[:, :, bass.ds(e, 1)], posm[:, :, bass.ds(e, 1)], float(-CAP), None,
                                             ALU.add))
                    v.wait_ge(up_used, UP_SLOTS * (i + 1))
                    gu = ps[:, 0:2, :].rearrange("p b (n two) -> p b n two", two=2)
                    v.tensor_scalar(glu.rearrange("p (b n) -> p b n", b=2), gu[:, :, :, 0], LIMIT, None,
                                    ALU.min).then_inc(glu_ready, 1)
                    v.tensor_scalar(lin.rearrange("p (b n) -> p b n", b=2), gu[:, :, :, 1], LIMIT, -LIMIT,
                                    ALU.min, ALU.max).then_inc(gu_free, 1)
                    v.wait_ge(glu_ready, i + 1)
                    v.wait_ge(gu_free, i + 2)
                    own.done(v.scalar_tensor_tensor(out=lin, in0=lin, scalar=1.0, in1=glu, op0=ALU.add, op1=ALU.mult))
                    own.wait()
                    v.wait_ge(sig_ready, i + 1)
                    v.tensor_tensor(act_sb, lin, sig, ALU.mult).then_inc(act_ready, 1)
                    select(e_next)
                    if p == 0:
                        accumulate(m)
                    else:
                        v.wait_ge(wp_turned, m + 1)
                        v.tensor_copy(st, ps[:, 7, 0:S]).then_inc(st_ready, 1)
                    if not (last and p == 1):
                        v.wait_ge(gather_done, i + 2)
                        tokens_in()
                    v.wait_ge(down_used, 4 * i + 4)
                    for half in range(2):
                        rows_in = slice(CAP * half, CAP * half + CAP)
                        ins = v.tensor_tensor(y2[CAP * p:CAP * p + CAP, 512 * half:512 * half + 512],
                                              ps[rows_in, 6, :], g2b[rows_in, 512 * half:512 * half + 512], ALU.mult)
                    ins.then_inc(y_ready, 1)

            with v.Fori(0, final) as m:
                own.n, own.base = before, per_pair * m
                pair(m, False)
                assert own.n == before + per_pair, own.n - before
            own.n, own.base = before, per_pair * final
            pair(final, True)
            for n in range(2 * T):
                part = acc[:, n // 2, 512 * (n % 2):512 * (n % 2) + 512]
                v.wait_ge(last_scatter, n + 1)
                v.tensor_tensor(part, part, ps[:, 4 + n, :], ALU.add).then_inc(fin_ready, 1)
            v.wait_ge(nf_landed, 16)
            for n in range(2 * T):
                t, cols = n // 2, slice(512 * (n % 2), 512 * (n % 2) + 512)
                v.wait_ge(r_fin_ready, t + 1)
                v.wait_ge(fin_ready, n + 1)
                v.scalar_tensor_tensor(out=acc[:, t, cols], in0=acc[:, t, cols], scalar=stat[:, 2 + t:3 + t],
                                       in1=nfb[:, cols], op0=ALU.mult, op1=ALU.mult).then_inc(y_out, 1)


def distance_bucket(dist):
    exact = NB // 2
    d = np.maximum(dist, 1).astype(np.float32)
    large = exact + (np.log(d / np.float32(exact)) / np.float32(math.log(MAX_DISTANCE / exact))
                     * np.float32(NB - exact)).astype(np.int32)
    return np.where(dist < exact, dist, np.minimum(large, NB - 1))


def constants():
    cst = np.zeros((P, NCONST), np.float32)
    cst[:, C_ID:C_ID + P] = np.eye(P)
    cst[:, C_TRI:C_TRI + P] = np.triu(np.ones((P, P)), 1)
    cst[:, C_ONE:C_ONE + P] = 1.0
    cst[:, C_IOTA:C_IOTA + CAP] = np.arange(CAP)
    cst[:, C_THR:C_THR + ROUNDS - 1] = CAP * np.arange(1, ROUNDS)
    cst[:, C_FLIP:C_FLIP + P] = np.eye(P)[::-1]
    dist = np.maximum(S - 1 - np.arange(384), 0)
    hot = (distance_bucket(dist)[None, :] == np.arange(NB)[:, None]).astype(np.float32)
    return cst, hot


_INS = ["x", "c", "w_ada", "b_ada", "norm1_g", "norm2_g", "w_in", "conv_w", "conv_b", "w_out_conv",
        "lambda_q1", "lambda_k1", "lambda_q2", "lambda_k2", "subln_g", "w_o_attn", "w_merge",
        "w_router", "b_router", "w_gate_up", "b_gate_up", "w_down", "b_down", "rel_bias_table", "normf_g"]


def kernel(**inputs):
    import concourse.bacc as _bacc
    from concourse.bass_utils import run_bass_kernel_spmd as _run

    nc = _bacc.Bacc("TRN2", target_bir_lowering=False, num_devices=1)
    cst, hot = constants()
    given = {n: np.ascontiguousarray(inputs[n]) for n in _INS} | {"consts": cst, "buckets": hot}
    arrays, args = {}, []
    for name, a in given.items():
        arrays[f"in_{name}"] = a
        args.append(nc.dram_tensor(f"in_{name}", a.shape, mybir.dt.from_np(a.dtype), kind="ExternalInput").ap())
    args.append(nc.dram_tensor("out_0", (1, S, D), F32, kind="ExternalOutput").ap())
    block_kernel(nc, *args)
    r = _run(nc, [arrays], core_ids=[0])
    return r.results[0]["out_0"]
```

```python
import math
from contextlib import ExitStack

import numpy as np
import concourse.bass as bass
from concourse import mybir

F32 = mybir.dt.float32
F32R = mybir.dt.float32r
I32 = mybir.dt.int32
ALU = mybir.AluOpType
ACT = mybir.ActivationFunctionType
AX = mybir.AxisListType.X

P = 128
D = 1024
S = 256
KD = D // P
T = S // P
CONV = 512
KC = CONV // P
H = 8
HD = 64
VD = 2 * HD
NB = 32
MAX_DISTANCE = 128
E = 32
TOPK = 4
F = 1024
CAP = 64
LIMIT = 7.0
ALPHA = 1.702
EPS = 1e-6
LAM_INIT = 0.8 - 0.6 * math.exp(-0.3 * 0)
MASKED = -3.0e38
TAKEN = 3.0e38
SLOT = 2048
NSLOT = 12
UP_SLOTS = 8
TWICE = 6
ROUNDS = -(-S // CAP)
CATCH_UP = 8
LAST_PARTS = [(0, 0, 4), (1, 0, 5), (0, 1, 2), (1, 1, 7)]

V_G1, V_G2, V_CB, V_CW, V_SUB, V_C = 0, 8, 16, 20, 32, 33
NVEC = 41
M_SH1, M_SC1, M_SH2, M_SC2 = 0, 8, 24, 32
C_ID, C_TRI, C_ONE, C_IOTA, C_THR, C_PAIR, C_FLIP = 0, 128, 256, 384, 448, 452, 454
NCONST = 454 + 128
NSMALL = 1300

Q0, K0, V0, Q1, K1, V1, CB, CC, CU, GA0, GA1, GB0, GB1, OC0, OC1, WO0, WO1, MG0, MG1 = range(19)
PANEL_COL = {CB: 0, CC: 512, CU: 1024, Q0: 1536, Q1: 2048, K0: 2560, K1: 3072, V0: 3584, V1: 4096,
             GA0: 4608, GA1: 5120, GB0: 5632, GB1: 6144}
CHUNKS = [(p, j) for j in range(2) for p in (Q0, K0, V0)]
CHUNKS += [(p, j) for p in range(Q1, 19) for j in range(1 if p in (OC0, OC1) else 2)]
CHUNK_NO = {pj: n for n, pj in enumerate(CHUNKS)}
LAST_CHUNK = {p: CHUNK_NO[(p, 0 if p in (OC0, OC1) else 1)] for p in range(19)}
ADA_FROM = 3
STREAM = [("w", n) for n in range(ADA_FROM)]
_ada = [("ada", b, k) for b in (1, 2) for k in range(KD)]
for _n in range(ADA_FROM, len(CHUNKS)):
    STREAM.append(("w", _n))
    if _ada:
        STREAM.append(_ada.pop(0))
STAGE, WIDE, WIDE_UNTIL = 3, 5, 16
BUFFER, BEFORE, USES = {}, {}, {}
_last = {}
_uses = {b: 0 for b in range(WIDE)}
_wide = True
for _n in range(len(STREAM)):
    _wide = _wide and not (STREAM[_n][0] == "w" and STREAM[_n][1] > WIDE_UNTIL)
    _b = min(range(WIDE if _wide else STAGE), key=lambda b: _last.get(b, -1))
    BEFORE[_n] = _last.get(_b)
    _last[_b] = _n
    _uses[_b] += 1
    BUFFER[_n], USES[_n] = _b, _uses[_b]
FLIP_AFTER = 6
STAGE_ORDER = sorted(range(STAGE), key=lambda b: _last[b])
STAGE_LAST = [STREAM[_last[b]][1] for b in STAGE_ORDER]
AFTER = {7: [("att", 0)], 8: [("att", 1)], 9: [("att", 2)], 10: [("att", 3)], 11: [("att", 4)], 12: [("att", 5)],
         13: [("att", 6)], 14: [("att", 7)], 15: [("att", 8)], 16: [("att", 9)], 17: [("att", 10)],
         19: [("modt", 0)], 20: [("modt", 1)], 21: [("modt", 2)], 22: [("modt", 3)]}
CONV_TAPS, CONV_HI, CONV_LO, ROUTER_WEIGHTS, ROUTER_BIAS, BDOWN_SCALED = (18, 19, 20), 23, 24, 23, 25, 27
EARLY = {8: 0, 11: 1, 20: 2, 28: 3, 32: 4, 33: 5}


class Steps:

    def __init__(self, eng, sem):
        self.eng, self.sem, self.n, self.base = eng, sem, 0, None

    def value(self):
        return self.n if self.base is None else self.base + self.n

    def done(self, ins):
        self.n += 1
        return ins.then_inc(self.sem, 1)

    def wait(self):
        self.eng.wait_ge(self.sem, self.value())


def dap(ap, offset, dims):
    return bass.AP(tensor=ap.tensor, offset=ap.offset + offset, ap=dims)


def block_kernel(nc, x, c, w_ada, b_ada, norm1_g, norm2_g, w_in, conv_w, conv_b, w_out_conv,
                 lambda_q1, lambda_k1, lambda_q2, lambda_k2, subln_g, w_o_attn, w_merge,
                 w_router, b_router, w_gate_up, b_gate_up, w_down, b_down, rel_bias_table, normf_g,
                 consts, buckets, out):
    with ExitStack() as ctx:
        base = [(nc.sbuf_base + 31) // 32 * 32]

        def region(cols):
            cols = -(-cols // 8) * 8
            base[0] += 4 * cols
            return base[0] - 4 * cols

        def at(name, offset, cols, dt=F32):
            return nc.alloc_sbuf_tensor_at(name, [P, cols], dt, offset=offset)

        def sb(name, cols):
            return at(name, region(cols), cols)

        def sem(name):
            return ctx.enter_context(nc.semaphore(name))

        x_sb = sb("x_sb", T * D)[:, :].rearrange("p (t n) -> p t n", t=T)
        o_xn = region(2048)
        r_xn = at("r_xn", o_xn, 2048)
        o_ht = region(2048)
        r_ht = at("r_ht", o_ht, 2048)
        r_q = sb("r_q", 2048)
        o_k = region(2048)
        r_k = at("r_k", o_k, 2048)
        r_v = sb("r_v", 2048)
        o_bias = region(2048)
        r_bias = at("r_bias", o_bias, 2048)
        o_gb = region(2048)
        r_gb = at("r_gb", o_gb, 2048)
        r_work = sb("r_work", 2756)
        r_cu = sb("r_cu", 1544)
        cst = sb("cst", NCONST - 128)
        small = sb("small", NSMALL)
        o_gate, o_oh, o_ol, o_conv, o_bp = region(4096), region(2048), region(2048), region(2048), region(2048)
        o_stage = [region(SLOT) for _ in range(STAGE)]
        o_w = [region(SLOT) for _ in range(4)]
        o_hh, o_hl = region(2048), region(2048)
        assert base[0] <= nc.sbuf_usable_end
        r_gate = at("r_gate", o_gate, 4096)
        r_conv = at("r_conv", o_conv, 2048)
        stage = [at(f"stage{n}", o, SLOT) for n, o in enumerate([*o_stage, o_gate, o_gate + 8192])]
        w_hi = [at(f"w_hi{n}", o_w[2 * n], SLOT, F32R)[:, :].rearrange("p (k n) -> p k n", k=4) for n in range(2)]
        w_lo = [at(f"w_lo{n}", o_w[2 * n + 1], SLOT, F32R)[:, :].rearrange("p (k n) -> p k n", k=4) for n in range(2)]
        x_hi = at("x_hi", o_hh, 2048, F32R)[:, :].rearrange("p (k n) -> p k n", k=KD)
        x_lo = at("x_lo", o_hl, 2048, F32R)[:, :].rearrange("p (k n) -> p k n", k=KD)
        o_hi = at("o_hi", o_oh, 2048, F32R)[:, :].rearrange("p (k n) -> p k n", k=KD)
        o_lo = at("o_lo", o_ol, 2048, F32R)[:, :].rearrange("p (k n) -> p k n", k=KD)
        b_parts = at("b_parts", o_bp, 2048, F32R)
        b_hi = b_parts[:, 0:1024].rearrange("p (k n) -> p k n", k=KC)
        b_lo = b_parts[:, 1024:2048].rearrange("p (k n) -> p k n", k=KC)
        r_bada = at("r_bada", o_bp, 2048)
        ada_first = [at(f"ada_first{n}", o, SLOT)
                     for n, o in enumerate([o_oh, o_ol, o_k, o_gb, o_bias, o_oh, o_ol, o_k])]
        order = [o_xn, o_ht, o_bias, o_conv, o_bp, o_gate, o_oh, o_ol, o_gate + 8192,
                 *(o_stage[b] for b in STAGE_ORDER), *o_w, o_hh, o_hl]
        expert = [at(f"expert{n}", o, SLOT) for n, o in enumerate(order)]

        xn = r_xn[:, :].rearrange("p (t n) -> p t n", t=T)
        hT = r_ht[:, :].rearrange("p (k n) -> p k n", k=KD)
        qT = r_q[:, :].rearrange("p (k n) -> p k n", k=H)
        mT = r_q[:, :].rearrange("p (k n) -> p k n", k=KD)
        h_sb = r_q[:, :].rearrange("p (k n) -> p k n", k=KD)
        acc = r_q[:, :].rearrange("p (t n) -> p t n", t=T)
        kT = r_k[:, :].rearrange("p (k n) -> p k n", k=H)
        bgu = r_k[:, :]
        x1T = r_v[:, :].rearrange("p (k n) -> p k n", k=KD)
        v_sb = r_v[:, :].rearrange("p (t n) -> p t n", t=T)
        hankel = r_gb[:, :].rearrange("p (h n) -> p h n", h=H)
        glu, lin, sig, act_sb = (r_v[:, 512 * n:512 * n + 512] for n in range(4))
        bias_t = r_bias[:, :].rearrange("p (h n) -> p h n", h=H)
        ga = r_gate[:, 0:2048].rearrange("p (k n) -> p k n", k=KD)
        gb = r_gate[:, 2048:4096].rearrange("p (k n) -> p k n", k=KD)
        bada = r_bada[:, :].rearrange("p (b n) -> p b n", b=4)
        mod = [bada[:, b, :] for b in range(4)]
        bT = r_conv[:, 0:1024].rearrange("p (k n) -> p k n", k=KC)
        cT = r_conv[:, 1024:2048].rearrange("p (k n) -> p k n", k=KC)
        cu = r_cu[:, 0:1032].rearrange("p (k n) -> p k n", k=KC)
        flip = r_conv[:, 0:128]
        hot = r_conv[0:NB, 128:512]
        g_sb = r_conv[0:H, 512:896]
        rows = r_conv[0:NVEC, 896:1024]
        cs32 = r_cu[:, 1288:1544].rearrange("p (k n) -> p k n", k=KD)
        lam_rows = r_conv[0:1, 1280:1536].rearrange("p (a n) -> p a n", a=4)
        table = r_conv[0:NB, 1536:1544]
        lam_s = r_conv[0:1, 1544:1552]
        csig = r_conv[:, 1552:1560]
        nfb = r_gb[:, 0:D]
        g1b, g2b = r_gb[:, 0:D], r_gb[:, D:2 * D]
        logit = r_work[:, 0:768].rearrange("p (m n) -> p m n", m=2)
        attn = r_work[:, 768:1152]
        pT = r_work[:, 1152:1536]
        o_n = r_work[:, 1536:1792].rearrange("p (t n) -> p t n", t=T)
        junk = r_work[:, 1792:2048]
        xg = r_work[:, 0:512].rearrange("p (k n) -> p k n", k=KD)
        g_rows = r_cu[:, 512:1024]
        y2 = r_work[:, 512:1536]
        st = r_work[:, 1536:1792]
        wp = r_work[:, 1792:2048].rearrange("p (t n) -> p t n", t=T)
        g_hot = r_work[:, 2048:2176].rearrange("p (t n) -> p t n", t=T)
        sel = r_work[:, 2176:2240]
        aT = r_work[:, 2240:2752].rearrange("p (c n) -> p c n", c=4)
        ident = cst[:, C_ID:C_ID + 128]
        tri = cst[:, C_TRI:C_TRI + 128]
        ones = cst[:, C_ONE:C_ONE + 128]
        iota = cst[:, C_IOTA:C_IOTA + CAP]
        pair_sum = cst[:, C_PAIR:C_PAIR + 2]
        thr = cst[:, C_THR:C_THR + ROUNDS - 1]

        used_small = [0]

        def piece(n):
            used_small[0] += n
            assert used_small[0] <= NSMALL
            return small[:, used_small[0] - n:used_small[0]]

        vecT = piece(NVEC)
        modT = piece(48)
        a1 = piece(KD)
        a2 = piece(KD)
        wr = piece(KD * E).rearrange("p (k n) -> p k n", k=KD)
        wra = piece(KD * E).rearrange("p (k n) -> p k n", k=KD)
        wsh = piece(E)
        brb = piece(E)
        stat = piece(8)
        padded, minus_half = piece(2), piece(2)
        neg_max = piece(4)
        sums = piece(4)
        inv = piece(4)
        nlam = piece(1)
        sub = piece(1)
        oss = piece(2)
        ors = piece(2)
        lg = [piece(E + TOPK) for _ in range(T)]
        top = piece(8 * T).rearrange("p (t n) -> p t n", t=T)
        rep = piece(8 * T).rearrange("p (t n) -> p t n", t=T)
        left = piece((E + TOPK) * T).rearrange("p (t n) -> p t n", t=T)
        mask = piece(E * T).rearrange("p (t n) -> p t n", t=T)
        ex = piece(E * T).rearrange("p (t n) -> p t n", t=T)
        comb = piece(E * T).rearrange("p (t n) -> p t n", t=T)
        posm = piece(E * T).rearrange("p (t n) -> p t n", t=T)
        ntop = piece(T)
        wsum = piece(T)
        cntm = piece(1)
        over = piece(4)
        last_f = piece(1)
        scrap = piece(3)
        junk2 = r_cu[:, 0:512]
        last_pair = at("last_pair", region(8), 1, I32)
        ps = ctx.enter_context(nc.psum_tensor("ps", [P, 8, 512], F32))

        scratch = nc.dram_tensor("bias_rows", (H, 384), F32, kind="Internal").ap()

        first_landed = [sem(f"first{n}_landed") for n in range(KD)]
        stage_landed = [sem(f"stage{n}_landed") for n in range(WIDE)]
        slot_landed = [sem(f"slot{n}_landed") for n in range(NSLOT + TWICE)]
        ada_used, up_used, down_used = sem("ada_used"), sem("up_used"), sem("down_used")
        x_landed, rows_landed, ada_b_landed = sem("x_landed"), sem("rows_landed"), sem("ada_b_landed")
        ada_rest_landed = sem("ada_rest_landed")
        bada_cleared = sem("bada_cleared")
        bias_in, bias_out, bias_back = sem("bias_in"), sem("bias_out"), sem("bias_back")
        wr_landed, late_landed, nf_landed = sem("wr_landed"), sem("late_landed"), sem("nf_landed")
        vec_turned, vec_ready = sem("vec_turned"), sem("vec_ready")
        c_ready, lam_landed, lam_exp, lam_ready, lam_out = (sem("c_ready"), sem("lam_landed"), sem("lam_exp"),
                                                          sem("lam_ready"), sem("lam_out"))
        csig_ready = sem("csig_ready")
        g_made, g_ready, flip_done, flip_read, bias_whole = (sem("g_made"), sem("g_ready"), sem("flip_done"),
                                                             sem("flip_read"), sem("bias_whole"))
        sumsq, xn_ready, x_turned = sem("sumsq"), sem("xn_ready"), sem("x_turned")
        xT_act, xT_dve = sem("xT_act"), sem("xT_dve")
        mod_ready, mod_turned, modT_ready = sem("mod_ready"), sem("mod_turned"), sem("modT_ready")
        gate_rows, gates_ready, a1_ready = sem("gate_rows"), sem("gates_ready"), sem("a1_ready")
        half_done, hi_ready, lo_ready = sem("half_done"), sem("hi_ready"), sem("lo_ready")
        h_hi_ready, h_lo_ready, conv_hi, conv_lo = sem("h_hi_ready"), sem("h_lo_ready"), sem("conv_hi"), sem("conv_lo")
        oT_hi, m_ready, m_hi, m_lo = sem("oT_hi"), sem("m_ready"), sem("m_hi"), sem("m_lo")
        bank_free = [sem("bank0_free"), sem("bank1_free")]
        scores_done, scores_read, exp_done, attn_ready = (sem("scores_done"), sem("scores_read"),
                                                          sem("exp_done"), sem("attn_ready"))
        attn_turned, pT_ready, pv_done, osq_done, o_ready, o_turned, oT_ready = (
            sem("attn_turned"), sem("pT_ready"), sem("pv_done"), sem("osq_done"), sem("o_ready"),
            sem("o_turned"), sem("oT_ready"))
        conv_ready, x1_ready, x1_sumsq = sem("conv_ready"), sem("x1_ready"), sem("x1_sumsq")
        x1T_dve = sem("x1T_dve")
        x1_turned, x1T_ready, bias_r_done, bias_r_ready, wra_ready = (
            sem("x1_turned"), sem("x1T_ready"), sem("bias_r_done"), sem("bias_r_ready"),
            sem("wra_ready"))
        logits_done, lg_ready, ex_ready, mask_ready, pos_done, comb_ready, routed = (
            sem("logits_done"), sem("lg_ready"), sem("ex_ready"), sem("mask_ready"), sem("pos_done"),
            sem("comb_ready"), sem("routed"))
        comb_turned, acc_started, last_scatter = sem("comb_turned"), sem("acc_started"), sem("last_scatter")
        last_rows = sem("last_rows")
        zeroed, kv_dead = sem("zeroed"), sem("kv_dead")
        gathered, gathered_read = sem("gathered"), sem("gathered_read")
        hot_ready, sel_ready, gather_done, xg_ready = (sem("hot_ready"), sem("sel_ready"), sem("gather_done"),
                                                       sem("xg_ready"))
        gu_free, glu_ready, sig_ready, act_ready = (sem("gu_free"), sem("glu_ready"),
                                                             sem("sig_ready"), sem("act_ready"))
        act_turned, aT_ready, y_ready = sem("act_turned"), sem("aT_ready"), sem("y_ready")
        wp_ready, wp_turned, st_ready, scatter_done, acc_ready = (sem("wp_ready"), sem("wp_turned"),
                                                                  sem("st_ready"), sem("scatter_done"),
                                                                  sem("acc_ready"))
        fin_ready, fin_sumsq, y_out, stored = sem("fin_ready"), sem("fin_sumsq"), sem("y_out"), sem("stored")
        r_x_ready, r_o_ready, r_x1_ready, r_fin_ready = (
            sem("r_x_ready"), sem("r_o_ready"), sem("r_x1_ready"), sem("r_fin_ready"))
        dve_step, act_step, pool_step = sem("dve_step"), sem("act_step"), sem("pool_step")

        def slot(j, parity):
            return NSLOT + j if j < TWICE and parity else j

        def wait_slot(eng, j, m, parity):
            eng.wait_ge(slot_landed[slot(j, parity)], 16 * m + 16 if j < TWICE else 16 * (2 * m + parity) + 16)

        def front_chunk(n):
            return stage[BUFFER[n]], stage_landed[BUFFER[n]], 16 * USES[n]

        def wait_chunk(eng, what):
            _, landed, value = front_chunk(STREAM.index(what))
            eng.wait_ge(landed, value)

        def wait_front_used(eng, what):
            if what[0] == "ada":
                eng.wait_ge(ada_used, KD * what[1] + what[2] + 1)
            else:
                eng.wait_ge(lo_ready, what[1] + 1)

        def wait_product(eng, p, h):
            eng.wait_ge(half_done, 2 * LAST_CHUNK[p] + h + 1)

        def panel_bank(p, h):
            return 2 * p + h if p in (Q0, K0, V0) else h

        def wait_evacuated(eng, p, h):
            eng.wait_ge(bank_free[h], p + 1)

        win = w_in[0].rearrange("(k p) n -> p k n", p=P)
        x_dram = x[0].rearrange("(t p) n -> t p n", p=P)
        out_dram = out[0].rearrange("(t p) n -> t p n", p=P)

        def front_source(what):
            if what[0] == "ada":
                _, b, k = what
                return w_ada[0, P * k:P * k + P, SLOT * b:SLOT * b + SLOT]
            p, j = CHUNKS[what[1]]
            if p in PANEL_COL:
                w, col = win, PANEL_COL[p]
            else:
                w = {OC0: w_out_conv, OC1: w_out_conv, WO0: w_o_attn, WO1: w_o_attn, MG0: w_merge, MG1: w_merge}[p]
                w, col = w[0].rearrange("(k p) n -> p k n", p=P), 512 * (p in (OC1, WO1, MG1))
            return w[:, 4 * j:4 * j + 4, col:col + 512]

        block = ctx.enter_context(nc.Block())

        @block.sync
        def _(sp):
            def load_slot(j, e, parity):
                n = slot(j, parity)
                if j < UP_SLOTS:
                    sp.dma_start(expert[n][:, :], w_gate_up[0, e, P * j:P * j + P, :]).then_inc(slot_landed[n], 16)
                else:
                    d = (j - UP_SLOTS) * 2 * P
                    src = w_down[0, e, d:d + 2 * P, :].rearrange("(k p) n -> p k n", p=P)
                    sp.dma_start(expert[n][:, :].rearrange("p (k n) -> p k n", k=2), src).then_inc(slot_landed[n], 16)

            for t in range(T):
                sp.dma_start(x_sb[:, t, :], x_dram[t]).then_inc(x_landed, 16)
            sp.dma_start(cst[:, :], consts[:, 0:C_FLIP]).then_inc(rows_landed, 16)

            def ada_half(half):
                for c in range(4):
                    n = 4 * half + c
                    if n >= 5:
                        sp.wait_ge(ada_used, n - 4)
                    for j in range(2):
                        row = P * (2 * c + j)
                        src = w_ada[0, row:row + P, 0:SLOT].rearrange("p (g h n) -> p g h n", g=2, h=2)[:, :, half, :]
                        dst = ada_first[n][:, 1024 * j:1024 * j + 1024].rearrange("p (g n) -> p g n", g=2)
                        sp.dma_start(dst, src).then_inc(first_landed[n], 16)
                    if n == 0:
                        for i, v in enumerate((lambda_q1, lambda_k1, lambda_q2, lambda_k2)):
                            sp.dma_start(lam_rows[:, i, :], v).then_inc(lam_landed, 16)
                        sp.dma_start(table, rel_bias_table).then_inc(bias_in, 16)
                        sp.dma_start(hot, buckets).then_inc(bias_in, 16)
                        sp.dma_start(flip, consts[:, C_FLIP:C_FLIP + 128]).then_inc(bias_in, 16)
                    if n == 1:
                        sp.wait_ge(bada_cleared, 1)
                        for g in range(2):
                            sp.dma_start(bada[32 * g:32 * g + 32, 0:2, :],
                                         dap(b_ada, 1024 * g, [[0, 32], [512, 2], [1, 512]])).then_inc(ada_b_landed, 16)

            ada_half(0)
            for n, what in enumerate(STREAM):
                if what == ("w", 3):
                    ada_half(1)
                buf, landed, _ = front_chunk(n)
                if BEFORE[n] is not None:
                    wait_front_used(sp, STREAM[BEFORE[n]])
                dst = buf[:, :] if what[0] == "ada" else buf[:, :].rearrange("p (k n) -> p k n", k=4)
                sp.dma_start(dst, front_source(what)).then_inc(landed, 16)
                early = EARLY.get(what[1]) if what[0] == "w" else None
                if early == 0:
                    sp.wait_ge(x_turned, 1)
                elif early == 1:
                    sp.wait_ge(h_hi_ready, 2)
                    sp.wait_ge(h_lo_ready, 2)
                elif early == 2:
                    sp.wait_ge(scores_read, H)
                elif early == 3:
                    sp.wait_ge(conv_lo, 1)
                elif early == 4:
                    wait_product(sp, OC1, 1)
                elif early == 5:
                    wait_evacuated(sp, OC1, 1)
                if early is not None:
                    load_slot(early, 0, 0)

            for j in range(len(EARLY), NSLOT + TWICE):
                if j < 8:
                    wait_product(sp, WO1, 1)
                elif j < 9:
                    sp.wait_ge(m_ready, 4)
                elif j < 9 + STAGE:
                    sp.wait_ge(lo_ready, STAGE_LAST[j - 9] + 1)
                elif j < 11 + STAGE:
                    sp.wait_ge(half_done, 2 * (len(CHUNKS) - 1))
                else:
                    wait_product(sp, MG1, 1)
                load_slot(j % NSLOT, j // NSLOT, j // NSLOT)
            sp.wait_ge(routed, 1)
            final = sp.value_load(last_pair[0:1, 0:1], min_val=E // 2 - 1, max_val=ROUNDS * E // 2 - 1)

            def rest_of_next(i, parity):
                for j in range(TWICE, NSLOT):
                    if j < UP_SLOTS:
                        sp.wait_ge(up_used, UP_SLOTS * i + (j + 1))
                    else:
                        sp.wait_ge(down_used, 4 * i + (j - UP_SLOTS + 1))
                    load_slot(j, (i + 1) % E, 1 - parity)

            def first_of_second(i, parity):
                for j in range(TWICE):
                    sp.wait_ge(up_used, UP_SLOTS * i + (j + 1))
                    load_slot(j, (i + 2) % E, parity)

            with sp.Fori(0, CATCH_UP) as m:
                for p in range(2):
                    first_of_second(2 * m + p, p)
                    rest_of_next(2 * m + p, p)
            with sp.Fori(CATCH_UP, final) as m:
                for p in range(2):
                    rest_of_next(2 * m + p, p)
                    first_of_second(2 * m + p, p)
            rest_of_next(2 * final, 0)
            for n in range(2 * T):
                t, cols = n // 2, slice(512 * (n % 2), 512 * (n % 2) + 512)
                sp.wait_ge(y_out, n + 1)
                sp.dma_start(out_dram[t, :, cols], acc[:, t, cols]).then_inc(stored, 16)
            sp.wait_ge(stored, 16 * 2 * T)

        @block.gpsimd
        def _(pool):
            own = Steps(pool, pool_step)

            def root(dst, src, n, t=0):
                w = slice(t, t + src.shape[1])
                own.done(nc.gpsimd.tensor_scalar(padded[:, w], src, 1.0 / n, EPS, ALU.mult, ALU.add))
                own.wait()
                return nc.gpsimd.tensor_tensor(dst, padded[:, w], minus_half[:, w], ALU.pow)

            def root_of_halves(t):
                own.done(nc.gpsimd.tensor_tensor(stat[:, 4 + t:5 + t], stat[:, 4 + t:5 + t], stat[:, 6 + t:7 + t],
                                                 ALU.add))
                own.wait()
                return root(stat[:, 2 + t:3 + t], stat[:, 4 + t:5 + t], D, t)

            nc.gpsimd.memset(r_bada[:, 0:1024], 0.0).then_inc(bada_cleared, 1)
            own.done(nc.gpsimd.memset(minus_half, -0.5))

            pool.wait_ge(sumsq, 2)
            root(stat[:, 2:4], stat[:, 0:2], D).then_inc(r_x_ready, 1)
            pool.wait_ge(flip_read, 4)
            nc.gpsimd.affine_select(out=bias_t, in_=bias_t, compare_op=ALU.is_ge, fill=MASKED, base=P,
                                    pattern=[[0, H], [-1, S]], channel_multiplier=1).then_inc(bias_whole, 1)
            for h in range(H):
                pool.wait_ge(osq_done, h + 1)
                if h >= 1:
                    pool.wait_ge(o_ready, h)
                root(ors, oss, VD).then_inc(r_o_ready, 1)
            pool.wait_ge(scores_done, H)
            pool.wait_ge(o_turned, H)
            nc.gpsimd.memset(bgu, 0.0).then_inc(kv_dead, 1)
            pool.wait_ge(pT_ready, H)
            pool.wait_ge(o_ready, H)
            nc.gpsimd.memset(y2, 0.0).then_inc(zeroed, 1)
            nc.gpsimd.memset(st, 0.0).then_inc(zeroed, 1)
            for t in range(T):
                pool.wait_ge(x1_sumsq, T + t + 1)
                root_of_halves(t).then_inc(r_x1_ready, 1)
            pool.wait_ge(m_lo, 4)
            for t in range(T):
                nc.gpsimd.tensor_copy(acc[:, t, :], x_sb[:, t, :]).then_inc(acc_started, 1)
            for t in range(T):
                pool.wait_ge(fin_sumsq, 2 * t + 2)
                root_of_halves(t).then_inc(r_fin_ready, 1)

        @block.tensor
        def _(pe):
            pe.wait_ge(rows_landed, 16 * 7)
            pe.transpose(ps[:, 7, 0:NVEC], rows, ident[0:NVEC, 0:NVEC]).then_inc(vec_turned, 1)
            pe.wait_ge(bias_in, 48)
            pe.matmul(ps[0:H, 6, 0:384], table, hot, start=True, stop=True).then_inc(g_made, 1)
            for t in range(T):
                pe.wait_ge(xn_ready, t + 1)
                for k in range(KD):
                    m = pe.transpose(ps[:, 2 + k // 2, (k % 2) * S + t * P:(k % 2) * S + t * P + P],
                                     xn[:, t, k * P:k * P + P], ident)
            m.then_inc(x_turned, 1)
            pe.wait_ge(lam_out, 1)
            pe.wait_ge(vec_ready, 1)
            pe.matmul(ps[:, 7, 0:1], ones[0:1, :], lam_s[:, 4:5], start=True, stop=True).then_inc(lam_ready, 1)

            def ada_chunk(b, k):
                if k == 0:
                    pe.wait_ge(mod_ready, b + 1)
                wait_chunk(pe, ("ada", b, k))
                buf = front_chunk(STREAM.index(("ada", b, k)))[0]
                for g in range(4):
                    m = pe.matmul(ps[32 * g:32 * g + 32, 6, :], cs32[:, k, :], buf[:, 512 * g:512 * g + 512],
                                  start=(k == 0), stop=(k == KD - 1))
                m.then_inc(ada_used, 1)

            def ada_first_chunk(half, c):
                if c == 0 and half == 0:
                    pe.wait_ge(c_ready, 1)
                    pe.wait_ge(g_ready, 1)
                elif c == 0:
                    pe.wait_ge(mod_ready, 1)
                pe.wait_ge(first_landed[4 * half + c], 32)
                for r in range(4):
                    m = pe.matmul(ps[32 * r:32 * r + 32, 6, :], cs32[:, 2 * c + r // 2, :],
                                  ada_first[4 * half + c][:, 512 * r:512 * r + 512], start=(c == 0), stop=(c == 3))
                m.then_inc(ada_used, 1)

            def mod_turn(b):
                for j in range(4):
                    row = mod[b][:, j * P:j * P + P]
                    if b < 2:
                        m = pe.matmul(ps[:, 7, 2 * j:2 * j + 2], row, pair_sum, start=True, stop=True)
                    else:
                        m = pe.transpose(ps[:, 7, j * P:j * P + P], row, ident)
                m.then_inc(mod_turned, 1)

            for c in range(4):
                ada_first_chunk(0, c)
            pe.wait_ge(mod_ready, 1)
            pe.wait_ge(lam_ready, 2)
            mod_turn(0)

            def product(n):
                p, j = CHUNKS[n]
                if p in PANEL_COL:
                    hi, lo = x_hi, x_lo
                    pe.wait_ge(h_lo_ready, 1 if n < 3 else 2)
                elif p in (OC0, OC1):
                    hi, lo = b_hi, b_lo
                    pe.wait_ge(conv_lo, 1)
                elif p in (WO0, WO1):
                    hi, lo = o_hi, o_lo
                    pe.wait_ge(oT_ready, H)
                else:
                    hi, lo = x_hi, x_lo
                    pe.wait_ge(m_lo, 2 * j + 2)
                pe.wait_ge(lo_ready, n + 1)
                wh, wl = w_hi[n % 2], w_lo[n % 2]
                ends = n == LAST_CHUNK[p]
                for h in range(2):
                    bank = panel_bank(p, h)
                    if n in (1, 2):
                        pe.wait_ge(xT_act, 2)
                        pe.wait_ge(xT_dve, 2)
                    elif j == 0 and p > Q0:
                        wait_evacuated(pe, Q0 if p == Q1 else p - 1, h)
                    if n == 2 and h == 1:
                        pe.wait_ge(mod_ready, 2)
                        pe.wait_ge(modT_ready, 1)
                        mod_turn(1)
                    if p in (V0, V1, MG0, MG1):
                        toks = slice(h * P, h * P + P)
                        parts = [(ps[:, bank, :], x_part[:, 4 * j + k, toks], w_part[:, k, :])
                                 for k in range(4) for x_part, w_part in ((hi, wh), (hi, wl), (lo, wh))]
                        groups = [parts]
                    else:
                        groups = []
                        for blk in range(2):
                            col = (2 * h + blk) * P
                            groups.append([(ps[:, bank, blk * S:blk * S + S], w_part[:, k, col:col + P],
                                            x_part[:, 4 * j + k, :])
                                           for k in range(4) for w_part, x_part in ((wh, hi), (wh, lo), (wl, hi))])
                    for group in groups:
                        for i, (out_ap, lhs, rhs) in enumerate(group):
                            first = group is groups[0] and j == 0 and i == 0
                            last = group is groups[-1] and ends and i == len(group) - 1
                            m = pe.matmul(out_ap, lhs, rhs, start=first, stop=last, skip_group_check=True)
                    m.then_inc(half_done, 1)

            def attention(n):
                if n < H:
                    half = n // 4
                    for p in (Q0, K0) if half == 0 else (Q1, K1):
                        for h in range(2):
                            wait_evacuated(pe, p, h)
                    if n > 0:
                        pe.wait_ge(scores_read, n)
                    else:
                        pe.wait_ge(flip_read, 4)
                    for m in range(2):
                        q, k = qT[HD * m:HD * m + HD, n, :], kT[HD * m:HD * m + HD, n, :]
                        pe.matmul(ps[:, 2 + m, 0:P], q[:, 0:P], k[:, 0:P], start=True, stop=True)
                        mm = pe.matmul(ps[:, 2 + m, P:P + S], q[:, P:S], k, start=True, stop=True)
                    mm.then_inc(scores_done, 1)
                if 1 <= n <= H:
                    pe.wait_ge(attn_ready, n)
                    if n >= 2:
                        pe.wait_ge(pT_ready, n - 1)
                    for j in range(3):
                        mm = pe.transpose(ps[:, 4, j * P:j * P + P], attn[:, j * P:j * P + P], ident)
                    mm.then_inc(attn_turned, 1)
                if 2 <= n <= H + 1:
                    h = n - 2
                    pe.wait_ge(pT_ready, h + 1)
                    if h >= 1:
                        pe.wait_ge(o_ready, h)
                    for hh in range(2):
                        wait_evacuated(pe, V0 if h < 4 else V1, hh)
                    cols = slice(h * VD, h * VD + VD)
                    pe.matmul(ps[:, 5, 0:P], pT[:, 0:P], v_sb[:, 0, cols], start=True, stop=True)
                    pe.matmul(ps[:, 5, P:S], pT[:, P:S], v_sb[:, 0, cols], start=True, stop=False)
                    pe.matmul(ps[:, 5, P:S], pT[:, S:S + P], v_sb[:, 1, cols], start=False,
                              stop=True).then_inc(pv_done, 1)
                if 3 <= n <= H + 2:
                    h = n - 3
                    pe.wait_ge(o_ready, h + 1)
                    if h >= 1:
                        pe.wait_ge(oT_ready, h)
                    for t in range(T):
                        mm = pe.transpose(ps[:, 7, t * P:t * P + P], o_n[:, t, :], ident)
                    mm.then_inc(o_turned, 1)

            def mod_step(n):
                if n < 2:
                    pe.wait_ge(mod_ready, n + 3)
                    pe.wait_ge(oT_ready, H)
                    pe.wait_ge(modT_ready, n + 2)
                    mod_turn(n + 2)
                    return
                b, g = (2, 0) if n == 2 else (3, 2)
                pe.wait_ge(mod_ready, 4)
                if n == 2:
                    pe.wait_ge(modT_ready, 4)
                else:
                    pe.wait_ge(gates_ready, 1)
                for half in range(2):
                    r = 32 * (g + half)
                    mm = pe.matmul(ps[:, 6 + half, :], ones[r:r + 1, :], mod[b][r:r + 1, :], start=True, stop=True)
                mm.then_inc(gate_rows, 1)

            def turn_x1(half, t):
                pe.wait_ge(x1_ready, 2 * half + t + 1)
                for k in range(4):
                    mm = pe.transpose(ps[:, 2 + 2 * t + half, k * P:k * P + P],
                                      x_sb[:, t, 512 * half + k * P:512 * half + k * P + P], ident)
                mm.then_inc(x1_turned, 1)

            def route(half, t):
                if half and t:
                    pe.wait_ge(x1T_dve, 1)
                else:
                    pe.wait_ge(x1T_ready, 2 * half + t + 1)
                for k in range(4 * half, 4 * half + 4):
                    mm = pe.matmul(ps[:, 6 + t, 0:E], x1T[:, k, t * P:t * P + P], wra[:, k, :],
                                   start=(k == 0), stop=(k == KD - 1))
                if half:
                    mm.then_inc(logits_done, 1)

            for n in range(len(CHUNKS)):
                what = STREAM.index(("w", n)) + 1
                if what < len(STREAM) and STREAM[what][0] == "ada":
                    ada_chunk(*STREAM[what][1:])
                if n in (1, 2):
                    ada_first_chunk(1, 2 * n - 2)
                    ada_first_chunk(1, 2 * n - 1)
                product(n)
                if n == FLIP_AFTER:
                    wait_evacuated(pe, V0, 0)
                    wait_evacuated(pe, V0, 1)
                    pe.wait_ge(bias_back, 16)
                    for b in range(4):
                        pe.matmul(ps[:, 2 + b, :], flip, hankel[:, 2 * b:2 * b + 2, :], start=True,
                                  stop=True).then_inc(flip_done, 1)
                for kind, step in AFTER.get(n, []):
                    if kind == "att":
                        attention(step)
                    else:
                        mod_step(step)
                if n == ROUTER_BIAS:
                    pe.wait_ge(wra_ready, 1)
                    pe.wait_ge(gates_ready, 2)
                    pe.matmul(ps[:, 7, 0:E], ones, wsh, start=True, stop=True).then_inc(bias_r_done, 1)
                if n == LAST_CHUNK[MG1] - 1:
                    for t in range(T):
                        turn_x1(0, t)
            pe.wait_ge(bias_r_ready, 1)
            for t in range(T):
                route(0, t)

            for t in range(T):
                turn_x1(1, t)
            for t in range(T):
                route(1, t)

            def gate_up_bias(i):
                pe.wait_ge(gu_free, i + 1)
                pe.wait_ge(sel_ready, i + 1)
                for j in range(2):
                    for g in range(2):
                        col = 1024 * g + 512 * j
                        pe.matmul(ps[CAP * g:CAP * g + CAP, j, :], sel, bgu[:, col:col + 512],
                                  start=True, stop=False)

            pe.wait_ge(late_landed, 32)
            gate_up_bias(0)
            pe.wait_ge(mask_ready, 2)
            pe.matmul(ps[:, 2, 0:E], tri, mask[:, 0, :], start=True, stop=True)
            pe.matmul(ps[:, 2, E:2 * E], ones, mask[:, 0, :], start=True, stop=False)
            pe.matmul(ps[:, 2, E:2 * E], tri, mask[:, 1, :], start=False, stop=True).then_inc(pos_done, 1)
            pe.matmul(ps[:, 3, 0:E], ones, mask[:, 0, :], start=True, stop=False)
            pe.matmul(ps[:, 3, 0:E], ones, mask[:, 1, :], start=False, stop=True).then_inc(pos_done, 1)

            def gather():
                for t in range(T):
                    for half in range(2):
                        mm = pe.matmul(ps[CAP * half:CAP * half + CAP, 2, :], g_hot[:, t, :],
                                       x_sb[:, t, 512 * half:512 * half + 512], start=(t == 0), stop=(t == T - 1))
                mm.then_inc(gathered, 1)

            def turn_gathered(i):
                pe.wait_ge(gathered_read, i + 1)
                for q in range(4):
                    mm = pe.transpose(ps[:, 2, q * P:q * P + P], g_rows[:, q * P:q * P + P], ident)
                mm.then_inc(gather_done, 1)

            pe.wait_ge(hot_ready, 1)
            gather()
            turn_gathered(0)
            pe.wait_ge(comb_ready, 2)
            for t in range(T):
                mm = pe.transpose(ps[0:E, 7, t * P:t * P + P], comb[:, t, :], ident)
            mm.then_inc(comb_turned, 1)

            def scatter(m):
                pe.wait_ge(st_ready, m + 1)
                pe.wait_ge(y_ready, 2 * m + 1)
                pe.wait_ge(acc_ready, m + 1)
                for t in range(T):
                    for half in range(2):
                        mm = pe.matmul(ps[:, 4 + 2 * t + half, :], st[:, t * P:t * P + P],
                                       y2[:, 512 * half:512 * half + 512], start=True, stop=True)
                    mm.then_inc(scatter_done, 1)

            pe.wait_ge(routed, 1)
            final = pe.value_load(last_pair[0:1, 0:1], min_val=E // 2 - 1, max_val=ROUNDS * E // 2 - 1)

            def pair(m, last):
                for p in range(2):
                    i = 2 * m + p
                    if p == 1:
                        pe.wait_ge(wp_ready, i + 1)
                        pe.wait_ge(acc_ready, m + 2)
                        for t in range(T):
                            mm = pe.transpose(ps[:, 7, t * P:t * P + P], wp[:, t, :], ident)
                        mm.then_inc(wp_turned, 1)
                    pe.wait_ge(xg_ready, 2 * i + 1)
                    for k in range(KD):
                        if k == 2:
                            pe.wait_ge(xg_ready, 2 * i + 2)
                        wait_slot(pe, k, m, p)
                        buf = expert[slot(k, p)]
                        for j in range(2):
                            for g in range(2):
                                col = 1024 * g + 512 * j
                                mm = pe.matmul(ps[CAP * g:CAP * g + CAP, j, :], xg[:, 2 * (k % 4) + k // 4, :],
                                               buf[:, col:col + 512], start=False, stop=(k == KD - 1))
                        mm.then_inc(up_used, 1)
                    if p == 0:
                        scatter(m)
                    if last and p == 1:
                        pe.wait_ge(st_ready, m + 2)
                        pe.wait_ge(y_ready, i + 1)
                        for half, t, bank in LAST_PARTS:
                            pe.matmul(ps[:, bank, :], st[0:CAP, t * P:t * P + P],
                                      y2[0:CAP, 512 * half:512 * half + 512], start=True, stop=False)
                    else:
                        pe.wait_ge(hot_ready, i + 2)
                        gather()
                        gate_up_bias(i + 1)
                    pe.wait_ge(act_ready, i + 1)
                    for q in range(4):
                        mm = pe.transpose(ps[:, 3, q * P:q * P + P], act_sb[:, q * P:q * P + P], ident)
                    mm.then_inc(act_turned, 1)
                    if not (last and p == 1):
                        turn_gathered(i + 1)
                    pe.wait_ge(aT_ready, i + 1)
                    if p == 0:
                        pe.wait_ge(acc_ready, m + 2)
                    else:
                        pe.wait_ge(y_ready, i + 1)
                    for q in range(F // P):
                        n = UP_SLOTS + q // 2
                        g, ch = q // 4, q % 4
                        if q % 2 == 0:
                            wait_slot(pe, n, m, p)
                        for half in range(2):
                            mm = pe.matmul(ps[CAP * half:CAP * half + CAP, 6, :], aT[:, ch, CAP * g:CAP * g + CAP],
                                           expert[n][:, 1024 * (q % 2) + 512 * half:1024 * (q % 2) + 512 * half + 512],
                                           start=(q == 0), stop=(q == F // P - 1))
                        if q % 2 == 1:
                            mm.then_inc(down_used, 1)

            with pe.Fori(0, final) as m:
                pair(m, False)
            pair(final, True)
            for n, (half, t, bank) in enumerate(LAST_PARTS):
                pe.wait_ge(last_rows, half + 1)
                pe.matmul(ps[:, bank, :], st[CAP:P, t * P:t * P + P],
                          y2[CAP:P, 512 * half:512 * half + 512], start=False, stop=True).then_inc(last_scatter, 1)

        @block.scalar
        def _(act):
            own = Steps(act, act_step)
            act.dma_start(rows[V_C:V_C + KD, :], c[0].rearrange("(k n) -> k n", n=P)).then_inc(rows_landed, 16)
            act.dma_start(rows[V_G1:V_G1 + KD, :], norm1_g[0].rearrange("(k n) -> k n", n=P)).then_inc(rows_landed, 16)
            act.dma_start(rows[V_G2:V_G2 + KD, :], norm2_g[0].rearrange("(k n) -> k n", n=P)).then_inc(rows_landed, 16)
            act.dma_start(rows[V_CB:V_CB + KC, :], conv_b[0].rearrange("(k n) -> k n", n=P)).then_inc(rows_landed, 16)
            act.dma_start(rows[V_CW:V_CW + 3 * KC, :],
                          conv_w[0].rearrange("j (k n) -> (j k) n", n=P)).then_inc(rows_landed, 16)
            act.dma_start(rows[V_SUB:V_SUB + 1, :], subln_g).then_inc(rows_landed, 16)

            for t in range(T):
                act.wait_ge(x_landed, 16 * T)
                act.activation(xn[:, t, :], x_sb[:, t, :], ACT.Square, accum_out=stat[:, t:t + 1]).then_inc(sumsq, 1)
            act.wait_ge(vec_ready, 1)
            act.activation(csig, vecT[:, V_C:V_C + KD], ACT.Sigmoid).then_inc(csig_ready, 1)
            act.wait_ge(lam_exp, 1)
            act.activation(lam_s[:, 2:4], lam_s[:, 0:2], ACT.Exp).then_inc(lam_exp, 1)
            act.wait_ge(g_ready, 1)
            act.dma_start(scratch, g_sb).then_inc(bias_out, 16)
            act.wait_ge(x_turned, 1)
            for b in (1, 3):
                act.activation(hT[:, 2 * b:2 * b + 2, :], ps[:, 2 + b, :].rearrange("p (k n) -> p k n", k=2),
                               ACT.Copy).then_inc(xT_act, 1)

            def h_parts(half):
                act.wait_ge(a1_ready, half + 1)
                act.wait_ge(xT_act, 2)
                act.wait_ge(xT_dve, 2)
                for k in range(4 * half, 4 * half + 4):
                    ins = act.activation(x_hi[:, k, :], hT[:, k, :], ACT.Identity, scale=a1[:, k:k + 1],
                                         bias=modT[:, M_SH1 + k:M_SH1 + k + 1])
                ins.then_inc(h_hi_ready, 1)

            def split(n):
                wait_chunk(act, ("w", n))
                if n >= 2:
                    act.wait_ge(half_done, 2 * (n - 2) + 2)
                src = front_chunk(STREAM.index(("w", n)))[0][:, :].rearrange("p (k n) -> p k n", k=4)
                act.activation(w_hi[n % 2], src, ACT.Copy).then_inc(hi_ready, 1)

            def evacuate(p, h):
                src = ps[:, panel_bank(p, h), :]
                pair = src.rearrange("p (b n) -> p b n", b=2)
                if p == CU or p > GB1:
                    return
                wait_product(act, p, h)
                if p in (Q0, Q1):
                    first = 4 * (p == Q1) + 2 * h
                    ins = act.activation(qT[:, first:first + 2, :], pair, ACT.Copy, scale=HD ** -0.5)
                elif p in (K0, K1):
                    first = 4 * (p == K1) + 2 * h
                    ins = act.activation(kT[:, first:first + 2, :], pair, ACT.Copy)
                elif p in (V0, V1):
                    first = 512 * (p == V1)
                    ins = act.activation(v_sb[:, h, first:first + 512], src, ACT.Copy)
                elif p == CB:
                    ins = act.activation(bT[:, 2 * h:2 * h + 2, :], pair, ACT.Copy)
                elif p == CC:
                    ins = act.activation(cT[:, 2 * h:2 * h + 2, :], pair, ACT.Copy)
                else:
                    gate = ga if p in (GA0, GA1) else gb
                    first = 4 * (p in (GA1, GB1)) + 2 * h
                    ins = act.activation(gate[:, first:first + 2, :], pair, ACT.Sigmoid)
                ins.then_inc(bank_free[h], 1)

            def attention(n):
                if n < H:
                    act.wait_ge(scores_read, n + 1)
                    for s in range(4):
                        b, m = s // 2, s % 2
                        seg = logit[:, m, 0:P] if b == 0 else logit[:, m, P:P + S]
                        ins = act.activation(seg, seg, ACT.Exp, bias=neg_max[:, s:s + 1],
                                             accum_out=sums[:, s:s + 1])
                    ins.then_inc(exp_done, 1)
                if 1 <= n <= H:
                    act.wait_ge(attn_turned, n)
                    if n >= 2:
                        act.wait_ge(pv_done, n - 1)
                    act.activation(pT, ps[:, 4, 0:384], ACT.Copy).then_inc(pT_ready, 1)
                if 2 <= n <= H + 1:
                    act.wait_ge(pv_done, n - 1)
                    for t in range(T):
                        ins = own.done(act.activation(junk[:, 0:P], ps[:, 5, t * P:t * P + P], ACT.Square,
                                                      accum_out=oss[:, t:t + 1]))
                        own.wait()
                    act.activation(junk[:, P:P + 1], junk[:, 0:1], ACT.Copy).then_inc(osq_done, 1)
                if 3 <= n <= H + 2:
                    act.wait_ge(o_turned, n - 2)
                    act.activation(o_hi[:, n - 3, :], ps[:, 7, 0:S], ACT.Copy, scale=sub[:, 0:1]).then_inc(oT_hi, 1)

            split(0)
            h_parts(0)
            act.wait_ge(bias_out, 16)
            act.wait_ge(ada_used, 4)
            act.dma_start(hankel, dap(scratch, 0, [[1, P], [384, H], [1, S]])).then_inc(bias_back, 16)
            split(1)
            for g in range(4):
                act.dma_start(bada[32 * g:32 * g + 32, 2:4, :],
                              dap(b_ada, SLOT + 512 * g, [[0, 32], [SLOT, 2], [1, 512]])).then_inc(ada_rest_landed, 16)
            act.dma_start(wr, w_router[0].rearrange("(k p) n -> p k n", p=P)).then_inc(wr_landed, 16)
            act.dma_start(brb, dap(b_router, 0, [[0, P], [1, E]])).then_inc(wr_landed, 16)
            for n, (p, j) in enumerate(CHUNKS):
                if n == LAST_CHUNK[p]:
                    for h in range(2):
                        evacuate(p, h)
                if n + 2 < len(CHUNKS):
                    split(n + 2)
                if n == 1:
                    h_parts(1)
                if n == FLIP_AFTER:
                    for b in range(4):
                        act.wait_ge(flip_done, b + 1)
                        act.activation(bias_t[:, 2 * b:2 * b + 2, :],
                                       ps[:, 2 + b, :].rearrange("p (h n) -> p h n", h=2),
                                       ACT.Copy).then_inc(flip_read, 1)
                for kind, step in AFTER.get(n, []):
                    if kind == "att":
                        attention(step)
                if n == CONV_HI:
                    act.wait_ge(conv_ready, 1)
                    act.wait_ge(gates_ready, 2)
                    act.activation(b_hi, bT, ACT.Copy).then_inc(conv_hi, 1)
                if n == LAST_CHUNK[CU]:
                    act.wait_ge(kv_dead, 1)
                    act.dma_start(bgu[0:E, :], b_gate_up[0]).then_inc(late_landed, 16)
                    act.wait_ge(zeroed, 2)
                    act.dma_start(y2[0:E, :], b_down[0]).then_inc(late_landed, 16)
                if p in (WO0, WO1) and n == LAST_CHUNK[p]:
                    for q in (2 * (p == WO1), 2 * (p == WO1) + 1):
                        act.wait_ge(m_ready, q + 1)
                        act.activation(x_hi[:, 2 * q:2 * q + 2, :], mT[:, 2 * q:2 * q + 2, :],
                                       ACT.Copy).then_inc(m_hi, 1)
            act.activation(scrap[:, 0:1], ones[:, 0:1], ACT.Exp)
            for half in range(2):
                for t in range(T):
                    act.wait_ge(x1_ready, 2 * half + t + 1)
                    if half or t:
                        act.wait_ge(x1_sumsq, 2 * half + t)
                    act.activation(junk2, x_sb[:, t, 512 * half:512 * half + 512], ACT.Square,
                                   accum_out=stat[:, 4 + 2 * half + t:5 + 2 * half + t]).then_inc(x1_sumsq, 1)
                    if not (half and t):
                        act.wait_ge(x1_turned, 2 * half + t + 1)
                        act.activation(x1T[:, 4 * half:4 * half + 4, t * P:t * P + P],
                                       ps[:, 2 + 2 * t + half, :].rearrange("p (k n) -> p k n", k=4),
                                       ACT.Copy).then_inc(x1T_ready, 1)
            for t in range(T):
                act.wait_ge(lg_ready, 1)
                act.activation(ex[:, t, :], lg[t][:, 0:E], ACT.Exp, bias=ntop[:, t:t + 1]).then_inc(ex_ready, 1)

            def read_gathered(i):
                act.wait_ge(gathered, i + 1)
                act.activation(g_rows, ps[:, 2, :], ACT.Copy).then_inc(gathered_read, 1)

            read_gathered(0)
            act.dma_start(nfb, dap(normf_g, 0, [[0, P], [1, D]])).then_inc(nf_landed, 16)
            act.wait_ge(routed, 1)
            final = act.value_load(last_pair[0:1, 0:1], min_val=E // 2 - 1, max_val=ROUNDS * E // 2 - 1)

            def pair(m, last):
                for p in range(2):
                    i = 2 * m + p
                    act.wait_ge(glu_ready, i + 1)
                    act.activation(sig, glu, ACT.Sigmoid, scale=ALPHA).then_inc(sig_ready, 1)
                    if not (last and p == 1):
                        read_gathered(i + 1)
                    act.wait_ge(act_turned, i + 1)
                    act.activation(aT, ps[:, 3, :].rearrange("p (c n) -> p c n", c=4), ACT.Copy).then_inc(aT_ready, 1)

            with act.Fori(0, final) as m:
                pair(m, False)
            pair(final, True)
            for n, (half, t, bank) in enumerate(LAST_PARTS):
                act.wait_ge(fin_ready, n + 1)
                if n:
                    act.wait_ge(fin_sumsq, n)
                act.activation(junk2, acc[:, t, 512 * half:512 * half + 512], ACT.Square,
                               accum_out=stat[:, 4 + 2 * half + t:5 + 2 * half + t]).then_inc(fin_sumsq, 1)

        @block.vector
        def _(v):
            own = Steps(v, dve_step)

            def normalise(dst, src, r):
                return v.tensor_scalar(dst, src, r, None, ALU.mult)

            v.wait_ge(vec_turned, 1)
            v.tensor_copy(vecT, ps[:, 7, 0:NVEC]).then_inc(vec_ready, 1)
            v.wait_ge(lam_landed, 64)
            lam = lam_rows.rearrange("p (a b) n -> p a b n", b=2)
            own.done(v.tensor_tensor(lam[:, :, 0, :], lam[:, :, 0, :], lam[:, :, 1, :], ALU.mult))
            own.wait()
            v.tensor_reduce(lam_s[:, 0:2], lam[:, :, 0, :], AX, ALU.add).then_inc(lam_exp, 1)
            v.wait_ge(g_made, 1)
            v.tensor_copy(g_sb, ps[0:H, 6, 0:384]).then_inc(g_ready, 1)
            v.wait_ge(csig_ready, 1)
            own.done(v.tensor_tensor(csig, csig, vecT[:, V_C:V_C + KD], ALU.mult))
            own.wait()
            v.tensor_copy(cs32, csig.unsqueeze(2).broadcast_to([P, KD, 32])).then_inc(c_ready, 1)
            v.wait_ge(r_x_ready, 1)
            for t in range(T):
                normalise(xn[:, t, :], x_sb[:, t, :], stat[:, 2 + t:3 + t]).then_inc(xn_ready, 1)
            v.wait_ge(lam_exp, 2)
            own.done(v.tensor_tensor(lam_s[:, 4:5], lam_s[:, 3:4], lam_s[:, 2:3], ALU.subtract))
            own.wait()
            v.tensor_scalar(lam_s[:, 4:5], lam_s[:, 4:5], -LAM_INIT, None, ALU.add).then_inc(lam_out, 1)
            v.wait_ge(lam_ready, 1)
            v.tensor_copy(nlam, ps[:, 7, 0:1]).then_inc(lam_ready, 1)
            v.tensor_scalar(sub, vecT[:, V_SUB:V_SUB + 1], 1.0 - LAM_INIT, None, ALU.mult)
            v.wait_ge(x_turned, 1)
            for b in (0, 2):
                v.tensor_copy(hT[:, 2 * b:2 * b + 2, :],
                              ps[:, 2 + b, :].rearrange("p (k n) -> p k n", k=2)).then_inc(xT_dve, 1)

            def mod_rows(b):
                v.wait_ge(ada_used, 4 * (b + 1) if b < 2 else KD * b)
                v.wait_ge(ada_b_landed, 32)
                if b >= 2:
                    v.wait_ge(ada_rest_landed, 64)
                v.tensor_tensor(mod[b], ps[:, 6, :], bada[:, b, :], ALU.add).then_inc(mod_ready, 1)

            def mod_cols(b):
                v.wait_ge(mod_turned, b + 1)
                if b < 2:
                    dst = modT[:, 0:16].rearrange("p (g h j) -> p g h j", g=2, h=2)[:, :, b, :]
                    src = ps[:, 7, 0:8].rearrange("p (j g) -> p g j", g=2)
                else:
                    dst = modT[:, 16 * (b - 1):16 * b].rearrange("p (g j) -> p g j", g=4)
                    src = ps[:, 7, :].rearrange("p (j g r) -> p g j r", j=4, r=32)[:, :, :, 0]
                v.tensor_copy(dst, src).then_inc(modT_ready, 1)

            def scale1(half):
                v.wait_ge(modT_ready, half + 1)
                ks = slice(4 * half, 4 * half + 4)
                v.scalar_tensor_tensor(out=a1[:, ks], in0=modT[:, M_SC1 + 4 * half:M_SC1 + 4 * half + 4], scalar=1.0,
                                       in1=vecT[:, V_G1 + 4 * half:V_G1 + 4 * half + 4],
                                       op0=ALU.add, op1=ALU.mult).then_inc(a1_ready, 1)
                v.wait_ge(a1_ready, half + 1)

            def h_parts(half):
                v.wait_ge(xT_act, 2)
                v.wait_ge(xT_dve, 2)
                for k in range(4 * half, 4 * half + 4):
                    own.done(v.tensor_scalar(h_sb[:, k, :], hT[:, k, :], a1[:, k:k + 1],
                                             modT[:, M_SH1 + k:M_SH1 + k + 1], ALU.mult, ALU.add))
                own.wait()
                v.wait_ge(h_hi_ready, half + 1)
                ks = slice(4 * half, 4 * half + 4)
                v.tensor_tensor(x_lo[:, ks, :], h_sb[:, ks, :], x_hi[:, ks, :], ALU.subtract).then_inc(h_lo_ready, 1)

            def split(n):
                v.wait_ge(hi_ready, n + 1)
                src = front_chunk(STREAM.index(("w", n)))[0][:, :].rearrange("p (k n) -> p k n", k=4)
                v.tensor_tensor(w_lo[n % 2], src, w_hi[n % 2], ALU.subtract).then_inc(lo_ready, 1)

            def attention(n, between):
                if n < H:
                    v.wait_ge(scores_done, n + 1)
                    if n == 0:
                        v.wait_ge(bias_whole, 1)
                    else:
                        v.wait_ge(attn_ready, n)
                    own.done(v.tensor_tensor(logit[:, :, 0:P], ps[:, 2:4, 0:P],
                                             bias_t[:, n, P:S].unsqueeze(1).broadcast_to([P, 2, P]), ALU.add))
                    own.done(v.tensor_tensor(logit[:, :, P:P + S], ps[:, 2:4, P:P + S],
                                             bias_t[:, n, :].unsqueeze(1).broadcast_to([P, 2, S]), ALU.add))
                    own.wait()
                    v.tensor_reduce(neg_max[:, 0:2], logit[:, :, 0:P], AX, ALU.max, negate=True)
                    v.tensor_reduce(neg_max[:, 2:4], logit[:, :, P:P + S], AX, ALU.max,
                                    negate=True).then_inc(scores_read, 1)
                between()
                if 3 <= n <= H + 2:
                    h = n - 3
                    v.wait_ge(oT_hi, h + 1)
                    v.scalar_tensor_tensor(out=o_lo[:, h, :], in0=ps[:, 7, 0:S], scalar=sub[:, 0:1],
                                           in1=o_hi[:, h, :], op0=ALU.mult, op1=ALU.subtract).then_inc(oT_ready, 1)
                if n < H:
                    v.wait_ge(exp_done, n + 1)
                    own.done(v.reciprocal(inv, sums))
                    own.wait()
                    own.done(v.tensor_scalar(inv[:, 1:4:2], inv[:, 1:4:2], nlam, None, ALU.mult))
                    own.wait()
                    segs = (slice(0, P), slice(P, P + S))
                    for b in range(2):
                        own.done(v.tensor_scalar(logit[:, 1, segs[b]], logit[:, 1, segs[b]],
                                                 inv[:, 2 * b + 1:2 * b + 2], None, ALU.mult))
                    own.wait()
                    if n >= 1:
                        v.wait_ge(attn_turned, n)
                    for b in range(2):
                        ins = v.scalar_tensor_tensor(out=attn[:, segs[b]], in0=logit[:, 0, segs[b]],
                                                     scalar=inv[:, 2 * b:2 * b + 1], in1=logit[:, 1, segs[b]],
                                                     op0=ALU.mult, op1=ALU.add)
                    ins.then_inc(attn_ready, 1)
                if 2 <= n <= H + 1:
                    v.wait_ge(r_o_ready, n - 1)
                    if n >= 3:
                        v.wait_ge(o_turned, n - 2)
                    for t in range(T):
                        ins = normalise(o_n[:, t, :], ps[:, 5, t * P:t * P + P], ors[:, t:t + 1])
                    ins.then_inc(o_ready, 1)

            def mod_step(n):
                if n < 2:
                    mod_cols(n + 2)
                    return
                v.wait_ge(gate_rows, n - 1)
                v.tensor_copy((g1b if n == 2 else g2b).rearrange("p (b n) -> p b n", b=2),
                              ps[:, 6:8, :]).then_inc(gates_ready, 1)

            def router_weights():
                v.wait_ge(modT_ready, 4)
                own.done(v.scalar_tensor_tensor(out=a2, in0=modT[:, M_SC2:M_SC2 + KD], scalar=1.0,
                                                in1=vecT[:, V_G2:V_G2 + KD], op0=ALU.add, op1=ALU.mult))
                own.wait()
                v.wait_ge(wr_landed, 32)
                own.done(v.tensor_tensor(wra, wr, modT[:, M_SH2:M_SH2 + KD].unsqueeze(2).broadcast_to([P, KD, E]),
                                         ALU.mult))
                own.wait()
                own.done(v.tensor_reduce(wsh, wra.rearrange("p k n -> p n k"), AX, ALU.add))
                own.wait()
                v.tensor_tensor(wra, wr, a2.unsqueeze(2).broadcast_to([P, KD, E]), ALU.mult).then_inc(wra_ready, 1)

            def conv_u(h):
                if h == 0:
                    own.done(v.memset(cu[:, :, 0:2], 0.0))
                wait_product(v, CU, h)
                wait_evacuated(v, CC, 0)
                wait_evacuated(v, CC, 1)
                v.tensor_tensor(cu[:, 2 * h:2 * h + 2, 2:2 + S], ps[:, h, :].rearrange("p (b n) -> p b n", b=2),
                                cT[:, 2 * h:2 * h + 2, :], ALU.mult).then_inc(bank_free[h], 1)

            def conv_tap(j):
                wait_evacuated(v, CU, 0)
                wait_evacuated(v, CU, 1)
                own.wait()
                for k in range(KC):
                    w = vecT[:, V_CW + j * KC + k:V_CW + j * KC + k + 1]
                    tap = cu[:, k, j:j + S]
                    if j == 0:
                        own.done(v.tensor_scalar(cT[:, k, :], tap, w, vecT[:, V_CB + k:V_CB + k + 1],
                                                 ALU.mult, ALU.add))
                    else:
                        own.done(v.scalar_tensor_tensor(out=cT[:, k, :], in0=tap, scalar=w, in1=cT[:, k, :],
                                                        op0=ALU.mult, op1=ALU.add))

            def merge_a(p, h):
                q = 2 * (p == OC1) + h
                wait_product(v, p, h)
                v.tensor_tensor(mT[:, 2 * q:2 * q + 2, :], ps[:, h, :].rearrange("p (b n) -> p b n", b=2),
                                ga[:, 2 * q:2 * q + 2, :], ALU.mult).then_inc(bank_free[h], 1)

            def merge_b(p, h):
                q = 2 * (p == WO1) + h
                wait_product(v, p, h)
                g = gb[:, 2 * q:2 * q + 2, :]
                v.tensor_tensor(g, ps[:, h, :].rearrange("p (b n) -> p b n", b=2), g, ALU.mult).then_inc(bank_free[h], 1)
                wait_evacuated(v, p, h)
                v.tensor_tensor(mT[:, 2 * q:2 * q + 2, :], mT[:, 2 * q:2 * q + 2, :], g, ALU.add).then_inc(m_ready, 1)

            def merged_lo(q):
                v.wait_ge(m_hi, q + 1)
                v.tensor_tensor(x_lo[:, 2 * q:2 * q + 2, :], mT[:, 2 * q:2 * q + 2, :], x_hi[:, 2 * q:2 * q + 2, :],
                                ALU.subtract).then_inc(m_lo, 1)

            def residual(half, t):
                n, cols = 2 * half + t, slice(512 * half, 512 * half + 512)
                p = (MG0, MG1)[half]
                tmp = r_cu[:, 512:1024] if n % 2 else r_cu[:, 1032:1544]
                wait_product(v, p, t)
                v.tensor_tensor(tmp, ps[:, t, :], g1b[:, cols], ALU.mult).then_inc(bank_free[t], 1)
                wait_evacuated(v, p, t)
                v.tensor_tensor(x_sb[:, t, cols], x_sb[:, t, cols], tmp, ALU.add).then_inc(x1_ready, 1)

            mod_rows(0)
            mod_cols(0)
            scale1(0)
            split(0)
            h_parts(0)
            split(1)
            for n, (p, j) in enumerate(CHUNKS):
                if n == 1:
                    mod_rows(1)

                def split_next():
                    if n + 2 < len(CHUNKS):
                        split(n + 2)

                what = STREAM.index(("w", n))
                if STREAM[what + 1:what + 2] and STREAM[what + 1][0] == "ada" and STREAM[what + 1][2] == KD - 1:
                    mod_rows(STREAM[what + 1][1] + 1)
                ends = n == LAST_CHUNK[p]
                for h in range(2 if ends else 0):
                    if p == CU:
                        conv_u(h)
                    elif p in (OC0, OC1):
                        merge_a(p, h)
                    elif p in (WO0, WO1):
                        merge_b(p, h)
                    elif p == MG0:
                        residual(0, h)
                steps = AFTER.get(n, [])
                if not steps or steps[0][0] != "att":
                    split_next()
                if n == 1:
                    mod_cols(1)
                    scale1(1)
                    h_parts(1)
                if n == CONV_LO:
                    v.wait_ge(conv_hi, 1)
                    v.tensor_tensor(b_lo, bT, b_hi, ALU.subtract).then_inc(conv_lo, 1)
                if ends and p in (WO0, WO1):
                    for q in (2 * (p == WO1), 2 * (p == WO1) + 1):
                        merged_lo(q)
                for kind, step in steps:
                    if kind == "att":
                        attention(step, split_next)
                    else:
                        mod_step(step)
                if n in CONV_TAPS:
                    conv_tap(CONV_TAPS.index(n))
                if n == CONV_TAPS[-1]:
                    own.wait()
                    v.tensor_tensor(bT, bT, cT, ALU.mult).then_inc(conv_ready, 1)
                if n == ROUTER_WEIGHTS:
                    router_weights()
                if n == BDOWN_SCALED:
                    v.wait_ge(late_landed, 32)
                    v.wait_ge(gates_ready, 2)
                    v.tensor_tensor(y2[0:E, :], y2[0:E, :], g2b[0:E, :], ALU.mult).then_inc(y_ready, 1)
                if n == ROUTER_BIAS + 1:
                    v.wait_ge(bias_r_done, 1)
                    v.tensor_tensor(brb, brb, ps[:, 7, 0:E], ALU.add).then_inc(bias_r_ready, 1)
            for t in range(T):
                residual(1, t)
            v.wait_ge(x1_turned, 4)
            v.tensor_copy(x1T[:, 4:8, P:S], ps[:, 5, :].rearrange("p (k n) -> p k n", k=4)).then_inc(x1T_dve, 1)

            def select(e):
                src = ident[:, bass.ds(e, 1)] if not isinstance(e, int) else ident[:, e:e + 1]
                v.tensor_copy(sel, src.broadcast_to([P, CAP])).then_inc(sel_ready, 1)

            select(0)
            v.tensor_copy(scrap[:, 1:2], ones[:, 0:1]).then_inc(gu_free, 1)
            for t in range(T):
                own.done(v.memset(lg[t][:, E:E + TOPK], TAKEN))
                own.done(v.memset(rep[:, t, TOPK:8], TAKEN))
            for t in range(T):
                v.wait_ge(logits_done, t + 1)
                v.wait_ge(r_x1_ready, t + 1)
                own.done(v.scalar_tensor_tensor(out=lg[t][:, 0:E], in0=ps[:, 6 + t, 0:E], scalar=stat[:, 2 + t:3 + t],
                                                in1=brb, op0=ALU.mult, op1=ALU.add))
            own.wait()
            for t in range(T):
                own.done(v.max(top[:, t, :], lg[t][:, 0:E]))
            own.wait()
            own.done(v.tensor_copy(rep[:, :, 0:TOPK], top[:, :, 0:TOPK]))
            v.tensor_scalar(ntop, top[:, :, 0], -1.0, None, ALU.mult).then_inc(lg_ready, 1)
            own.wait()
            for t in range(T):
                own.done(v.match_replace(left[:, t, :], rep[:, t, :], lg[t], -TAKEN))
            own.wait()
            for t in range(T):
                v.tensor_tensor(mask[:, t, :], left[:, t, 0:E], lg[t][:, 0:E], ALU.not_equal).then_inc(mask_ready, 1)
            v.wait_ge(mask_ready, T)
            v.wait_ge(ex_ready, T)
            own.done(v.tensor_tensor(ex, ex, mask, ALU.mult))
            own.wait()
            own.done(v.tensor_reduce(wsum, ex, AX, ALU.add))
            own.wait()
            own.done(v.reciprocal(wsum, wsum))
            own.wait()
            for t in range(T):
                v.tensor_scalar(comb[:, t, :], ex[:, t, :], wsum[:, t:t + 1], None, ALU.mult).then_inc(comb_ready, 1)
            v.wait_ge(pos_done, 1)
            own.done(v.scalar_tensor_tensor(out=posm, in0=ps[:, 2, 0:2 * E].rearrange("p (t n) -> p t n", t=T),
                                            scalar=1.0, in1=mask, op0=ALU.add, op1=ALU.mult))
            own.wait()

            def gather_hot(e):
                for t in range(T):
                    ins = v.tensor_scalar(g_hot[:, t, :], iota, posm[:, t, bass.ds(e, 1)] if not isinstance(e, int)
                                          else posm[:, t, e:e + 1], stat[:, 2 + t:3 + t], ALU.is_equal, ALU.mult)
                ins.then_inc(hot_ready, 1)

            def tokens_in():
                def per_chunk(cols, qs):
                    return cols.rearrange("p (h q) -> p q h", h=2)[:, qs, :].unsqueeze(3).broadcast_to([P, 2, 2, CAP])

                dst = xg.rearrange("p (q h) n -> p q h n", h=2)
                src = ps[:, 2, :].rearrange("p (q h n) -> p q h n", q=4, h=2)
                for qs in (slice(0, 2), slice(2, 4)):
                    own.done(v.tensor_tensor(dst[:, qs], src[:, qs], per_chunk(a2, qs), ALU.mult))
                    own.wait()
                    v.tensor_tensor(dst[:, qs], dst[:, qs], per_chunk(modT[:, M_SH2:M_SH2 + KD], qs),
                                    ALU.add).then_inc(xg_ready, 1)

            gather_hot(0)
            v.wait_ge(pos_done, 2)
            own.done(v.tensor_reduce(cntm, ps[:, 3, 0:E], AX, ALU.max))
            own.wait()
            own.done(v.tensor_scalar(over[:, 0:ROUNDS - 1], thr, cntm, None, ALU.is_lt))
            own.wait()
            own.done(v.tensor_reduce(last_f, over[:, 0:ROUNDS - 1], AX, ALU.add))
            own.wait()
            own.done(v.tensor_scalar(last_f, last_f, float(E // 2), float(E // 2 - 1), ALU.mult, ALU.add))
            own.wait()
            v.tensor_copy(last_pair[0:1, :], last_f[0:1, :]).then_inc(routed, 1)
            v.wait_ge(gather_done, 1)
            tokens_in()
            v.wait_ge(comb_turned, 1)
            v.wait_ge(zeroed, 2)
            v.tensor_copy(st[0:E, :], ps[0:E, 7, 0:S]).then_inc(st_ready, 1)
            v.wait_ge(st_ready, 1)
            v.tensor_copy(scrap[:, 2:3], ones[:, 0:1]).then_inc(acc_ready, 1)
            v.wait_ge(acc_started, T)
            own.wait()

            def accumulate(m):
                for t in range(T):
                    v.wait_ge(scatter_done, 2 * m + t + 1)
                    ins = v.tensor_tensor(acc[:, t, :], acc[:, t, :],
                                          ps[:, 4 + 2 * t:6 + 2 * t, :].rearrange("p b n -> p (b n)"), ALU.add)
                ins.then_inc(acc_ready, 1)

            final = v.value_load(last_pair[0:1, 0:1], min_val=E // 2 - 1, max_val=ROUNDS * E // 2 - 1)
            before, per_pair = own.n, 2 * 4

            def pair(m, last):
                for p in range(2):
                    i = 2 * m + p
                    e, e_next = (2 * m + p) % E, (2 * m + p + 1) % E
                    if not (last and p == 1):
                        v.wait_ge(gather_done, i + 1)
                        gather_hot(e_next)
                        select(e_next)
                    if p == 0:
                        v.wait_ge(st_ready, m + 1)
                    for t in range(T):
                        ins = v.tensor_scalar(wp[:, t, CAP * p:CAP * p + CAP], iota, posm[:, t, bass.ds(e, 1)],
                                              comb[:, t, bass.ds(e, 1)], ALU.is_equal, ALU.mult)
                    ins.then_inc(wp_ready, 1)
                    if p == 1:
                        v.wait_ge(wp_turned, m + 1)
                        v.tensor_copy(st, ps[:, 7, 0:S]).then_inc(st_ready, 1)
                    v.wait_ge(wp_ready, i + 1)
                    own.done(v.tensor_scalar(posm[:, :, bass.ds(e, 1)], posm[:, :, bass.ds(e, 1)], float(-CAP), None,
                                             ALU.add))
                    v.wait_ge(up_used, UP_SLOTS * (i + 1))
                    gu = ps[:, 0:2, :].rearrange("p b (n two) -> p b n two", two=2)
                    v.tensor_scalar(glu.rearrange("p (b n) -> p b n", b=2), gu[:, :, :, 0], LIMIT, None,
                                    ALU.min).then_inc(glu_ready, 1)
                    v.tensor_scalar(lin.rearrange("p (b n) -> p b n", b=2), gu[:, :, :, 1], LIMIT, -LIMIT,
                                    ALU.min, ALU.max).then_inc(gu_free, 1)
                    v.wait_ge(glu_ready, i + 1)
                    v.wait_ge(gu_free, i + 2)
                    own.done(v.scalar_tensor_tensor(out=lin, in0=lin, scalar=1.0, in1=glu, op0=ALU.add, op1=ALU.mult))
                    own.wait()
                    v.wait_ge(sig_ready, i + 1)
                    v.tensor_tensor(act_sb, lin, sig, ALU.mult).then_inc(act_ready, 1)
                    if p == 0:
                        accumulate(m)
                    if not (last and p == 1):
                        v.wait_ge(gather_done, i + 2)
                        tokens_in()
                    v.wait_ge(down_used, 4 * i + 4)
                    for half in range(2):
                        rows_in = slice(CAP * half, CAP * half + CAP)
                        ins = v.tensor_tensor(y2[CAP * p:CAP * p + CAP, 512 * half:512 * half + 512],
                                              ps[rows_in, 6, :], g2b[rows_in, 512 * half:512 * half + 512], ALU.mult)
                        if last and p == 1:
                            ins.then_inc(last_rows, 1)
                    if not (last and p == 1):
                        ins.then_inc(y_ready, 1)

            with v.Fori(0, final) as m:
                own.n, own.base = before, per_pair * m
                pair(m, False)
                assert own.n == before + per_pair, own.n - before
            own.n, own.base = before, per_pair * final
            pair(final, True)
            for n, (half, t, bank) in enumerate(LAST_PARTS):
                part = acc[:, t, 512 * half:512 * half + 512]
                v.wait_ge(last_scatter, n + 1)
                v.tensor_tensor(part, part, ps[:, bank, :], ALU.add).then_inc(fin_ready, 1)
            v.wait_ge(nf_landed, 16)
            for n in range(2 * T):
                t, cols = n // 2, slice(512 * (n % 2), 512 * (n % 2) + 512)
                v.wait_ge(r_fin_ready, t + 1)
                v.wait_ge(fin_ready, 2 * T)
                v.scalar_tensor_tensor(out=acc[:, t, cols], in0=acc[:, t, cols], scalar=stat[:, 2 + t:3 + t],
                                       in1=nfb[:, cols], op0=ALU.mult, op1=ALU.mult).then_inc(y_out, 1)


def distance_bucket(dist):
    exact = NB // 2
    d = np.maximum(dist, 1).astype(np.float32)
    large = exact + (np.log(d / np.float32(exact)) / np.float32(math.log(MAX_DISTANCE / exact))
                     * np.float32(NB - exact)).astype(np.int32)
    return np.where(dist < exact, dist, np.minimum(large, NB - 1))


def constants():
    cst = np.zeros((P, NCONST), np.float32)
    cst[:, C_ID:C_ID + P] = np.eye(P)
    cst[:, C_TRI:C_TRI + P] = np.triu(np.ones((P, P)), 1)
    cst[:, C_ONE:C_ONE + P] = 1.0
    cst[:, C_IOTA:C_IOTA + CAP] = 1 + np.arange(CAP)
    cst[:, C_THR:C_THR + ROUNDS - 1] = CAP * np.arange(1, ROUNDS)
    for g in range(2):
        cst[[32 * g, 64 + 32 * g], C_PAIR + g] = 1.0
    cst[:, C_FLIP:C_FLIP + P] = np.eye(P)[::-1]
    dist = np.maximum(S - 1 - np.arange(384), 0)
    hot = (distance_bucket(dist)[None, :] == np.arange(NB)[:, None]).astype(np.float32)
    return cst, hot


_INS = ["x", "c", "w_ada", "b_ada", "norm1_g", "norm2_g", "w_in", "conv_w", "conv_b", "w_out_conv",
        "lambda_q1", "lambda_k1", "lambda_q2", "lambda_k2", "subln_g", "w_o_attn", "w_merge",
        "w_router", "b_router", "w_gate_up", "b_gate_up", "w_down", "b_down", "rel_bias_table", "normf_g"]


def kernel(**inputs):
    import concourse.bacc as _bacc
    from concourse.bass_utils import run_bass_kernel_spmd as _run

    nc = _bacc.Bacc("TRN2", target_bir_lowering=False, num_devices=1)
    cst, hot = constants()
    given = {n: np.ascontiguousarray(inputs[n]) for n in _INS} | {"consts": cst, "buckets": hot}
    arrays, args = {}, []
    for name, a in given.items():
        arrays[f"in_{name}"] = a
        args.append(nc.dram_tensor(f"in_{name}", a.shape, mybir.dt.from_np(a.dtype), kind="ExternalInput").ap())
    args.append(nc.dram_tensor("out_0", (1, S, D), F32, kind="ExternalOutput").ap())
    block_kernel(nc, *args)
    r = _run(nc, [arrays], core_ids=[0])
    return r.results[0]["out_0"]
```
